# Optimizing a Trainium2 kernel written in Bass

```python
import math
import jax, jax.numpy as jnp
from jax import lax
import numpy as np

D_MODEL = 1024
BATCH = 1
SEQ = 512
DEPTH = 1

HEAD_DIM = 64
FOX_HEADS = 8
NSA_HEADS = 8
NSA_KV_HEADS = 2
CMP_BLOCK = 32
CMP_STRIDE = 16
CMP_HIDDEN = 256
SLC_BLOCK = 64
SLC_TOPK = 16
WINDOW = 512
Q_BLOCK = 128
N_GROUPS = 4
EXPERTS_PER_GROUP = 4
N_EXPERTS = N_GROUPS * EXPERTS_PER_GROUP
TOP_K_IN_GROUP = 2
D_EXPERT = 512
RMS_EPS = 1e-6
NEG_INF = -1e30
FORCE_SCORE = 1e4

FOX_W = FOX_HEADS * HEAD_DIM
NSA_W = NSA_HEADS * HEAD_DIM
NSA_KV_W = NSA_KV_HEADS * HEAD_DIM
IN_COLS = (FOX_W, FOX_W, FOX_W, FOX_HEADS,
           NSA_W, NSA_KV_W, NSA_KV_W, NSA_KV_W, NSA_KV_W, NSA_KV_W, NSA_KV_W, 3 * NSA_HEADS,
           D_MODEL, D_MODEL)
D_IN = sum(IN_COLS)


def rms_norm(x, g):
    xf = x.astype(jnp.float32)
    y = xf * lax.rsqrt(jnp.mean(xf * xf, axis=-1, keepdims=True) + RMS_EPS)
    return (y * g.astype(jnp.float32)).astype(x.dtype)

def split_cols(z):
    outs, off = [], 0
    for c in IN_COLS:
        outs.append(z[..., off:off + c])
        off += c
    return outs

def to_heads(t, n):
    B, S, _ = t.shape
    return t.reshape(B, S, n, HEAD_DIM).transpose(0, 2, 1, 3)

def from_heads(t):
    B, n, S, dh = t.shape
    return t.transpose(0, 2, 1, 3).reshape(B, S, n * dh)

def alibi_slopes(n):
    return jnp.asarray([2.0 ** (-8.0 * (h + 1) / n) for h in range(n)], jnp.float32)

def fox_attention(q, k, v, log_f):
    B, H, S, dh = q.shape
    cum = jnp.cumsum(log_f, axis=-1)
    scale = dh ** -0.5
    kpos = jnp.arange(S)

    def block(i):
        q0 = i * Q_BLOCK
        qpos = q0 + jnp.arange(Q_BLOCK)
        qb = lax.dynamic_slice_in_dim(q, q0, Q_BLOCK, axis=2)
        cb = lax.dynamic_slice_in_dim(cum, q0, Q_BLOCK, axis=2)
        s = jnp.einsum('bhqd,bhkd->bhqk', qb, k, preferred_element_type=jnp.float32) * scale
        s = s + cb[..., :, None] - cum[..., None, :]
        s = jnp.where(kpos[None, :] <= qpos[:, None], s, NEG_INF)
        p = jax.nn.softmax(s, axis=-1)
        return jnp.einsum('bhqk,bhkd->bhqd', p.astype(v.dtype), v)

    o = lax.map(block, jnp.arange(S // Q_BLOCK))
    return jnp.moveaxis(o, 0, 2).reshape(B, H, S, dh)

def compress_blocks(t, w1, w2, pos):
    B, S, G, dh = t.shape
    n_cmp = (S - CMP_BLOCK) // CMP_STRIDE + 1
    idx = jnp.arange(n_cmp)[:, None] * CMP_STRIDE + jnp.arange(CMP_BLOCK)[None, :]
    blk = t[:, idx] + pos[None, None, :, None, :]
    blk = jnp.moveaxis(blk, 3, 1).reshape(B, G, n_cmp, CMP_BLOCK * dh)
    return jax.nn.gelu(blk @ w1) @ w2

def nsa_attention(q, k_cmp, v_cmp, k_slc, v_slc, k_win, v_win, gates):
    B, H, S, dh = q.shape
    G = k_slc.shape[1]
    R = H // G
    n_cmp = k_cmp.shape[2]
    n_slc = S // SLC_BLOCK
    top_n = min(SLC_TOPK, n_slc)
    scale = dh ** -0.5
    slopes = alibi_slopes(H).reshape(G, R)[None, :, :, None, None]

    cmp_start = jnp.arange(n_cmp) * CMP_STRIDE
    cmp_end = cmp_start + CMP_BLOCK - 1
    slc_start = jnp.arange(n_slc) * SLC_BLOCK
    ov = jnp.minimum(cmp_start[:, None] + CMP_BLOCK, slc_start[None, :] + SLC_BLOCK) - \
        jnp.maximum(cmp_start[:, None], slc_start[None, :])
    overlap = jnp.clip(ov, 0, None).astype(jnp.float32) / CMP_BLOCK
    slc_ids = jnp.arange(n_slc)

    k_sb = k_slc.reshape(B, G, n_slc, SLC_BLOCK, dh)
    v_sb = v_slc.reshape(B, G, n_slc, SLC_BLOCK, dh)
    pad = ((0, 0), (0, 0), (WINDOW, 0), (0, 0))
    k_wp = jnp.pad(k_win, pad)
    v_wp = jnp.pad(v_win, pad)
    gather = jax.vmap(jax.vmap(lambda blocks, idx: blocks[idx]))

    def block(i):
        q0 = i * Q_BLOCK
        qpos = q0 + jnp.arange(Q_BLOCK)
        qb = lax.dynamic_slice_in_dim(q, q0, Q_BLOCK, axis=2).reshape(B, G, R, Q_BLOCK, dh)

        s = jnp.einsum('bgrqd,bgnd->bgrqn', qb, k_cmp, preferred_element_type=jnp.float32) * scale
        dist = (qpos[:, None] - cmp_end[None, :]).astype(jnp.float32)
        valid = dist >= 0
        s = jnp.where(valid, s - slopes * dist, NEG_INF)
        p_cmp = jax.nn.softmax(s, axis=-1) * jnp.any(valid, axis=-1)[:, None].astype(jnp.float32)
        o_cmp = jnp.einsum('bgrqn,bgnd->bgrqd', p_cmp.astype(v_cmp.dtype), v_cmp)

        imp = jnp.einsum('bgrqn,nj->bgqj', p_cmp, overlap)
        qblk = qpos // SLC_BLOCK
        forced = (slc_ids[None, :] == 0) | (slc_ids[None, :] == qblk[:, None]) | \
            (slc_ids[None, :] == qblk[:, None] - 1)
        future = slc_ids[None, :] * SLC_BLOCK > qpos[:, None]
        score = jnp.where(future, -1.0, jnp.where(forced, FORCE_SCORE, imp))
        _, idx = lax.top_k(score, top_n)
        n_tok = top_n * SLC_BLOCK
        ks_g = gather(k_sb, idx).reshape(B, G, Q_BLOCK, n_tok, dh)
        vs_g = gather(v_sb, idx).reshape(B, G, Q_BLOCK, n_tok, dh)
        spos = (idx[..., None] * SLC_BLOCK + jnp.arange(SLC_BLOCK)).reshape(B, G, Q_BLOCK, n_tok)
        dist = (qpos[:, None] - spos).astype(jnp.float32)[:, :, None]
        s = jnp.einsum('bgrqd,bgqkd->bgrqk', qb, ks_g, preferred_element_type=jnp.float32) * scale
        s = jnp.where(dist >= 0, s - slopes * dist, NEG_INF)
        o_slc = jnp.einsum('bgrqk,bgqkd->bgrqd', jax.nn.softmax(s, axis=-1).astype(vs_g.dtype), vs_g)

        kw_b = lax.dynamic_slice_in_dim(k_wp, q0, WINDOW + Q_BLOCK, axis=2)
        vw_b = lax.dynamic_slice_in_dim(v_wp, q0, WINDOW + Q_BLOCK, axis=2)
        wpos = q0 - WINDOW + jnp.arange(WINDOW + Q_BLOCK)
        dist = (qpos[:, None] - wpos[None, :]).astype(jnp.float32)
        valid = (dist >= 0) & (dist < WINDOW) & (wpos[None, :] >= 0)
        s = jnp.einsum('bgrqd,bgkd->bgrqk', qb, kw_b, preferred_element_type=jnp.float32) * scale
        s = jnp.where(valid, s - slopes * dist, NEG_INF)
        o_win = jnp.einsum('bgrqk,bgkd->bgrqd', jax.nn.softmax(s, axis=-1).astype(vw_b.dtype), vw_b)

        gb = lax.dynamic_slice_in_dim(gates, q0, Q_BLOCK, axis=2).reshape(B, G, R, Q_BLOCK, 3)
        o = gb[..., 0:1] * o_cmp + gb[..., 1:2] * o_slc + gb[..., 2:3] * o_win
        return o.reshape(B, H, Q_BLOCK, dh)

    o = lax.map(block, jnp.arange(S // Q_BLOCK))
    return jnp.moveaxis(o, 0, 2).reshape(B, H, S, dh)

def hierarchical_moe(x, w_group, b_group, w_router, b_router, w_gate, w_up, w_down):
    B, S, D = x.shape
    t = x.reshape(B * S, D)
    g_logits = (t @ w_group).astype(jnp.float32) + b_group.astype(jnp.float32)
    p_g, g_top = lax.top_k(jax.nn.softmax(g_logits, axis=-1), 1)
    e_logits = ((t @ w_router).astype(jnp.float32) + b_router.astype(jnp.float32)).reshape(-1, N_GROUPS, EXPERTS_PER_GROUP)
    e_in = jnp.take_along_axis(e_logits, g_top[:, :, None], axis=1)[:, 0]
    top_p, top_i = lax.top_k(jax.nn.softmax(e_in, axis=-1), TOP_K_IN_GROUP)
    w = top_p / jnp.sum(top_p, axis=-1, keepdims=True) * p_g
    expert_id = g_top * EXPERTS_PER_GROUP + top_i
    combine = jnp.sum(jax.nn.one_hot(expert_id, N_EXPERTS, dtype=jnp.float32) * w[..., None], axis=1)
    hid = jax.nn.silu(jnp.einsum('td,edf->etf', t, w_gate)) * jnp.einsum('td,edf->etf', t, w_up)
    hid = hid * combine.T.astype(hid.dtype)[:, :, None]
    y = jnp.einsum('etf,efd->td', hid, w_down)
    return y.reshape(B, S, D)

def first_inputs(seed: int = 0) -> dict:
    key = jax.random.key(seed)
    ks = jax.random.split(key, 26)
    L = DEPTH

    def nrm(k, shape, scale):
        return jax.random.normal(k, shape, jnp.float32) * scale

    def gain(k, shape):
        return 1.0 + 0.02 * jax.random.normal(k, shape, jnp.float32)

    cmp_in = CMP_BLOCK * HEAD_DIM
    return {
        "x": nrm(ks[0], (BATCH, SEQ, D_MODEL), 1.0),
        "norm_mix_g": gain(ks[1], (L, D_MODEL)),
        "w_in": nrm(ks[2], (L, D_MODEL, D_IN), D_MODEL ** -0.5),
        "b_forget": jnp.linspace(1.0, 6.0, FOX_HEADS, dtype=jnp.float32)[None, :] + nrm(ks[3], (L, FOX_HEADS), 0.1),
        "fox_q_g": gain(ks[4], (L, HEAD_DIM)),
        "fox_k_g": gain(ks[5], (L, HEAD_DIM)),
        "nsa_q_g": gain(ks[6], (L, HEAD_DIM)),
        "nsa_k_g": gain(ks[7], (L, HEAD_DIM)),
        "cmp_k_w1": nrm(ks[8], (L, cmp_in, CMP_HIDDEN), cmp_in ** -0.5),
        "cmp_k_w2": nrm(ks[9], (L, CMP_HIDDEN, HEAD_DIM), CMP_HIDDEN ** -0.5),
        "cmp_k_pos": nrm(ks[10], (L, CMP_BLOCK, HEAD_DIM), 0.1),
        "cmp_v_w1": nrm(ks[11], (L, cmp_in, CMP_HIDDEN), cmp_in ** -0.5),
        "cmp_v_w2": nrm(ks[12], (L, CMP_HIDDEN, HEAD_DIM), CMP_HIDDEN ** -0.5),
        "cmp_v_pos": nrm(ks[13], (L, CMP_BLOCK, HEAD_DIM), 0.1),
        "w_fox_up": nrm(ks[14], (L, FOX_W, D_MODEL), FOX_W ** -0.5),
        "w_nsa_up": nrm(ks[15], (L, NSA_W, D_MODEL), NSA_W ** -0.5),
        "w_out": nrm(ks[16], (L, D_MODEL, D_MODEL), D_MODEL ** -0.5),
        "norm_ffn_g": gain(ks[17], (L, D_MODEL)),
        "w_group": nrm(ks[18], (L, D_MODEL, N_GROUPS), D_MODEL ** -0.5),
        "b_group": nrm(ks[19], (L, N_GROUPS), 0.01),
        "w_router": nrm(ks[20], (L, D_MODEL, N_EXPERTS), D_MODEL ** -0.5),
        "b_router": nrm(ks[21], (L, N_EXPERTS), 0.01),
        "w_gate": nrm(ks[22], (L, N_EXPERTS, D_MODEL, D_EXPERT), D_MODEL ** -0.5),
        "w_up": nrm(ks[23], (L, N_EXPERTS, D_MODEL, D_EXPERT), D_MODEL ** -0.5),
        "w_down": nrm(ks[24], (L, N_EXPERTS, D_EXPERT, D_MODEL), D_EXPERT ** -0.5),
    }

def first_block(x, norm_mix_g, w_in, b_forget, fox_q_g, fox_k_g, nsa_q_g, nsa_k_g,
              cmp_k_w1, cmp_k_w2, cmp_k_pos, cmp_v_w1, cmp_v_w2, cmp_v_pos,
              w_fox_up, w_nsa_up, w_out, norm_ffn_g, w_group, b_group, w_router, b_router,
              w_gate, w_up, w_down):
    B, S, D = x.shape
    for l in range(DEPTH):
        h = rms_norm(x, norm_mix_g[l])
        (f_q, f_k, f_v, f_f, n_q, k_c, v_c, k_s, v_s, k_w, v_w, n_g, g_a, g_b) = split_cols(h @ w_in[l])

        qa = rms_norm(to_heads(f_q, FOX_HEADS), fox_q_g[l])
        ka = rms_norm(to_heads(f_k, FOX_HEADS), fox_k_g[l])
        va = to_heads(f_v, FOX_HEADS)
        log_f = jax.nn.log_sigmoid(f_f.astype(jnp.float32) + b_forget[l].astype(jnp.float32)).transpose(0, 2, 1)
        out_a = from_heads(fox_attention(qa, ka, va, log_f)) @ w_fox_up[l]

        qb = rms_norm(to_heads(n_q, NSA_HEADS), nsa_q_g[l])
        kc = compress_blocks(k_c.reshape(B, S, NSA_KV_HEADS, HEAD_DIM), cmp_k_w1[l], cmp_k_w2[l], cmp_k_pos[l])
        kc = rms_norm(kc, nsa_k_g[l])
        vc = compress_blocks(v_c.reshape(B, S, NSA_KV_HEADS, HEAD_DIM), cmp_v_w1[l], cmp_v_w2[l], cmp_v_pos[l])
        ks_ = rms_norm(to_heads(k_s, NSA_KV_HEADS), nsa_k_g[l])
        vs_ = to_heads(v_s, NSA_KV_HEADS)
        kw_ = rms_norm(to_heads(k_w, NSA_KV_HEADS), nsa_k_g[l])
        vw_ = to_heads(v_w, NSA_KV_HEADS)
        gates = jax.nn.sigmoid(n_g.reshape(B, S, NSA_HEADS, 3)).transpose(0, 2, 1, 3)
        out_b = from_heads(nsa_attention(qb, kc, vc, ks_, vs_, kw_, vw_, gates)) @ w_nsa_up[l]

        mix = jax.nn.sigmoid(g_a) * out_a + jax.nn.sigmoid(g_b) * out_b
        x = x + mix @ w_out[l]

        x = x + hierarchical_moe(rms_norm(x, norm_ffn_g[l]), w_group[l], b_group[l], w_router[l], b_router[l],
                                 w_gate[l], w_up[l], w_down[l])
    return x


A_HEADS = 8
A_HEAD_DIM = 64
A_WIDTH = A_HEADS * A_HEAD_DIM
DECAY_LORA = 64
ICLR_LORA = 64
DECAY_SCALE = 0.6065306597
GN_EPS = 64e-5
B_HEADS = 8
QK_NOPE_DIM = 64
QK_ROPE_DIM = 32
V_HEAD_DIM = 64
Q_LORA_RANK = 256
KV_LORA_RANK = 128
B_WIDTH = B_HEADS * V_HEAD_DIM
ROPE_THETA = 10000.0
NORM_EPS = 1e-6
N_BRANCHES = 2
SHIFT_COLS = 3 * A_WIDTH + DECAY_LORA + ICLR_LORA
IN_COLS_2 = SHIFT_COLS + A_WIDTH + Q_LORA_RANK + KV_LORA_RANK + QK_ROPE_DIM + B_WIDTH + N_BRANCHES * D_MODEL


def rmsnorm(x, g, eps=NORM_EPS):
    xf = x.astype(jnp.float32)
    y = xf * lax.rsqrt(jnp.mean(xf * xf, axis=-1, keepdims=True) + eps)
    return (y * g.astype(jnp.float32)).astype(x.dtype)

def split_cols_2(t, sizes):
    idx = np.cumsum(sizes)[:-1].tolist()
    return jnp.split(t, idx, axis=-1)

def token_shift(feat, mu):
    prev = jnp.pad(feat, ((0, 0), (1, 0), (0, 0)))[:, :-1, :]
    return feat + mu * (prev - feat)

def rwkv7_branch(feat, z, mu_shift, w0, w_decay_up, a0, w_iclr_up, k_k, k_a, r_k, gn_gain, gn_bias, w_out_a):
    bsz, seq, _ = feat.shape
    dt = feat.dtype
    f = token_shift(feat, mu_shift)
    r, k, v, wd, ad = split_cols_2(f, [A_WIDTH, A_WIDTH, A_WIDTH, DECAY_LORA, ICLR_LORA])
    w_logit = (w0 + jnp.tanh(wd) @ w_decay_up).astype(jnp.float32)
    w = jnp.exp(-DECAY_SCALE * jax.nn.sigmoid(w_logit))
    a = jax.nn.sigmoid((a0 + ad @ w_iclr_up).astype(jnp.float32))
    hs = lambda t: t.reshape(bsz, seq, A_HEADS, A_HEAD_DIM).astype(jnp.float32)
    r, k, v, w, a = hs(r), hs(k), hs(v), hs(w), hs(a)
    kk = k * k_k.reshape(A_HEADS, A_HEAD_DIM)
    kk = kk / jnp.maximum(jnp.linalg.norm(kk, axis=-1, keepdims=True), 1e-12)
    k = k * (1.0 + (a - 1.0) * k_a.reshape(A_HEADS, A_HEAD_DIM))

    def step(S, inp):
        r_t, w_t, k_t, v_t, kk_t, a_t = inp
        sa = jnp.einsum('bhvk,bhk->bhv', S, -kk_t)
        S = S * w_t[:, :, None, :] + sa[..., None] * (kk_t * a_t)[:, :, None, :] + v_t[..., None] * k_t[:, :, None, :]
        return S, jnp.einsum('bhvk,bhk->bhv', S, r_t)

    tm = lambda t: jnp.moveaxis(t, 1, 0)
    S0 = jnp.zeros((bsz, A_HEADS, A_HEAD_DIM, A_HEAD_DIM), jnp.float32)
    _, y = lax.scan(step, S0, (tm(r), tm(w), tm(k), tm(v), tm(kk), tm(a)))
    y = jnp.moveaxis(y, 0, 1)
    mean = jnp.mean(y, axis=-1, keepdims=True)
    var = jnp.mean(jnp.square(y - mean), axis=-1, keepdims=True)
    y = (y - mean) * lax.rsqrt(var + GN_EPS)
    y = y * gn_gain.reshape(A_HEADS, A_HEAD_DIM) + gn_bias.reshape(A_HEADS, A_HEAD_DIM)
    y = y + jnp.sum(r * k * r_k, axis=-1, keepdims=True) * v
    y = y.reshape(bsz, seq, A_WIDTH).astype(dt) * jax.nn.silu(z)
    return y @ w_out_a

def rope(t, cos, sin):
    t1, t2 = jnp.split(t, 2, axis=-1)
    return jnp.concatenate([t1 * cos - t2 * sin, t2 * cos + t1 * sin], axis=-1)

def mla_branch(c_q, c_kv, k_pe, z, positions, g_q, w_uq, g_kv, w_ukv, w_out_b):
    bsz, seq, _ = c_q.shape
    dt = c_q.dtype
    q = (rmsnorm(c_q, g_q) @ w_uq).reshape(bsz, seq, B_HEADS, QK_NOPE_DIM + QK_ROPE_DIM)
    q_nope, q_pe = q[..., :QK_NOPE_DIM], q[..., QK_NOPE_DIM:]
    kv = (rmsnorm(c_kv, g_kv) @ w_ukv).reshape(bsz, seq, B_HEADS, QK_NOPE_DIM + V_HEAD_DIM)
    k_nope, v = kv[..., :QK_NOPE_DIM], kv[..., QK_NOPE_DIM:]
    inv_freq = ROPE_THETA ** (-jnp.arange(0, QK_ROPE_DIM, 2, dtype=jnp.float32) / QK_ROPE_DIM)
    ang = positions.astype(jnp.float32)[..., None] * inv_freq
    cos, sin = jnp.cos(ang).astype(dt), jnp.sin(ang).astype(dt)
    q_pe = rope(q_pe, cos[:, :, None, :], sin[:, :, None, :])
    k_pe = rope(k_pe, cos, sin)
    scale = 1.0 / math.sqrt(QK_NOPE_DIM + QK_ROPE_DIM)
    nb = seq // Q_BLOCK
    blk = lambda t: jnp.moveaxis(t.reshape(bsz, nb, Q_BLOCK, *t.shape[2:]), 1, 0)
    key_idx = jnp.arange(seq)

    def attend(args):
        qn, qp, b = args
        s = jnp.einsum('bqhd,bkhd->bhqk', qn, k_nope) + jnp.einsum('bqhr,bkr->bhqk', qp, k_pe)
        s = s.astype(jnp.float32) * scale
        q_idx = b * Q_BLOCK + jnp.arange(Q_BLOCK)
        s = jnp.where(key_idx[None, :] <= q_idx[:, None], s, jnp.finfo(jnp.float32).min)
        p = jax.nn.softmax(s, axis=-1).astype(dt)
        return jnp.einsum('bhqk,bkhd->bqhd', p, v)

    o = lax.map(attend, (blk(q_nope), blk(q_pe), jnp.arange(nb)))
    o = jnp.moveaxis(o, 0, 1).reshape(bsz, seq, B_WIDTH)
    return (o * jax.nn.silu(z)) @ w_out_b

def second_inputs(seed: int = 0) -> dict:
    key = jax.random.key(seed)
    ks = jax.random.split(key, 24)
    n = lambda i, shape, s=1.0: s * jax.random.normal(ks[i], shape, jnp.float32)
    x = n(0, (BATCH, SEQ, D_MODEL))
    positions = (jnp.arange(SEQ, dtype=jnp.int32)[None, :]
                 + jax.random.randint(ks[1], (BATCH, 1), 0, 1024, dtype=jnp.int32))
    return {
        'x': x,
        'positions': positions,
        'g_pre': 1.0 + n(2, (D_MODEL,), 0.05),
        'w_in': n(3, (D_MODEL, IN_COLS_2), D_MODEL ** -0.5),
        'b_gate': n(4, (N_BRANCHES * D_MODEL,), 0.01),
        'mu_shift': jax.random.uniform(ks[5], (SHIFT_COLS,), jnp.float32),
        'w0': n(6, (A_WIDTH,), 0.5),
        'w_decay_up': n(7, (DECAY_LORA, A_WIDTH), 0.1),
        'a0': n(8, (A_WIDTH,), 0.5),
        'w_iclr_up': n(9, (ICLR_LORA, A_WIDTH), 0.5 * ICLR_LORA ** -0.5),
        'k_k': 0.85 + n(10, (A_WIDTH,), 0.05),
        'k_a': 1.0 + n(11, (A_WIDTH,), 0.05),
        'r_k': n(12, (A_HEADS, A_HEAD_DIM), 0.1),
        'gn_gain': 1.0 + n(13, (A_WIDTH,), 0.05),
        'gn_bias': n(14, (A_WIDTH,), 0.01),
        'w_out_a': n(15, (A_WIDTH, D_MODEL), A_WIDTH ** -0.5),
        'g_q': 1.0 + n(16, (Q_LORA_RANK,), 0.05),
        'w_uq': n(17, (Q_LORA_RANK, B_HEADS * (QK_NOPE_DIM + QK_ROPE_DIM)), Q_LORA_RANK ** -0.5),
        'g_kv': 1.0 + n(18, (KV_LORA_RANK,), 0.05),
        'w_ukv': n(19, (KV_LORA_RANK, B_HEADS * (QK_NOPE_DIM + V_HEAD_DIM)), KV_LORA_RANK ** -0.5),
        'w_out_b': n(20, (B_WIDTH, D_MODEL), B_WIDTH ** -0.5),
        'w_o': n(21, (D_MODEL, D_MODEL), D_MODEL ** -0.5),
        'g_post': 1.0 + n(22, (D_MODEL,), 0.05),
    }

def second_block(x, positions, g_pre, w_in, b_gate, mu_shift, w0, w_decay_up, a0, w_iclr_up, k_k, k_a, r_k,
              gn_gain, gn_bias, w_out_a, g_q, w_uq, g_kv, w_ukv, w_out_b, w_o, g_post):
    h = x
    for _ in range(DEPTH):
        u = rmsnorm(h, g_pre)
        proj = u @ w_in
        feat_a, z_a, c_q, c_kv, k_pe, z_b, gate_logits = split_cols_2(
            proj, [SHIFT_COLS, A_WIDTH, Q_LORA_RANK, KV_LORA_RANK, QK_ROPE_DIM, B_WIDTH, N_BRANCHES * D_MODEL])
        y_a = rwkv7_branch(feat_a, z_a, mu_shift, w0, w_decay_up, a0, w_iclr_up, k_k, k_a, r_k,
                           gn_gain, gn_bias, w_out_a)
        y_b = mla_branch(c_q, c_kv, k_pe, z_b, positions, g_q, w_uq, g_kv, w_ukv, w_out_b)
        gates = jax.nn.sigmoid(gate_logits + b_gate)
        g_a, g_b = gates[..., :D_MODEL], gates[..., D_MODEL:]
        merged = g_a * y_a + g_b * y_b
        h = h + rmsnorm(merged @ w_o, g_post)
    return h


def setup_inputs(seed=0):
    out = dict(first_inputs(seed))
    for name, value in second_inputs(seed + 1).items():
        if name != "x":
            out[name + "_2"] = value
    return out


def reference(
    x, norm_mix_g, w_in, b_forget, fox_q_g, fox_k_g, nsa_q_g, nsa_k_g, cmp_k_w1, cmp_k_w2,
    cmp_k_pos, cmp_v_w1, cmp_v_w2, cmp_v_pos, w_fox_up, w_nsa_up, w_out, norm_ffn_g, w_group,
    b_group, w_router, b_router, w_gate, w_up, w_down, positions_2, g_pre_2, w_in_2, b_gate_2,
    mu_shift_2, w0_2, w_decay_up_2, a0_2, w_iclr_up_2, k_k_2, k_a_2, r_k_2, gn_gain_2,
    gn_bias_2, w_out_a_2, g_q_2, w_uq_2, g_kv_2, w_ukv_2, w_out_b_2, w_o_2, g_post_2,
):
    x = first_block(
        x, norm_mix_g, w_in, b_forget, fox_q_g, fox_k_g, nsa_q_g, nsa_k_g, cmp_k_w1, cmp_k_w2,
        cmp_k_pos, cmp_v_w1, cmp_v_w2, cmp_v_pos, w_fox_up, w_nsa_up, w_out, norm_ffn_g,
        w_group, b_group, w_router, b_router, w_gate, w_up, w_down,
    )
    return second_block(
        x, positions_2, g_pre_2, w_in_2, b_gate_2, mu_shift_2, w0_2, w_decay_up_2, a0_2,
        w_iclr_up_2, k_k_2, k_a_2, r_k_2, gn_gain_2, gn_bias_2, w_out_a_2, g_q_2, w_uq_2,
        g_kv_2, w_ukv_2, w_out_b_2, w_o_2, g_post_2,
    )


_drawn_inputs = setup_inputs


def setup_inputs(seed=0):
    import zlib

    import numpy as np

    out = dict(_drawn_inputs(seed))
    spreads = {}
    factors = {'fox_q_g': 6.794,
     'fox_k_g': 3.632,
     'nsa_q_g': 7.496,
     'nsa_k_g': 5.155,
     'b_router': 8.0,
     'b_gate_2': 23.002,
     'k_k_2': 47.704,
     'gn_bias_2': 57.281,
     'g_q_2': 8.0,
     'g_kv_2': 6.847,
     'w0_2': 3.307,
     'w_decay_up_2': 5.807,
     'w_iclr_up_2': 2.775,
     'k_a_2': 8.0,
     'gn_gain_2': 8.0}
    for name, (base, spread) in spreads.items():
        noise = np.random.default_rng([zlib.crc32(name.encode()), seed]).standard_normal(out[name].shape)
        drawn = base * np.exp(spread * noise) if base else spread * noise
        out[name] = __import__('jax').numpy.asarray(drawn.astype(out[name].dtype))
    for name, factor in factors.items():
        out[name] = (out[name] * factor).astype(out[name].dtype)
    return out
```

```python
from contextlib import ExitStack

import numpy as np

import concourse.bass as bass
from concourse import mybir

F32 = mybir.dt.float32
BF16 = mybir.dt.bfloat16
U32 = mybir.dt.uint32
I32 = mybir.dt.int32
ALU = mybir.AluOpType
ACT = mybir.ActivationFunctionType
AX = mybir.AxisListType

EPS = 1e-6
GN_EPS = 64e-5
NEG = -1e30
DECAY = 0.6065306597
TWO_PI = 2.0 * np.pi


def constants():
    p = np.arange(128)
    parts, off = [], {}

    def put(name, a):
        a = np.asarray(a, np.float32).reshape(128, -1)
        off[name] = (sum(x.shape[1] for x in parts), a.shape[1])
        parts.append(a)

    put("ident", np.eye(128))
    put("tri", (p[:, None] <= p[None, :]))
    put("stri", (p[:, None] < p[None, :]))
    put("ones", np.ones((128, 128)))
    put("bd", (p[:, None] // 64 == p[None, :] // 64))
    put("causal", np.where(p[None, :] <= p[:, None], 0.0, NEG))
    q = p[:, None] + 128 * np.arange(4)[None, :]
    n = np.arange(32)
    ok = (n[None, None, :] * 16 + 31 <= q[:, :, None]) & (n < 31)[None, None, :]
    put("cmask", np.where(ok, 0.0, NEG))
    put("anyv", (q >= 31))
    sl = 2.0 ** -(np.arange(8) + 1.0)
    qa = np.zeros((128, 4, 8, 2))
    qa[..., 0] = sl[None, None, :]
    qa[..., 1] = -sl[None, None, :] * q[:, :, None]
    put("qaug", qa)
    ka = np.zeros((128, 4, 2))
    ka[..., 0] = q
    ka[..., 1] = 1.0
    put("kaug", ka)
    ca = np.zeros((128, 2))
    ca[:, 0] = np.where(p % 32 < 31, (p % 32) * 16 + 31, 0)
    ca[:, 1] = 1.0
    put("caug", ca)
    for m in (1, 2, 4, 8, 16, 32, 64):
        j, t = p[:, None] // m, p[None, :] // m
        put(f"lv{m}", (t % 2 == 1) & (j == t - 1))
    put("hsel", (p[:, None] // 64 == np.arange(2)[None, :]))
    inv = (np.float32(10000.0) ** (-np.arange(0, 32, 2, dtype=np.float32) / np.float32(32))).astype(np.float32)
    put("invf", np.broadcast_to(inv, (128, 16)))
    put("e4", np.broadcast_to(np.arange(4), (128, 4)))
    return np.concatenate(parts, 1), off


class Engine:

    def __init__(self, eng, sem):
        self.eng, self.sem, self.n, self.seen = eng, sem, 0, {}

    def need(self, *tokens):
        for t in tokens:
            if t is not None and self.seen.get(t[0], 0) < t[2]:
                self.eng.wait_ge(t[1], t[2])
                self.seen[t[0]] = t[2]

    def mark(self, ins):
        self.n += 1
        ins.then_inc(self.sem, 1)
        return (id(self), self.sem, self.n)

    @property
    def last(self):
        return (id(self), self.sem, self.n) if self.n else None


class Queue:

    def __init__(self, engine, sems):
        self.engine, self.sems, self.n = engine, sems, 0

    def copy(self, dst, src, *tokens, **kw):
        i = self.n % len(self.sems)
        self.engine.need(*tokens, self.token(self.n - len(self.sems)))
        self.engine.eng.dma_start(dst, src, **kw).then_inc(self.sems[i], 16)
        self.n += 1
        return self.token(self.n - 1)

    def token(self, k):
        if k < 0:
            return None
        i = k % len(self.sems)
        return ((id(self), i), self.sems[i], 16 * (k // len(self.sems) + 1))

    def outstanding(self):
        return [self.token(k) for k in range(max(0, self.n - len(self.sems)), self.n)]


class Slot:
    def __init__(self, ap):
        self.ap, self.free = ap, []


class Ring:
    def __init__(self, aps):
        self.slots, self.n = [Slot(a) for a in aps], 0

    def get(self):
        self.n += 1
        return self.slots[(self.n - 1) % len(self.slots)]


def pipe(items, *stages):
    for step in range(len(items) + len(stages) - 1):
        for s, stage in enumerate(stages):
            if 0 <= step - s < len(items):
                stage(items[step - s])


def build(nc, a, coff, out, xs_dram):
    with ExitStack() as ctx:
        sem = lambda name: ctx.enter_context(nc.semaphore(name))
        pe = Engine(nc.tensor, sem("s_pe"))
        ve = Engine(nc.vector, sem("s_ve"))
        ac = Engine(nc.scalar, sem("s_ac"))
        po = Engine(nc.gpsimd, sem("s_po"))
        sy = Engine(nc.sync, sem("s_sy"))
        wq = Queue(sy, [sem(f"s_w{i}") for i in range(12)])
        mq = Queue(po, [sem(f"s_m{i}") for i in range(24)])
        oq = Queue(sy, [sem(f"s_o{i}") for i in range(4)])
        pt_, vt, st, gt = nc.tensor, nc.vector, nc.scalar, nc.gpsimd

        ncst = sum(v[1] for v in coff.values())
        sb = lambda name, shape, dt=F32: ctx.enter_context(nc.sbuf_tensor(name, shape, dt))
        cst = sb("cst", [128, ncst])
        C = {k: cst[:, o:o + n] for k, (o, n) in coff.items()}
        identb = sb("identb", [128, 128], BF16)
        causb = sb("causb", [128, 128], BF16)
        cmaskb = sb("cmaskb", [128, 128], BF16)
        X = sb("X", [128, 4, 1024])
        HT = sb("HT", [128, 8, 512])
        NW = 4
        Wt = sb("Wt", [128, NW, 4096])
        PR = sb("PR", [96, 128])
        PT = sb("PT", [128, 96])
        BR = sb("BR", [128, 28])
        SM = sb("SM", [128, 1024])
        ARN = 25200
        AR = sb("AR", [128, ARN])
        banks = [ctx.enter_context(nc.psum_tensor(f"pb{i}", [128, 512], F32)) for i in range(8)]
        SR = Ring([b[:, :] for b in banks[0:3]])
        TR = Ring([b[:, :] for b in banks[3:6]])
        OR = Ring([b[:, :] for b in banks[6:8]])
        WR = Ring([Wt[:, i, :] for i in range(NW)])

        class Place:

            def __init__(self, t, n, at=0):
                self.t, self.n, self.at = t, n, at

            def take(self, *shape):
                k = int(np.prod(shape))
                assert self.at + k <= self.n, (self.at, k, self.n)
                v = self.t[:, self.at:self.at + k]
                self.at += k
                if len(shape) == 2:
                    v = v.rearrange("p (a b) -> p a b", b=shape[1])
                if len(shape) == 3:
                    v = v.rearrange("p (a b c) -> p a b c", b=shape[1], c=shape[2])
                return v

        small = Place(SM, 1024)

        def barrier():
            toks = [e.last for e in (pe, ve, ac, po)] + mq.outstanding()
            for e in (pe, ve, ac, po):
                e.need(*toks)

        def mm(o, lhsT, rhs, start, stop, skip=False):
            return pt_.matmul(o, lhsT, rhs, start=start, stop=stop, skip_group_check=skip)

        def wload(src, k, cols, *more):
            s = WR.get()
            v = s.ap[:, 0:k * cols].rearrange("p (k n) -> p k n", n=cols)
            tok = wq.copy(v, src, *s.free)
            s.free = []
            return s, v, tok

        def wcols(w, c0, n, rows=1024):
            return w[0:rows, c0:c0 + n].rearrange("(k p) n -> p k n", p=128)

        t_x = wq.copy(X[:, :, :], a["x"][0].rearrange("(t p) d -> p t d", p=128))
        t_c = wq.copy(cst[:, :], a["consts"])
        t_m1 = ve.mark(vt.memset(PR[:, :], 1.0))
        rows = [("norm_mix_g", 0, 8), ("norm_ffn_g", 8, 8), ("g_pre_2", 16, 8), ("mu_shift_2", 24, 13),
                ("w0_2", 37, 4), ("a0_2", 41, 4), ("k_k_2", 45, 4), ("k_a_2", 49, 4), ("r_k_2", 53, 4),
                ("g_q_2", 57, 2), ("g_kv_2", 59, 1), ("fox_q_g", 60, 1), ("fox_k_g", 61, 1),
                ("nsa_q_g", 62, 1), ("nsa_k_g", 63, 1), ("cmp_k_pos", 64, 16), ("cmp_v_pos", 80, 16)]
        t_pr = []
        for name, r, n in rows:
            src = a[name]
            while len(src.shape) > 1:
                src = src.rearrange("a b -> (a b)") if len(src.shape) == 2 else src.rearrange("a b c -> (a b c)")
            w = src.shape[0] // n
            t_pr.append(mq.copy(PR[r:r + n, 0:w], src.rearrange("(r w) -> r w", w=w), t_m1))
        for name, o, n in (("b_forget", 0, 8), ("b_group", 8, 4), ("b_router", 12, 16)):
            t_pr.append(mq.copy(BR[:, o:o + n], a[name].to_broadcast([128, n])))
        t_br = t_pr[-3:]

        ve.need(t_c)
        ve.mark(vt.tensor_copy(identb[:, :], C["ident"]))
        ve.mark(vt.tensor_copy(causb[:, :], C["causal"]))
        t_cb = ve.mark(vt.tensor_copy(cmaskb[:, :], C["cmask"]))
        s = TR.get()
        pe.need(t_c, *t_pr)
        t = pe.mark(pt_.transpose(s.ap[:, 0:96], PR[:, :], C["ident"][0:96, 0:96]))
        ve.need(t)
        t_pt = ve.mark(vt.tensor_copy(PT[:, :], s.ap[:, 0:96]))
        s.free = [t_pt]
        ident = C["ident"]
        for e in (pe, ve, ac, po):
            e.need(t_c, t_cb, t_pt, *t_br)

        def rstd(dst, ss, n, scr, tok, s=1.0, eps=EPS):
            m, y = scr
            ve.need(tok)
            t = ve.mark(vt.tensor_scalar(m, ss, 1.0 / n, eps, ALU.mult, ALU.add))
            ac.need(t)
            t2 = ac.mark(st.activation(y, m, ACT.Ln))
            ac.need(t2)
            t3 = ac.mark(st.activation(y, y, ACT.Exp, scale=-0.5))
            ve.need(t3)
            t = ve.mark(vt.tensor_tensor(dst, y, y, ALU.mult))
            ve.need(t)
            t = ve.mark(vt.tensor_tensor(dst, dst, m, ALU.mult))
            ve.need(t)
            t = ve.mark(vt.tensor_scalar(dst, dst, -0.5 * s, 1.5 * s, ALU.mult, ALU.add))
            ve.need(t)
            return ve.mark(vt.tensor_tensor(dst, dst, y, ALU.mult))

        def bc(ap, n):
            return ap.unsqueeze(len(ap.shape)).to_broadcast([*ap.shape, n])

        def mid(ap, n):
            return ap.unsqueeze(1).to_broadcast([ap.shape[0], n, *ap.shape[1:]])

        def norm_turn(dst, gcol, scr, tokens):
            buf = scr.take(2, 1024)
            ss, rs, m, y = (small.take(4) for _ in range(4))
            ring = Ring([buf[:, i, :] for i in range(2)])
            toks = []
            for t in range(4):
                b = ring.get()
                ac.need(*tokens, *b.free)
                toks.append(ac.mark(st.activation(b.ap, X[:, t, :], ACT.Square, accum_out=ss[:, t:t + 1])))
                b.free = [toks[-1]]
            tr = rstd(rs, ss, 1024, (m, y), toks[-1])
            done = []

            def scale(t):
                b = ring.get()
                ve.need(tr, *b.free)
                tk = ve.mark(vt.tensor_scalar(b.ap, X[:, t, :], rs[:, t:t + 1], None, ALU.mult))
                state[t] = (b, tk)

            def turn(t):
                b, tk = state[t]
                pe.need(tk)
                for g in range(2):
                    s = TR.get()
                    pe.need(*s.free)
                    for j in range(4):
                        k = 4 * g + j
                        r = pt_.transpose(s.ap[:, j * 128:(j + 1) * 128], b.ap[:, k * 128:(k + 1) * 128], ident)
                    tp = pe.mark(r)
                    ve.need(tp)
                    for j in range(4):
                        k = 4 * g + j
                        r = ve.mark(vt.tensor_scalar(dst[:, k, t * 128:(t + 1) * 128],
                                                     s.ap[:, j * 128:(j + 1) * 128],
                                                     PT[:, gcol + k:gcol + k + 1], None, ALU.mult))
                    s.free = [r]
                b.free = [tp]
                done.append(r)

            state = {}
            pipe(range(4), scale, turn)
            return done[-1]

        def proj(lT, t, nk, w, c0, n, ring, *tokens):
            s = ring.get()
            pe.need(*s.free, *tokens)
            for k in range(nk):
                r = mm(s.ap[:, 0:n], lT[:, k, t * 128:(t + 1) * 128], w[:, k, c0:c0 + n], k == 0, k == nk - 1)
            return s, pe.mark(r)

        ALLT = range(4)

        class HeadTurn:
            def __init__(self, scr, nh):
                self.sq = Ring([scr.take(nh * 64) for _ in range(2)])
                self.au = Ring([scr.take(nh, 66) for _ in range(2)])
                self.nh = nh
                self.sm = [small.take(nh) for _ in range(4)]

            def norm(self, ps, p0, tp, s, aug, atok):
                nh = self.nh
                q, u = self.sq.get(), self.au.get()
                ss, rs, m, y = self.sm
                ac.need(tp, *q.free)
                t1 = ac.mark(st.activation(q.ap, ps.ap[:, p0:p0 + nh * 64], ACT.Square))
                ve.need(t1)
                t2 = ve.mark(vt.reduce_sum(ss, q.ap.rearrange("p (h d) -> p h d", d=64), AX.X))
                q.free = [t2]
                tr = rstd(rs, ss, 64, (m, y), t2, s)
                ve.need(tr, *u.free)
                t3 = ve.mark(vt.tensor_tensor(u.ap[:, :, 0:64],
                                              ps.ap[:, p0:p0 + nh * 64].rearrange("p (h d) -> p h d", d=64),
                                              bc(rs, 64), ALU.mult))
                ps.free = [t3]
                ve.need(atok)
                for c, src in aug:
                    t3 = ve.mark(vt.tensor_copy(u.ap[:, :, 64 + c[0]:64 + c[1]], src))
                return u, t3

            def turn(self, u, tk, dst, t, gcol):
                pe.need(tk)
                for g in range(0, self.nh, 4):
                    n = min(4, self.nh - g)
                    s = TR.get()
                    pe.need(*s.free)
                    for j in range(n):
                        r = pt_.transpose(s.ap[0:66, j * 128:(j + 1) * 128], u.ap[:, g + j, :], ident)
                    tp = pe.mark(r)
                    ac.need(tp)
                    te = ac.mark(st.activation(dst[0:66, g:g + n, t * 128:(t + 1) * 128],
                                               s.ap[0:66, 0:n * 128].rearrange("p (h q) -> p h q", q=128),
                                               ACT.Copy, scale=PT[0:66, gcol:gcol + 1]))
                    s.free = [te]
                u.free = [tp]
                return te

        class Attend:
            def __init__(self, scr):
                self.P = Ring([scr.take(512) for _ in range(3)])
                self.PT = Ring([scr.take(512) for _ in range(3)])
                self.nm = Ring([small.take(8) for _ in range(2)])
                self.rs = Ring([small.take(8) for _ in range(2)])

            def run(self, qT, kT, V, kd, fin, toks):
                items = [dict(i=i, h=h) for i in ALLT for h in range(8)]

                def score(x):
                    i, h = x["i"], x["h"]
                    L = (i + 1) * 128
                    s = SR.get()
                    pe.need(*s.free, *toks)
                    mm(s.ap[:, 0:L], qT(h)[0:kd, i * 128:(i + 1) * 128], kT(h)[0:kd, 0:L], True, True)
                    tp = pe.mark(mm(s.ap[:, L - 128:L], identb[:, :], causb[:, :], False, True, True))
                    if h == 0:
                        self.m, self.r = self.nm.get(), self.rs.get()
                    nm, rs = self.m, self.r
                    ve.need(tp, *nm.free)
                    tm = ve.mark(vt.tensor_reduce(nm.ap[:, h:h + 1], s.ap[:, 0:L], AX.X, ALU.max, negate=True))
                    p = self.P.get()
                    ac.need(tm, *p.free, *rs.free)
                    x["e"] = ac.mark(st.activation(p.ap[:, 0:L], s.ap[:, 0:L], ACT.Exp, bias=nm.ap[:, h:h + 1],
                                                   accum_out=rs.ap[:, h:h + 1]))
                    s.free = [x["e"]]
                    x["p"], x["rs"], x["nm"] = p, rs, nm
                    if h == 7:
                        nm.free = [x["e"]]

                def turn(x):
                    i = x["i"]
                    L = (i + 1) * 128
                    s, p, q = TR.get(), x["p"], self.PT.get()
                    pe.need(x["e"], *s.free)
                    for j in range(i + 1):
                        r = pt_.transpose(s.ap[:, j * 128:(j + 1) * 128], p.ap[:, j * 128:(j + 1) * 128], ident)
                    tp = pe.mark(r)
                    p.free = [tp]
                    ve.need(tp, *q.free)
                    x["c"] = ve.mark(vt.tensor_copy(q.ap[:, 0:L], s.ap[:, 0:L]))
                    s.free = [x["c"]]
                    x["q"] = q

                def value(x):
                    i, h = x["i"], x["h"]
                    if h == 0:
                        self.o = OR.get()
                        pe.need(*self.o.free)
                    pe.need(x["c"])
                    for j in range(i + 1):
                        r = mm(self.o.ap[:, h * 64:(h + 1) * 64], x["q"].ap[:, j * 128:(j + 1) * 128],
                               V(h, j), j == 0, j == i)
                    tp = pe.mark(r)
                    x["q"].free = [tp]
                    if h == 7:
                        self.o.free = [fin(i, self.o, tp, x["rs"], x["e"])]

                pipe(items, score, turn, value)

        def divide(dst, o, tp, rs, te, scr, gate=None):
            ri = scr
            ve.need(tp, te)
            t = ve.mark(vt.reciprocal(ri, rs.ap))
            rs.free = [t]
            if gate is not None:
                ve.need(t)
                t = ve.mark(vt.tensor_tensor(ri, ri, gate, ALU.mult))
            ve.need(t)
            return ve.mark(vt.tensor_tensor(dst.rearrange("p (h d) -> p h d", d=64),
                                            o.ap.rearrange("p (h d) -> p h d", d=64), bc(ri, 64), ALU.mult))

        def turn4(src, dst, t, n, tok, gcol=None):
            s = TR.get()
            pe.need(tok, *s.free)
            for j in range(n):
                r = pt_.transpose(s.ap[:, j * 128:(j + 1) * 128], src[:, j * 128:(j + 1) * 128], ident)
            tp = pe.mark(r)
            if gcol is None:
                ac.need(tp)
                te = ac.mark(st.activation(dst[:, 0:n, t * 128:(t + 1) * 128],
                                           s.ap[:, 0:n * 128].rearrange("p (k q) -> p k q", q=128), ACT.Copy))
            else:
                ve.need(tp)
                for j in range(n):
                    te = ve.mark(vt.tensor_scalar(dst[:, j, t * 128:(t + 1) * 128], s.ap[:, j * 128:(j + 1) * 128],
                                                  PT[:, gcol + j:gcol + j + 1], None, ALU.mult))
            s.free = [te]
            return te, tp

        smark = small.at
        w = a["w_in"][0]
        ar = Place(AR, ARN)
        foxO = ar.take(4, 512)
        nsaO = ar.take(4, 512)
        base = ar.at
        t_h = norm_turn(HT[:, :, :], 0, Place(AR, ARN, base), [t_x])
        barrier()
        qT = ar.take(8, 512)
        kT = ar.take(8, 512)
        fv = ar.take(4, 512)
        gates = small.take(4, 24)
        cum = small.take(4, 8)
        lf = small.take(4, 8)
        tmp8 = small.take(4, 8)
        off8 = small.take(8)
        scr = Place(AR, ARN, ar.at)
        ht8 = HeadTurn(scr, 8)

        s0 = WR.get()
        v0 = s0.ap[:, 0:8 * 32].rearrange("p (k n) -> p k n", n=32)
        tw1 = wq.copy(v0[:, :, 0:8], wcols(w, 1536, 8), *s0.free)
        tw2 = wq.copy(v0[:, :, 8:32], wcols(w, 2824, 24))
        for t in ALLT:
            s, tp = proj(HT, t, 8, v0, 0, 32, SR, t_h, tw1, tw2)
            ve.need(tp)
            t1 = ve.mark(vt.tensor_tensor(lf[:, t, :], s.ap[:, 0:8], BR[:, 0:8], ALU.add))
            t2 = ve.mark(vt.tensor_copy(gates[:, t, :], s.ap[:, 8:32]))
            s.free = [t2]
        s0.free = [tp]
        ac.need(t1)
        t3 = ac.mark(st.activation(tmp8, lf, ACT.Abs))
        ac.need(t3)
        t3 = ac.mark(st.activation(tmp8, tmp8, ACT.Exp, scale=-1.0))
        ac.need(t3)
        t3 = ac.mark(st.activation(tmp8, tmp8, ACT.Ln, bias=1.0))
        ve.need(t3)
        t4 = ve.mark(vt.scalar_tensor_tensor(out=lf, in0=lf, scalar=0.0, in1=tmp8, op0=ALU.min, op1=ALU.subtract))
        ac.need(t2)
        t5 = ac.mark(st.activation(gates, gates, ACT.Exp, scale=-1.0))
        ve.need(t5)
        t5 = ve.mark(vt.tensor_scalar(gates, gates, 1.0, None, ALU.add))
        ve.need(t5)
        t_g = ve.mark(vt.reciprocal(gates, gates))
        s = OR.get()
        pe.need(t4, *s.free)
        for t in ALLT:
            for j in range(t + 1):
                r = mm(s.ap[:, t * 8:t * 8 + 8], C["tri"] if j == t else C["ones"], lf[:, j, :], j == 0, j == t)
        tp = pe.mark(r)
        ve.need(tp)
        t_cum = ve.mark(vt.tensor_copy(cum, s.ap[:, 0:32].rearrange("p (t h) -> p t h", h=8)))
        s.free = [t_cum]
        ones48 = C["ones"][:, 0:8].unsqueeze(2)

        def heads(wv, tw, dst, aug, gcol, s_, atok):
            st8 = {}

            def p_(t):
                ps, tp = proj(HT, t, 8, wv, 0, 512, SR, tw)
                st8[t] = ht8.norm(ps, 0, tp, s_, aug(t), atok)
                st8["pe"] = tp

            def t_(t):
                st8["e"] = ht8.turn(*st8[t], dst, t, gcol)

            pipe(ALLT, p_, t_)
            return st8["e"], st8["pe"]

        sw, wv, tw = wload(wcols(w, 0, 512), 8, 512)
        t_q, tp = heads(wv, tw, qT, lambda t: [((0, 1), ones48), ((1, 2), cum[:, t, :].unsqueeze(2))], 60, 0.125, t_cum)
        sw.free = [tp]
        ncum = small.take(4, 8)
        ve.need(t_cum)
        t_nc = ve.mark(vt.tensor_scalar(ncum, cum, -1.0, None, ALU.mult))
        sw, wv, tw = wload(wcols(w, 512, 512), 8, 512)
        t_k, tp = heads(wv, tw, kT, lambda t: [((0, 1), ncum[:, t, :].unsqueeze(2)), ((1, 2), ones48)], 61, 1.0, t_nc)
        sw.free = [tp]
        sw, wv, tw = wload(wcols(w, 1024, 512), 8, 512)
        for t in ALLT:
            ps, tp = proj(HT, t, 8, wv, 0, 512, SR, tw)
            ac.need(tp)
            t_v = ac.mark(st.copy(fv[:, t, :], ps.ap))
            ps.free = [t_v]
        sw.free = [tp]
        att = Attend(scr)
        ri8 = small.take(8)

        def fin(i, o, tp, rs, te):
            return divide(foxO[:, i, :], o, tp, rs, te, ri8)

        att.run(lambda h: qT[:, h, :], lambda h: kT[:, h, :], lambda h, j: fv[:, j, h * 64:(h + 1) * 64],
                66, fin, [t_q, t_k, t_v])
        barrier()

        ar.at = scr.at
        nq = qT
        kT2 = kT[:, 0:4, :]
        kcT = kT[:, 4, 0:64]
        kvT = kT[:, 5:7, :]
        vbd = kT[:, 7, :].rearrange("p (g n) -> p g n", n=256)
        vT2 = fv[:, :, 0:256]
        X2 = scr.take(4, 512)
        hidT = scr.take(4, 64)
        posb = small.take(4)
        kcn = small.take(66)
        kcs = [small.take(1) for _ in range(4)]
        sw, wv, tw = wload(wcols(w, 1544, 512), 8, 512)
        t_q, tp = heads(wv, tw, nq, lambda t: [((0, 2), C["qaug"].rearrange("p (t h c) -> p t h c", h=8, c=2)[:, t])],
                        62, 0.125, t_c)
        sw.free = [tp]
        sw, wv, tw = wload(wcols(w, 2056, 256), 8, 256)
        pe.need(tw)
        for c in range(2):
            s = SR.get()
            pe.need(*s.free)
            for k in range(8):
                r = mm(s.ap, wv[:, k, c * 128:(c + 1) * 128], HT[:, k, :], k == 0, k == 7)
            tp = pe.mark(r)
            ac.need(tp)
            tk = ac.mark(st.copy(kvT[:, c, :], s.ap))
            s.free = [tk]
        sw.free = [tp]
        t_z = po.mark(gt.memset(X2[:, :, 511:512], 0.0))
        tx2 = []
        for c in range(2):
            for g in range(2):
                tx2.append(mq.copy(X2[0:64, 2 * c + g, :], kvT[64 * g:64 * g + 64, c, :], tk, t_z))
                tx2.append(mq.copy(X2[64:128, 2 * c + g, 0:511], kvT[64 * g:64 * g + 64, c, 1:512]))
        t_vz = po.mark(gt.memset(vbd, 0.0))
        t_hz = po.mark(gt.memset(hidT, 0.0))
        sv, wv, tw = wload(wcols(w, 2312, 512), 8, 512)
        ht2 = HeadTurn(scr, 2)
        ht2.au = Ring([scr.take(2, 66) for _ in range(4)])
        kvs = Ring([scr.take(256) for _ in range(2)])
        kaug = C["kaug"].rearrange("p (t c) -> p t c", c=2)
        st2 = {}

        def p_(t):
            ps, tp = proj(HT, t, 8, wv, 0, 512, SR, tw)
            kk2 = kvs.get()
            ac.need(tp, *kk2.free)
            for j in range(2):
                ac.mark(st.copy(vT2[:, t, j * 128:(j + 1) * 128], ps.ap[:, 256 * j + 128:256 * j + 256]))
            te = ac.mark(st.copy(kk2.ap.rearrange("p (j n) -> p j n", n=128),
                                 ps.ap.rearrange("p (j n) -> p j n", n=256)[:, :, 0:128]))
            ps.free = [te]
            aug = [((0, 2), mid(kaug[:, t, :], 2))]
            u0 = ht2.norm(kk2, 0, te, 1.0, aug, t_c)
            u1 = ht2.norm(kk2, 128, te, 1.0, aug, t_c)
            st2[t] = (u0, u1)
            st2["pe"], st2["v"] = tp, te

        def t_(t):
            for j in range(2):
                st2["e"] = ht2.turn(*st2[t][j], kT2[:, 2 * j:2 * j + 2, :], t, 63)

        pipe(ALLT, p_, t_)
        sv.free = [st2["pe"]]
        for c, nm_ in enumerate(("k", "v")):
            s1, w1, tw1 = wload(a[f"cmp_{nm_}_w1"][0].rearrange("(j p) n -> p j n", p=128), 16, 256)
            s2, w2, tw2 = wload(a[f"cmp_{nm_}_w2"][0].rearrange("(j p) n -> p j n", p=128), 2, 64)
            xw = X2.rearrange("p c (n s) -> p c n s", s=16)
            for hf in range(2):
                s = OR.get()
                pe.need(*s.free, tw1, tw2, *tx2)
                for j in range(16):
                    mm(s.ap[:, 62:63], w1[:, j, hf * 128:(hf + 1) * 128], PT[:, 64 + 16 * c + j:65 + 16 * c + j],
                       j == 0, j == 15)
                for j in range(16):
                    n0, sft = (0, 2 * j) if j < 8 else (1, 2 * j - 16)
                    r = mm(s.ap[:, 0:62], w1[:, j, hf * 128:(hf + 1) * 128],
                           xw[:, 2 * c:2 * c + 2, n0:n0 + 31, sft], j == 0, j == 15)
                tp = pe.mark(r)
                ve.need(tp)
                tv = ve.mark(vt.tensor_copy(posb[:, 2 * c + hf:2 * c + hf + 1], s.ap[:, 62:63]))
                ac.need(tv, t_hz)
                th = ac.mark(st.activation(
                    hidT[:, 2 * c + hf, :].rearrange("p (g n) -> p g n", n=32)[:, :, 0:31],
                    s.ap[:, 0:62].rearrange("p (g n) -> p g n", n=31), ACT.Gelu_apprx_tanh,
                    bias=posb[:, 2 * c + hf:2 * c + hf + 1]))
                s.free = [th]
            s1.free = [tp]
            s = OR.get()
            pe.need(*s.free, th)
            if c == 0:
                for hf in range(2):
                    r = mm(s.ap[0:64, 0:64], hidT[:, hf, :], w2[:, hf, :], hf == 0, hf == 1)
                tp = pe.mark(r)
                ac.need(tp)
                t1 = ac.mark(st.activation(kcn[0:64, 0:64], s.ap[0:64, 0:64], ACT.Square,
                                           accum_out=kcs[0][0:64, :]))
                t1 = rstd(kcs[1][0:64, :], kcs[0][0:64, :], 64, (kcs[2][0:64, :], kcs[3][0:64, :]), t1)
                ve.need(t1)
                t1 = ve.mark(vt.tensor_scalar(kcn[0:64, 0:64], s.ap[0:64, 0:64], kcs[1][0:64, :], None, ALU.mult))
                t2 = ve.mark(vt.tensor_copy(kcn[0:64, 64:66], C["caug"][0:64, :]))
                s.free = [t1]
                s = TR.get()
                pe.need(t2, *s.free)
                tp = pe.mark(pt_.transpose(s.ap[0:66, 0:64], kcn[0:64, :], ident[0:64, 0:64]))
                ac.need(tp)
                t_kc = ac.mark(st.activation(kcT[0:66, :], s.ap[0:66, 0:64], ACT.Copy, scale=PT[0:66, 63:64]))
                s.free = [t_kc]
            else:
                pe.need(t_vz)
                for g in range(2):
                    for r4 in range(4):
                        for hf in range(2):
                            r = mm(s.ap[32 * r4:32 * r4 + 32, g * 64:g * 64 + 64],
                                   hidT[:, 2 + hf, g * 32:g * 32 + 32], w2[:, hf, :], hf == 0, hf == 1)
                tp = pe.mark(r)
                ve.need(tp, t_vz)
                for g in range(2):
                    for r4 in range(4):
                        t_vc = ve.mark(vt.tensor_copy(vbd[32 * r4:32 * r4 + 32, g, 64 * r4:64 * r4 + 64],
                                                      s.ap[32 * r4:32 * r4 + 32, g * 64:g * 64 + 64]))
                s.free = [t_vc]
            s2.free = [tp]

        ri8b = small.take(8)
        nm8, rs8 = small.take(8), small.take(8)
        anyg = small.take(8)
        pc, pcT = att.P, att.PT
        cm = cmaskb[:, :].rearrange("p (t n) -> p t n", n=32)
        e_prev = None
        for i in ALLT:
            s = SR.get()
            pe.need(*s.free, t_q, t_kc)
            mm(s.ap[:, 0:256], identb[:, :], mid(cm[:, i, :], 8), True, True)
            for h in range(8):
                r = mm(s.ap[:, h * 32:h * 32 + 32], nq[0:66, h, i * 128:(i + 1) * 128],
                       kcT[0:66, (h // 4) * 32:(h // 4) * 32 + 32], False, True, True)
            tp = pe.mark(r)
            sv8 = s.ap[:, 0:256].rearrange("p (h n) -> p h n", n=32)
            ve.need(tp, e_prev)
            t1 = ve.mark(vt.tensor_reduce(nm8, sv8, AX.X, ALU.max, negate=True))
            p = pc.get()
            pv = p.ap[:, 0:256].rearrange("p (h n) -> p h n", n=32)
            ve.need(t1, *p.free)
            t1 = ve.mark(vt.tensor_tensor(pv, sv8, bc(nm8, 32), ALU.add))
            s.free = [t1]
            ac.need(t1)
            t2 = ac.mark(st.activation(p.ap[:, 0:256], p.ap[:, 0:256], ACT.Exp))
            ve.need(t2)
            t3 = ve.mark(vt.reduce_sum(rs8, pv, AX.X))
            ve.need(t3)
            t3 = ve.mark(vt.reciprocal(ri8b, rs8))
            ve.need(t3)
            t3 = ve.mark(vt.tensor_tensor(ri8b, ri8b, gates[:, i, :].rearrange("p (h c) -> p h c", c=3)[:, :, 0], ALU.mult))
            ve.need(t3)
            t3 = ve.mark(vt.tensor_scalar(ri8b, ri8b, C["anyv"][:, i:i + 1], None, ALU.mult))
            s = TR.get()
            pe.need(t2, *s.free)
            for g in range(2):
                r = pt_.transpose(s.ap[:, g * 128:(g + 1) * 128], p.ap[:, g * 128:(g + 1) * 128], ident)
            tp = pe.mark(r)
            p.free = [tp, t3]
            q = pcT.get()
            ve.need(tp, *q.free)
            tc = ve.mark(vt.tensor_copy(q.ap[:, 0:256], s.ap[:, 0:256]))
            s.free = [tc]
            s = OR.get()
            pe.need(tc, t_vc, *s.free)
            for g in range(2):
                r = mm(s.ap[:, g * 256:(g + 1) * 256], q.ap[:, g * 128:(g + 1) * 128], vbd[:, g, :], True, True)
            tp = pe.mark(r)
            q.free = [tp]
            ve.need(tp, t3)
            e_prev = ve.mark(vt.tensor_tensor(nsaO[:, i, :].rearrange("p (h d) -> p h d", d=64),
                                              s.ap.rearrange("p (h d) -> p h d", d=64), bc(ri8b, 64), ALU.mult))
            s.free = [e_prev]

        tmpo = scr.take(512)
        for j in range(2):
            def fin2(i, o, tp, rs, te, j=j):
                g8 = gates[:, i, :].rearrange("p (h c) -> p h c", c=3)[:, :, 1 + j]
                if fin2.prev is not None:
                    ve.need(fin2.prev)
                t = divide(tmpo, o, tp, rs, te, ri8, g8)
                ve.need(t)
                fin2.prev = ve.mark(vt.tensor_tensor(nsaO[:, i, :], nsaO[:, i, :], tmpo, ALU.add))
                return t

            fin2.prev = None
            att.run(lambda h: nq[:, h, :], lambda h, j=j: kT2[:, 2 * j + h // 4, :],
                    lambda h, jt, j=j: vT2[:, jt, j * 128 + (h // 4) * 64:j * 128 + (h // 4) * 64 + 64],
                    66, fin2, [t_q, st2["e"], st2["v"]])
        barrier()

        def merge(lT, w_in, c_a, outs, oTs, mix, mixT, scr, bias=None):
            sg = Ring([scr.take(512) for _ in range(3)])
            tb = Ring([scr.take(512) for _ in range(2)])
            items = []
            for c in range(2):
                for b in range(2):
                    for t in ALLT:
                        items.append((c, b, t))
            cur = {}

            def go(x):
                c, b, t = x
                if t == 0:
                    cur["g"] = wload(wcols(w_in, c_a + 1024 * b + 512 * c, 512), 8, 512)
                    cur["u"] = wload(outs[b][:, 512 * c:512 * c + 512].rearrange("(k p) n -> p k n", p=128), 4, 512)
                sg_, gv, tg = cur["g"]
                su_, uv, tu = cur["u"]
                ps, tp = proj(lT, t, 8, gv, 0, 512, SR, tg)
                z = sg.get()
                if bias is not None:
                    ve.need(tp, *z.free)
                    tz = ve.mark(vt.tensor_tensor(z.ap, ps.ap, bias[:, 1024 * b + 512 * c:1024 * b + 512 * c + 512],
                                                  ALU.add))
                    ps.free = [tz]
                    ac.need(tz)
                    tz = ac.mark(st.activation(z.ap, z.ap, ACT.Sigmoid))
                else:
                    ac.need(tp, *z.free)
                    tz = ac.mark(st.activation(z.ap, ps.ap, ACT.Sigmoid))
                    ps.free = [tz]
                pu, tp2 = proj(oTs[b], t, 4, uv, 0, 512, OR, tu)
                ve.need(tp2, tz)
                m = mix[:, t, c * 512:(c + 1) * 512]
                if b == 0:
                    tm = ve.mark(vt.tensor_tensor(m, pu.ap, z.ap, ALU.mult))
                    pu.free = [tm]
                    z.free = [tm]
                    cur[(c, t)] = tm
                else:
                    y = tb.get()
                    ve.need(*y.free)
                    tm = ve.mark(vt.tensor_tensor(y.ap, pu.ap, z.ap, ALU.mult))
                    pu.free = [tm]
                    z.free = [tm]
                    ve.need(tm, cur[(c, t)])
                    tm = ve.mark(vt.tensor_tensor(m, m, y.ap, ALU.add))
                    y.free = [tm]
                    cur[(c, t)] = tm
                if t == 3:
                    sg_.free = [tp]
                    su_.free = [tp2]

            def tn(x):
                c, b, t = x
                if b == 1:
                    cur["t"], _ = turn4(mix[:, t, c * 512:(c + 1) * 512], mixT[:, 4 * c:4 * c + 4, :], t, 4, cur[(c, t)])

            pipe(items, go, tn)
            return cur["t"]

        ar = Place(AR, ARN, base)
        mix = ar.take(4, 1024)
        mixT = ar.take(8, 512)
        foT = ar.take(4, 512)
        noT = ar.take(4, 512)
        scr = Place(AR, ARN, ar.at)
        for t in ALLT:
            turn4(foxO[:, t, :], foT, t, 4, None)
            te, _ = turn4(nsaO[:, t, :], noT, t, 4, None)
        pe.need(te)
        tm = merge(HT, w, 2848, [a["w_fox_up"][0], a["w_nsa_up"][0]], [foT, noT], mix, mixT, scr)
        for c in range(2):
            sw, wv, tw = wload(wcols(a["w_out"][0], 512 * c, 512), 8, 512)
            for t in ALLT:
                ps, tp = proj(mixT, t, 8, wv, 0, 512, SR, tw, tm)
                ve.need(tp)
                xs = X[:, t, c * 512:(c + 1) * 512]
                tx = ve.mark(vt.tensor_tensor(xs, ps.ap, xs, ALU.add))
                ps.free = [tx]
            sw.free = [tp]
        barrier()

        small.at = smark
        ar = Place(AR, ARN)
        t_h = norm_turn(HT[:, :, :], 8, Place(AR, ARN, 0), [])
        barrier()
        s0 = WR.get()
        v0 = s0.ap[:, 0:160].rearrange("p (k n) -> p k n", n=20)
        tw1 = wq.copy(v0[:, :, 0:4], a["w_group"][0].rearrange("(k p) n -> p k n", p=128), *s0.free)
        tw2 = wq.copy(v0[:, :, 4:20], a["w_router"][0].rearrange("(k p) n -> p k n", p=128))
        lg = small.take(4, 20)
        for t in ALLT:
            s, tp = proj(HT, t, 8, v0, 0, 20, SR, t_h, tw1, tw2)
            ve.need(tp)
            tl = ve.mark(vt.tensor_tensor(lg[:, t, :], s.ap[:, 0:20], BR[:, 8:28], ALU.add))
            s.free = [tl]
        s0.free = [tp]

        def vop(f, *tokens):
            ve.need(ve.last, *tokens)
            return ve.mark(f())

        m1 = small.take(4)
        g1 = small.take(4, 4)
        oh = small.take(4, 4)
        pg = small.take(4)
        e4 = mid(C["e4"], 4)

        def first_max(dst, src, mx, scr4, sc1):
            vop(lambda: vt.reduce_max(mx, src, AX.X))
            vop(lambda: vt.tensor_tensor(scr4, src, bc(mx, 4), ALU.is_ge))
            vop(lambda: vt.tensor_scalar(scr4, scr4, -100.0, 100.0, ALU.mult, ALU.add))
            vop(lambda: vt.tensor_tensor(scr4, scr4, e4, ALU.add))
            vop(lambda: vt.tensor_reduce(sc1, scr4, AX.X, ALU.min))
            return vop(lambda: vt.tensor_tensor(dst, e4, bc(sc1, 4), ALU.is_equal))

        f4, f1 = small.take(4, 4), small.take(4)
        gl = lg[:, :, 0:4]
        first_max(oh, gl, m1, f4, f1)
        t1 = vop(lambda: vt.tensor_tensor(g1, gl, bc(m1, 4), ALU.subtract))
        ac.need(t1)
        t1 = ac.mark(st.activation(g1, g1, ACT.Exp))
        vop(lambda: vt.reduce_sum(pg, g1, AX.X), t1)
        vop(lambda: vt.reciprocal(pg, pg))
        em = small.take(4, 4, 4)
        ein = small.take(4, 4)
        elg = lg[:, :, 4:20]
        for g in range(4):
            vop(lambda: vt.tensor_tensor(em[:, :, g, :], elg[:, :, 4 * g:4 * g + 4], bc(oh[:, :, g], 4), ALU.mult))
        vop(lambda: vt.reduce_sum(ein, em.rearrange("p t g j -> p t j g"), AX.X))
        vop(lambda: vt.reduce_max(m1, ein, AX.X))
        t1 = vop(lambda: vt.tensor_tensor(ein, ein, bc(m1, 4), ALU.subtract))
        ac.need(t1)
        t1 = ac.mark(st.activation(ein, ein, ACT.Exp))
        ve.need(t1)
        o1, o2, e2 = small.take(4, 4), small.take(4, 4), small.take(4, 4)
        p1, p2, ps_ = small.take(4), small.take(4), small.take(4)
        first_max(o1, ein, p1, f4, f1)
        vop(lambda: vt.tensor_scalar(e2, o1, -2.0, None, ALU.mult))
        vop(lambda: vt.tensor_tensor(e2, ein, e2, ALU.add))
        first_max(o2, e2, p2, f4, f1)
        vop(lambda: vt.tensor_tensor(ps_, p1, p2, ALU.add))
        vop(lambda: vt.reciprocal(ps_, ps_))
        vop(lambda: vt.tensor_tensor(ps_, ps_, pg, ALU.mult))
        vop(lambda: vt.tensor_tensor(o1, o1, o2, ALU.add))
        vop(lambda: vt.tensor_tensor(o1, o1, ein, ALU.mult))
        vop(lambda: vt.tensor_tensor(o1, o1, bc(ps_, 4), ALU.mult))
        comb = small.take(4, 16)
        for g in range(4):
            t_comb = vop(lambda: vt.tensor_tensor(comb[:, :, 4 * g:4 * g + 4], o1, bc(oh[:, :, g], 4), ALU.mult))

        hid = Ring([ar.take(4, 512) for _ in range(2)])
        sil = Ring([ar.take(512) for _ in range(3)])
        xt = {}
        est = {}

        def up(e):
            sg_, gv, tg = wload(a["w_gate"][0, e].rearrange("(k p) n -> p k n", p=128), 8, 512)
            su_, uv, tu = wload(a["w_up"][0, e].rearrange("(k p) n -> p k n", p=128), 8, 512)
            H = hid.get()
            for f in range(4):
                pss = []
                for wv_, tw_, rg in ((gv, tg, SR), (uv, tu, TR)):
                    s = rg.get()
                    pe.need(*s.free, tw_)
                    for k in range(8):
                        r = mm(s.ap, wv_[:, k, f * 128:(f + 1) * 128], HT[:, k, :], k == 0, k == 7)
                    pss.append((s, pe.mark(r)))
                (s1, tp1), (s2, tp2) = pss
                z = sil.get()
                ac.need(tp1, *z.free)
                tz = ac.mark(st.activation(z.ap, s1.ap, ACT.Silu))
                s1.free = [tz]
                ve.need(tz, tp2, *H.free)
                th = ve.mark(vt.tensor_tensor(H.ap[:, f, :], s2.ap, z.ap, ALU.mult))
                s2.free = [th]
                z.free = [th]
            sg_.free = [tp1]
            su_.free = [tp2]
            est[e] = (H, th)

        def down(e):
            sd_, dv, td = wload(a["w_down"][0, e].rearrange("(k p) n -> p k n", p=128), 4, 1024)
            H, th = est[e]
            for t in ALLT:
                for c in range(2):
                    s = OR.get()
                    pe.need(*s.free, td, th)
                    for f in range(4):
                        r = mm(s.ap, H.ap[:, f, t * 128:(t + 1) * 128], dv[:, f, c * 512:(c + 1) * 512],
                               f == 0, f == 3)
                    tp = pe.mark(r)
                    xs = X[:, t, c * 512:(c + 1) * 512]
                    ve.need(tp, xt.get((t, c)), t_comb)
                    xt[(t, c)] = ve.mark(vt.scalar_tensor_tensor(out=xs, in0=s.ap, scalar=comb[:, t, e:e + 1],
                                                                 in1=xs, op0=ALU.mult, op1=ALU.add))
                    s.free = [xt[(t, c)]]
            H.free = [tp]
            sd_.free = [tp]

        pipe(range(16), up, down)
        barrier()

        small.at = smark
        w = a["w_in_2"]
        t_h = norm_turn(HT[:, :, :], 16, Place(AR, ARN, 0), [])
        xv = xs_dram.rearrange("(t p) d -> p t d", p=128)
        mq.copy(xv, X[:, :, :])
        barrier()
        ar = Place(AR, ARN)
        oA = ar.take(4, 512)
        oB = ar.take(4, 512)
        base = ar.at

        qT = ar.take(8, 512)
        kT = ar.take(8, 512)
        fv = ar.take(4, 512)
        cT = ar.take(3, 512)
        kpe = ar.take(4, 32)
        cosb = ar.take(4, 16)
        sinb = ar.take(4, 16)
        scr = Place(AR, ARN, ar.at)
        posr = sb("posr", [128, 4], I32)
        posf = small.take(4)
        tpi = mq.copy(posr[:, :], a["positions_2"][0].rearrange("(t p) -> p t", p=128), allow_slow_non_contiguous=True)
        vop(lambda: vt.tensor_copy(posf, posr[:, :]), tpi)
        ang, kk_, rr = scr.take(4, 16), scr.take(4, 16), scr.take(4, 16)
        for t in ALLT:
            vop(lambda: vt.tensor_scalar(ang[:, t, :], C["invf"], posf[:, t:t + 1], None, ALU.mult))
        MAGIC = 12582912.0
        c1 = float(np.float32(6.28125))
        c2 = float(np.float32(TWO_PI - 6.28125))
        c3 = float(np.float32(TWO_PI - 6.28125 - float(np.float32(TWO_PI - 6.28125))))
        hp = float(np.float32(np.pi / 2))
        PIF = 3.1415925
        for dst, q0, ph in ((sinb, 0.0, 0.0), (cosb, 0.25, hp)):
            vop(lambda: vt.tensor_scalar(kk_, ang, float(1.0 / TWO_PI), q0, ALU.mult, ALU.add))
            vop(lambda: vt.tensor_scalar(kk_, kk_, MAGIC, None, ALU.add))
            vop(lambda: vt.tensor_scalar(kk_, kk_, -MAGIC, None, ALU.add))
            vop(lambda: vt.scalar_tensor_tensor(out=rr, in0=kk_, scalar=-c1, in1=ang, op0=ALU.mult, op1=ALU.add))
            vop(lambda: vt.scalar_tensor_tensor(out=rr, in0=kk_, scalar=-c2, in1=rr, op0=ALU.mult, op1=ALU.add))
            vop(lambda: vt.scalar_tensor_tensor(out=rr, in0=kk_, scalar=-c3, in1=rr, op0=ALU.mult, op1=ALU.add))
            vop(lambda: vt.tensor_scalar(rr, rr, ph, PIF, ALU.add, ALU.min))
            t1 = vop(lambda: vt.tensor_scalar(rr, rr, -PIF, None, ALU.max))
            ac.need(t1)
            t1 = ac.mark(st.activation(dst, rr, ACT.Sin))
            ve.need(t1)

        sw, wv, tw = wload(wcols(w, 2176, 416), 8, 416)
        cb = Ring([scr.take(384) for _ in range(2)])
        sqb = scr.take(384)
        sc = [small.take(1) for _ in range(8)]
        for t in ALLT:
            ps, tp = proj(HT, t, 8, wv, 0, 416, SR, tw)
            b = cb.get()
            ve.need(tp)
            tkp = ve.mark(vt.tensor_copy(kpe[:, t, :], ps.ap[:, 384:416]))
            lo = 0
            for n, o, k4 in ((256, 0, 0), (128, 256, 4)):
                ac.need(tp, ve.last)
                t1 = ac.mark(st.activation(sqb[:, o:o + n], ps.ap[:, o:o + n], ACT.Square, accum_out=sc[k4]))
                t1 = rstd(sc[k4 + 1], sc[k4], n, (sc[k4 + 2], sc[k4 + 3]), t1)
                ve.need(t1, *b.free)
                t1 = ve.mark(vt.tensor_scalar(b.ap[:, o:o + n], ps.ap[:, o:o + n], sc[k4 + 1], None, ALU.mult))
            ps.free = [t1, tkp]
            tcT, tpp = turn4(b.ap, cT, t, 3, t1, 57)
            b.free = [tpp]
        sw.free = [tp]
        c3_, s3_ = cosb, sinb
        ra = Ring([scr.take(8, 32) for _ in range(2)])

        def rope(dst, src, t, nh, scr_, tok):
            c, s = mid(cosb[:, t, :], nh), mid(sinb[:, t, :], nh)
            u = scr_
            ve.need(tok)
            ve.mark(vt.tensor_tensor(u[:, 0:nh, 0:16], src[:, :, 16:32], s, ALU.mult))
            t1 = ve.mark(vt.tensor_tensor(u[:, 0:nh, 16:32], src[:, :, 0:16], s, ALU.mult))
            ve.mark(vt.tensor_tensor(dst[:, :, 0:16], src[:, :, 0:16], c, ALU.mult))
            t2 = ve.mark(vt.tensor_tensor(dst[:, :, 16:32], src[:, :, 16:32], c, ALU.mult))
            ve.need(t1, t2)
            ve.mark(vt.tensor_tensor(dst[:, :, 0:16], dst[:, :, 0:16], u[:, 0:nh, 0:16], ALU.subtract))
            return ve.mark(vt.tensor_tensor(dst[:, :, 16:32], dst[:, :, 16:32], u[:, 0:nh, 16:32], ALU.add))

        kpr = scr.take(4, 32)
        for t in ALLT:
            tkr = rope(kpr[:, t:t + 1, :], kpe[:, t:t + 1, :], t, 1, ra.get().ap, tkp)
            ve.need(tkr)
        s1, wq_, tw1 = wload(a["w_uq_2"].rearrange("(k p) n -> p k n", p=128), 2, 768)
        s2, wk_, tw2 = wload(a["w_ukv_2"].rearrange("(k p) n -> p k n", p=128), 1, 1024)
        qb = Ring([scr.take(8, 96) for _ in range(2)])
        msc = 1.0 / float(np.sqrt(96.0))
        qp = scr.take(8, 32)
        stm = {}

        def turn_h(u, tk, dst, t):
            pe.need(tk)
            for g in range(2):
                s = TR.get()
                pe.need(*s.free)
                for j in range(4):
                    r = pt_.transpose(s.ap[0:96, j * 128:(j + 1) * 128], u.ap[:, 4 * g + j, :], ident)
                tp = pe.mark(r)
                ac.need(tp)
                te = ac.mark(st.activation(dst[0:96, 4 * g:4 * g + 4, t * 128:(t + 1) * 128],
                                           s.ap[0:96, :].rearrange("p (h q) -> p h q", q=128), ACT.Copy))
                s.free = [te]
            u.free = [tp]
            return te

        def mq_(t):
            u = qb.get()
            ve.need(*u.free)
            qt = {}
            for hf in range(2):
                ps, tp = proj(cT, t, 2, wq_, 384 * hf, 384, SR, tw1, tcT)
                v = ps.ap[:, 0:384].rearrange("p (h d) -> p h d", d=96)
                ve.need(tp)
                t1 = ve.mark(vt.tensor_scalar(u.ap[:, 4 * hf:4 * hf + 4, 0:64], v[:, :, 0:64], msc, None, ALU.mult))
                t2 = ve.mark(vt.tensor_scalar(qp[:, 4 * hf:4 * hf + 4, :], v[:, :, 64:96], msc, None, ALU.mult))
                ps.free = [t2]
            t3 = rope(u.ap[:, :, 64:96], qp, t, 8, ra.get().ap, t2)
            stm[("q", t)] = (u, t3)
            stm["pe"] = tp

        def mk_(t):
            u = qb.get()
            ve.need(*u.free)
            for hf in range(2):
                s = SR.get()
                pe.need(*s.free, tw2, tcT)
                tp = pe.mark(mm(s.ap, cT[:, 2, t * 128:(t + 1) * 128], wk_[:, 0, 512 * hf:512 * hf + 512], True, True))
                v = s.ap.rearrange("p (h d) -> p h d", d=128)
                ve.need(tp)
                t1 = ve.mark(vt.tensor_copy(u.ap[:, 4 * hf:4 * hf + 4, 0:64], v[:, :, 0:64]))
                ac.need(tp, t1)
                t2 = ac.mark(st.copy(fv[:, t, 256 * hf:256 * hf + 256].rearrange("p (h d) -> p h d", d=64),
                                     v[:, :, 64:128]))
                s.free = [t2]
            t3 = ve.mark(vt.tensor_copy(u.ap[:, :, 64:96], mid(kpr[:, t, :], 8)))
            stm[("k", t)] = (u, t3)
            stm["pe"], stm["v"] = tp, t2

        for t in ALLT:
            mq_(t)
            mk_(t)
            stm["e"] = turn_h(*stm[("q", t)], qT, t)
            stm["e"] = turn_h(*stm[("k", t)], kT, t)
        s1.free = [stm["pe"]]
        s2.free = [stm["pe"]]
        att = Attend(scr)
        ri8 = small.take(8)

        def fin3(i, o, tp, rs, te):
            return divide(oB[:, i, :], o, tp, rs, te, ri8)

        att.run(lambda h: qT[:, h, :], lambda h: kT[:, h, :], lambda h, j: fv[:, j, h * 64:(h + 1) * 64],
                96, fin3, [stm["e"], stm["v"]])
        barrier()

        ar = Place(AR, ARN, base)
        rT, kkT, vT, cumT = (ar.take(4, 512) for _ in range(4))
        aT = ar.take(4, 512)
        wa = ar.take(512)
        scr = Place(AR, ARN, ar.at)
        raw = Ring([scr.take(513) for _ in range(2)])
        dif = Ring([scr.take(512) for _ in range(2)])
        for r_ in raw.slots:
            r_.free = [po.mark(gt.memset(r_.ap[:, 0:1], 0.0))]
        dst = [rT, kkT, vT]
        tf = {}
        for n in range(13):
            if n % 4 == 0:
                wd_ = min(512, 1664 - 128 * n)
                sw, wv, tw = wload(wcols(w, 128 * n, wd_), 8, wd_)
            s = SR.get()
            pe.need(*s.free, tw)
            for k in range(8):
                r = mm(s.ap, wv[:, k, (n % 4) * 128:(n % 4) * 128 + 128], HT[:, k, :], k == 0, k == 7)
            tp = pe.mark(r)
            if n % 4 == 3 or n == 12:
                sw.free = [tp]
            b, d = raw.get(), dif.get()
            ac.need(tp, *b.free)
            t1 = ac.mark(st.copy(b.ap[:, 1:513], s.ap))
            s.free = [t1]
            ve.need(t1, *d.free, *b.free)
            t2 = ve.mark(vt.tensor_tensor(d.ap, b.ap[:, 0:512], b.ap[:, 1:513], ALU.subtract))
            o = dst[n // 4][:, n % 4, :] if n < 12 else wa
            ve.need(t2)
            t3 = ve.mark(vt.scalar_tensor_tensor(out=o, in0=d.ap, scalar=PT[:, 24 + n:25 + n], in1=b.ap[:, 1:513],
                                                 op0=ALU.mult, op1=ALU.add))
            b.free, d.free = [t3], [t3]
        t_f = t3
        s1, wl, tw1 = WR.get(), None, None
        wl = s1.ap[:, 0:512]
        tw1 = wq.copy(wl[0:64, :], a["w_decay_up_2"], *s1.free)
        tw2 = wq.copy(wl[64:128, :], a["w_iclr_up_2"])
        ac.need(t_f)
        t1 = ac.mark(st.activation(wa[0:64, :], wa[0:64, :], ACT.Tanh))
        for n in range(4):
            for j, (p0, col, d_) in enumerate(((0, 37, cumT), (64, 41, aT))):
                s = OR.get()
                pe.need(*s.free, t1, tw1, tw2)
                tp = pe.mark(mm(s.ap, wl[p0:p0 + 64, n * 128:(n + 1) * 128], wa[p0:p0 + 64, :], True, True))
                ac.need(tp)
                t2 = ac.mark(st.activation(d_[:, n, :], s.ap, ACT.Sigmoid, bias=PT[:, col + n:col + n + 1]))
                s.free = [t2]
        s1.free = [tp]
        t_sg = t2
        be = scr.take(4, 512)
        bufs = Ring([scr.take(512) for _ in range(2)])
        rkb = small.take(4)
        kap = kkT
        al = ar_al = None
        kn_at = scr.at
        kn = scr.take(4, 512)
        sel = small.take(4, 2)
        for n in range(4):
            ve.need(ve.last)
            ve.mark(vt.tensor_scalar(sel[:, n, :], C["hsel"], PT[:, 53 + n:54 + n], None, ALU.mult))
        dia = scr.take(4, 8)
        for n in range(4):
            b = bufs.get()
            t1 = vop(lambda: vt.tensor_scalar(kn[:, n, :], kkT[:, n, :], PT[:, 45 + n:46 + n], None, ALU.mult))
            ac.need(t1, *b.free)
            t2 = ac.mark(st.activation(b.ap, kn[:, n, :], ACT.Square))
            s = OR.get()
            pe.need(t2, *s.free)
            tp = pe.mark(mm(s.ap, C["bd"], b.ap, True, True))
            ve.need(tp)
            m_ = b.ap
            t3 = vop(lambda: vt.tensor_scalar(m_, s.ap, 1e-24, None, ALU.max))
            s.free = [t3]
            b2 = bufs.get()
            y_ = b2.ap
            ac.need(t3)
            t4 = ac.mark(st.activation(y_, m_, ACT.Sqrt, scale=float(2.0 ** 40)))
            vop(lambda: vt.reciprocal(y_, y_), t4)
            vop(lambda: vt.tensor_scalar(y_, y_, float(2.0 ** 20), None, ALU.mult))
            vop(lambda: vt.tensor_tensor(m_, m_, y_, ALU.mult))
            vop(lambda: vt.tensor_tensor(m_, m_, y_, ALU.mult))
            vop(lambda: vt.tensor_scalar(m_, m_, -0.5, 1.5, ALU.mult, ALU.add))
            vop(lambda: vt.tensor_tensor(y_, y_, m_, ALU.mult))
            vop(lambda: vt.tensor_tensor(kn[:, n, :], kn[:, n, :], y_, ALU.mult))
            vop(lambda: vt.tensor_tensor(be[:, n, :], kn[:, n, :], aT[:, n, :], ALU.mult), t_sg)
            vop(lambda: vt.tensor_scalar(m_, aT[:, n, :], 1.0, PT[:, 49 + n:50 + n], ALU.subtract, ALU.mult))
            t5 = vop(lambda: vt.scalar_tensor_tensor(out=kkT[:, n, :], in0=m_, scalar=1.0, in1=kkT[:, n, :],
                                                     op0=ALU.add, op1=ALU.mult))
            t6 = vop(lambda: vt.tensor_tensor(m_, rT[:, n, :], kkT[:, n, :], ALU.mult))
            s = OR.get()
            pe.need(t6, *s.free)
            for t in ALLT:
                r = mm(s.ap[:, 2 * t:2 * t + 2], m_[:, t * 128:(t + 1) * 128], sel[:, n, :], True, True)
            tp = pe.mark(r)
            b.free = [tp]
            t7 = vop(lambda: vt.tensor_copy(dia[:, :, 2 * n:2 * n + 2],
                                            s.ap[:, 0:8].rearrange("p (t c) -> p t c", c=2)), tp)
            s.free = [t7]
            b2.free = [t7]
        scn = bufs.get().ap
        on = bufs.get().ap
        po.need(*[x for b_ in bufs.slots for x in b_.free])
        to = po.mark(gt.memset(on, 1.0))
        dmid = small.take(4, 4)
        dend = small.take(4, 4)
        for n in range(4):
            for c in ALLT:
                vop(lambda: vt.tensor_tensor_scan(scn[:, c * 128:(c + 1) * 128], on[:, 0:128],
                                                  cumT[:, n, c * 128:(c + 1) * 128], 0.0, ALU.mult, ALU.add), to)
            for c in ALLT:
                vop(lambda: vt.tensor_copy(dmid[:, n, c:c + 1], scn[:, c * 128 + 63:c * 128 + 64]))
            t1 = vop(lambda: vt.tensor_tensor(scn.rearrange("p (c q) -> p c q", q=128),
                                              scn.rearrange("p (c q) -> p c q", q=128),
                                              bc(dmid[:, n, :], 128), ALU.subtract))
            t2 = vop(lambda: vt.tensor_tensor(aT[:, n, :], scn, cumT[:, n, :], ALU.subtract))
            ac.need(t2)
            t3 = ac.mark(st.activation(aT[:, n, :], aT[:, n, :], ACT.Exp, scale=-DECAY))
            t4 = ac.mark(st.activation(cumT[:, n, :], scn, ACT.Exp, scale=-DECAY))
            t5 = ac.mark(st.activation(scn, scn, ACT.Exp, scale=DECAY))
            vop(lambda: vt.scalar_tensor_tensor(out=kn[:, n, :], in0=kn[:, n, :], scalar=-1.0, in1=aT[:, n, :],
                                                op0=ALU.mult, op1=ALU.mult), t3)
            vop(lambda: vt.tensor_copy(dend[:, n, :], cumT[:, n, :].rearrange("p (c q) -> p c q", q=128)[:, :, 127]), t4)
            vop(lambda: vt.tensor_tensor(rT[:, n, :], rT[:, n, :], cumT[:, n, :], ALU.mult))
            vop(lambda: vt.tensor_tensor(be[:, n, :], be[:, n, :], scn, ALU.mult), t5)
            vop(lambda: vt.tensor_tensor(kkT[:, n, :], kkT[:, n, :], scn, ALU.mult))
        t1 = ve.last
        ac.need(t1)
        t_dm = ac.mark(st.activation(dmid, dmid, ACT.Exp, scale=-DECAY))
        barrier()

        alT, beT, kaT = kn, be, kkT
        scr2 = Place(AR, ARN, scr.at)
        vTM = ar_v = aT
        beTM = cumT
        kaTM = scr2.take(4, 512)
        for src, d_ in ((vT, vTM), (beT, beTM), (kaT, kaTM)):
            for n in range(4):
                s = TR.get()
                pe.need(*s.free)
                for t in ALLT:
                    r = pt_.transpose(s.ap[:, t * 128:(t + 1) * 128], src[:, n, t * 128:(t + 1) * 128], ident)
                tp = pe.mark(r)
                ac.need(tp)
                te = ac.mark(st.copy(d_[:, :, n * 128:(n + 1) * 128], s.ap.rearrange("p (t c) -> p t c", c=128)))
                s.free = [te]
        barrier()
        fr = Place(X[:, :, :].rearrange("p a b -> p (a b)"), 4096)
        w8 = lambda: fr.take(8, 128)
        LT, AK, RB, RK = vT.rearrange("p a b -> p (a b)")[:, 0:1024].rearrange("p (h t) -> p h t", t=128), w8(), \
            vT.rearrange("p a b -> p (a b)")[:, 1024:2048].rearrange("p (h t) -> p h t", t=128), w8()
        raws = Place(AR, ARN, ar.at - 512)
        T0 = raws.take(8, 128)
        TT0 = raws.take(8, 128)
        MS = w8()
        UU = w8()
        fr = Place(AR, ARN, scr2.at)
        S0 = bufs.slots[0].ap.rearrange("p (a b) -> p a b", b=128)
        SA = bufs.slots[1].ap
        RHS = fr.take(512)
        for z in (LT, AK, RB, RK):
            po.mark(gt.memset(z, 0.0))
        t_z = po.mark(gt.memset(S0, 0.0))
        ys = oA
        stri = C["stri"].bitcast(U32)
        tri = C["tri"].bitcast(U32)

        def two(dst, f):
            res = []
            for par in range(2):
                s = SR.get()
                pe.need(*s.free)
                for j in range(4):
                    l_, r_ = f(2 * j + par)
                    r = mm(s.ap[:, j * 128:(j + 1) * 128], l_, r_, True, True)
                res.append((s, pe.mark(r)))
            return res

        t_s = t_z
        for c in ALLT:
            cs = slice(c * 128, (c + 1) * 128)

            def hT(x, h):
                return x[64 * (h % 2):64 * (h % 2) + 64, h // 2, cs]

            for dst_, lx, rx, mk in ((LT, beT, alT, stri), (AK, kaT, alT, stri), (RB, beT, rT, tri), (RK, kaT, rT, tri)):
                for par, (s, tp) in enumerate(two(dst_, lambda h: (hT(lx, h), hT(rx, h)))):
                    v = dst_.rearrange("p (a b) t -> p a b t", b=2)[:, :, par, :]
                    ve.need(tp, t_z, pe.last)
                    te = ve.mark(vt.copy_predicated(v, mid(mk, 4), s.ap.rearrange("p (a t) -> p a t", t=128)))
                    s.free = [te]
            t1 = vop(lambda: vt.tensor_tensor(TT0, LT, mid(C["lv1"], 8), ALU.mult))
            t1 = vop(lambda: vt.tensor_tensor(TT0, TT0, mid(ident, 8), ALU.add))
            for g in range(2):
                s = TR.get()
                pe.need(*s.free, t1)
                for j in range(4):
                    r = pt_.transpose(s.ap[:, j * 128:(j + 1) * 128], TT0[:, 4 * g + j, :], ident)
                tp = pe.mark(r)
                ac.need(tp, pe.last)
                te = ac.mark(st.copy(T0[:, 4 * g:4 * g + 4, :], s.ap.rearrange("p (h t) -> p h t", t=128)))
                s.free = [te]
            tT = te
            tTT = t1
            for m in (2, 4, 8, 16, 32, 64):
                po.need(ve.last, pe.last)
                tM = po.mark(gt.tensor_tensor(MS, LT, mid(C[f"lv{m}"], 8), ALU.mult))
                for g in range(2):
                    s = SR.get()
                    pe.need(*s.free, tM, tT, tTT)
                    for j in range(4):
                        r = mm(s.ap[:, j * 128:(j + 1) * 128], MS[:, 4 * g + j, :], T0[:, 4 * g + j, :], True, True)
                    tp = pe.mark(r)
                    ac.need(tp)
                    tU = ac.mark(st.copy(UU[:, 4 * g:4 * g + 4, :], s.ap.rearrange("p (h t) -> p h t", t=128)))
                    s.free = [tU]
                nxt = []
                for g in range(2):
                    pe.need(tU)
                    for kind in range(2):
                        if kind == 0 and m == 64:
                            continue
                        s = TR.get() if kind else SR.get()
                        pe.need(*s.free)
                        for j in range(4):
                            h = 4 * g + j
                            if kind == 0:
                                r = mm(s.ap[:, j * 128:(j + 1) * 128], TT0[:, h, :], UU[:, h, :], True, True)
                            else:
                                r = mm(s.ap[:, j * 128:(j + 1) * 128], UU[:, h, :], TT0[:, h, :], True, True)
                        nxt.append((g, kind, s, pe.mark(r)))
                for g, kind, s, tp in nxt:
                    d_ = (T0, TT0)[kind][:, 4 * g:4 * g + 4, :]
                    ve.need(pe.last)
                    te = ve.mark(vt.tensor_tensor(d_, s.ap.rearrange("p (h t) -> p h t", t=128), d_, ALU.add))
                    s.free = [te]
                tT = tTT = te
            if c == 0:
                t_s0 = t_z
            ve.need(t_s, t_dm)
            for n in range(4):
                t_s0 = ve.mark(vt.tensor_scalar(S0[:, n, :], S0[:, n, :], dmid[:, n, c:c + 1], None, ALU.mult))
            s = OR.get()
            pe.need(*s.free, t_s0, tT)
            for n in range(4):
                mm(s.ap[:, n * 128:(n + 1) * 128], alT[:, n, cs], S0[:, n, :], n == 0, True, True)
            for h in range(8):
                r = mm(s.ap[:, h * 64:(h + 1) * 64], AK[:, h, :], vTM[:, c, h * 64:(h + 1) * 64], False, True, True)
            tp = pe.mark(r)
            ac.need(tp)
            t1 = ac.mark(st.copy(RHS, s.ap))
            s.free = [t1]
            s = OR.get()
            pe.need(*s.free, t1)
            for h in range(8):
                r = mm(s.ap[:, h * 64:(h + 1) * 64], TT0[:, h, :], RHS[:, h * 64:(h + 1) * 64], True, True)
            tp = pe.mark(r)
            ac.need(tp)
            t1 = ac.mark(st.copy(SA, s.ap))
            s.free = [t1]
            s = OR.get()
            pe.need(*s.free, t1)
            for n in range(4):
                mm(s.ap[:, n * 128:(n + 1) * 128], rT[:, n, cs], S0[:, n, :], n == 0, True, True)
            for h in range(8):
                mm(s.ap[:, h * 64:(h + 1) * 64], RB[:, h, :], SA[:, h * 64:(h + 1) * 64], False, True, True)
                r = mm(s.ap[:, h * 64:(h + 1) * 64], RK[:, h, :], vTM[:, c, h * 64:(h + 1) * 64], False, True, True)
            tp = pe.mark(r)
            ac.need(tp)
            t1 = ac.mark(st.copy(ys[:, c, :], s.ap))
            s.free = [t1]
            s = SR.get()
            pe.need(*s.free)
            for n in range(4):
                mm(s.ap[:, n * 128:(n + 1) * 128], beTM[:, c, n * 128:(n + 1) * 128], SA[:, n * 128:(n + 1) * 128],
                   True, False)
                r = mm(s.ap[:, n * 128:(n + 1) * 128], kaTM[:, c, n * 128:(n + 1) * 128],
                       vTM[:, c, n * 128:(n + 1) * 128], False, True)
            tp = pe.mark(r)
            ve.need(tp)
            for par in range(2):
                q = slice(64 * par, 64 * par + 64)
                sv_ = s.ap[q, :].rearrange("p (n v) -> p n v", v=128)[:, :, 64 * par:64 * par + 64]
                S_ = S0[q, :, 64 * par:64 * par + 64]
                vop(lambda: vt.tensor_tensor(S_, sv_, S_, ALU.add))
                t_s = vop(lambda: vt.tensor_tensor(S_, S_, bc(dend[q, :, c], 64), ALU.mult))
            s.free = [ve.last]
        barrier()

        mq.copy(X[:, :, :], xv)

        ar = Place(AR, ARN, base)
        vTM_ = vTM
        nf = Place(AR, ARN, scr2.at)
        gnb = nf.take(1024)
        bgb = rT.rearrange("p a b -> p (a b)")
        gpb = be.rearrange("p a b -> p (a b)")[:, 0:1024]
        tg = [mq.copy(gnb[:, 0:512], a["gn_gain_2"].unsqueeze(0).to_broadcast([128, 512])),
              mq.copy(gnb[:, 512:1024], a["gn_bias_2"].unsqueeze(0).to_broadcast([128, 512])),
              mq.copy(bgb, a["b_gate_2"].unsqueeze(0).to_broadcast([128, 2048])),
              mq.copy(gpb, a["g_post_2"].unsqueeze(0).to_broadcast([128, 1024]))]
        ve.need(*tg)
        v8 = lambda x: x.rearrange("p (h d) -> p h d", d=64)
        t8 = [b_.ap for b_ in bufs.slots]
        mu8, va8, rs8, m8, y8 = (small.take(8) for _ in range(5))
        for t in ALLT:
            y = v8(ys[:, t, :])
            vop(lambda: vt.reduce_sum(mu8, y, AX.X))
            vop(lambda: vt.tensor_scalar(mu8, mu8, 1.0 / 64, None, ALU.mult))
            t1 = vop(lambda: vt.tensor_tensor(y, y, bc(mu8, 64), ALU.subtract))
            ac.need(t1)
            t2 = ac.mark(st.activation(t8[0], ys[:, t, :], ACT.Square))
            t3 = vop(lambda: vt.reduce_sum(va8, v8(t8[0]), AX.X), t2)
            rstd(rs8, va8, 64, (m8, y8), t3, 1.0, GN_EPS)
            vop(lambda: vt.tensor_tensor(y, y, bc(rs8, 64), ALU.mult))
            vop(lambda: vt.tensor_tensor(ys[:, t, :], ys[:, t, :], gnb[:, 0:512], ALU.mult))
            vop(lambda: vt.tensor_tensor(ys[:, t, :], ys[:, t, :], gnb[:, 512:1024], ALU.add))
            vop(lambda: vt.tensor_tensor(v8(t8[1]), v8(vTM[:, t, :]), bc(dia[:, t, :], 64), ALU.mult))
            vop(lambda: vt.tensor_tensor(ys[:, t, :], ys[:, t, :], t8[1], ALU.add))
        for c0, o_ in ((1664, oA), (2592, oB)):
            sw, wv, tw = wload(wcols(w, c0, 512), 8, 512)
            for t in ALLT:
                ps, tp = proj(HT, t, 8, wv, 0, 512, SR, tw)
                ac.need(tp, ve.last)
                t1 = ac.mark(st.activation(t8[t % 2], ps.ap, ACT.Silu))
                ps.free = [t1]
                vop(lambda: vt.tensor_tensor(o_[:, t, :], o_[:, t, :], t8[t % 2], ALU.mult), t1)
            sw.free = [tp]
        barrier()
        oAT, oBT = kkT, vT
        for t in ALLT:
            turn4(oA[:, t, :], oAT, t, 4, None)
            te, _ = turn4(oB[:, t, :], oBT, t, 4, None)
        pe.need(te)
        mx = AR[:, base + 3 * 2048:base + 5 * 2048].rearrange("p (a b) -> p a b", b=1024)
        mxT = AR[:, kn_at:kn_at + 4096].rearrange("p (a b) -> p a b", b=512)
        mscr = Place(AR, base + 5 * 2048 + 512 + 2050, base + 5 * 2048)
        tm = merge(HT, w, 3104, [a["w_out_a_2"], a["w_out_b_2"]], [oAT, oBT], mx, mxT, mscr, bgb)
        barrier()
        yo = mx
        for c in range(2):
            sw, wv, tw = wload(wcols(a["w_o_2"], 512 * c, 512), 8, 512)
            for t in ALLT:
                ps, tp = proj(mxT, t, 8, wv, 0, 512, SR, tw, tm)
                ac.need(tp)
                t1 = ac.mark(st.copy(yo[:, t, c * 512:(c + 1) * 512], ps.ap))
                ps.free = [t1]
            sw.free = [tp]
        ss, rs, m, y = (small.take(4) for _ in range(4))
        junk = HT[:, 0:2, :].rearrange("p a b -> p (a b)")
        barrier()
        for t in ALLT:
            ac.need(ac.last)
            t1 = ac.mark(st.activation(junk, yo[:, t, :], ACT.Square, accum_out=ss[:, t:t + 1]))
        rstd(rs, ss, 1024, (m, y), t1)
        outv = out[0].rearrange("(t p) d -> p t d", p=128)
        for t in ALLT:
            vop(lambda: vt.scalar_tensor_tensor(out=yo[:, t, :], in0=yo[:, t, :], scalar=rs[:, t:t + 1], in1=gpb,
                                                op0=ALU.mult, op1=ALU.mult))
            t2 = vop(lambda: vt.tensor_tensor(yo[:, t, :], yo[:, t, :], X[:, t, :], ALU.add))
            oq.copy(outv[:, t, :], yo[:, t, :], t2)
        sy.need(*oq.outstanding())


_INS = ["x", "norm_mix_g", "w_in", "b_forget", "fox_q_g", "fox_k_g", "nsa_q_g", "nsa_k_g", "cmp_k_w1", "cmp_k_w2",
        "cmp_k_pos", "cmp_v_w1", "cmp_v_w2", "cmp_v_pos", "w_fox_up", "w_nsa_up", "w_out", "norm_ffn_g", "w_group",
        "b_group", "w_router", "b_router", "w_gate", "w_up", "w_down", "positions_2", "g_pre_2", "w_in_2",
        "b_gate_2", "mu_shift_2", "w0_2", "w_decay_up_2", "a0_2", "w_iclr_up_2", "k_k_2", "k_a_2", "r_k_2",
        "gn_gain_2", "gn_bias_2", "w_out_a_2", "g_q_2", "w_uq_2", "g_kv_2", "w_ukv_2", "w_out_b_2", "w_o_2",
        "g_post_2"]


def kernel(**inputs):
    import numpy as _np
    import concourse.bacc as _bacc
    from concourse import mybir as _mybir
    from concourse.bass_utils import run_bass_kernel_spmd as _run

    nc = _bacc.Bacc("TRN2", target_bir_lowering=False, num_devices=1)
    consts, coff = constants()
    arrays, args = {}, {}
    for name in _INS:
        arrays[f"in_{name}_dram"] = _np.ascontiguousarray(inputs[name])
    arrays["in_consts_dram"] = consts
    for key, arr in arrays.items():
        args[key[3:-5]] = nc.dram_tensor(key, arr.shape, _mybir.dt.from_np(arr.dtype), kind="ExternalInput").ap()
    out = nc.dram_tensor("out_0_dram", (1, 512, 1024), _mybir.dt.float32, kind="ExternalOutput").ap()
    spill = nc.dram_tensor("spill", (512, 1024), _mybir.dt.float32, kind="Internal").ap()
    build(nc, args, coff, out, spill)
    r = _run(nc, [arrays], core_ids=[0])
    return r.results[0]["out_0_dram"]
```

```python
from contextlib import ExitStack

import numpy as np

import concourse.bass as bass
from concourse import mybir

F32 = mybir.dt.float32
BF16 = mybir.dt.bfloat16
U32 = mybir.dt.uint32
I32 = mybir.dt.int32
ALU = mybir.AluOpType
ACT = mybir.ActivationFunctionType
AX = mybir.AxisListType

EPS = 1e-6
GN_EPS = 64e-5
NEG = -1e30
DECAY = 0.6065306597
TWO_PI = 2.0 * np.pi


def constants():
    p = np.arange(128)
    parts, off = [], {}

    def put(name, a):
        a = np.asarray(a, np.float32).reshape(128, -1)
        off[name] = (sum(x.shape[1] for x in parts), a.shape[1])
        parts.append(a)

    put("ident", np.eye(128))
    put("tri", (p[:, None] <= p[None, :]))
    put("stri", (p[:, None] < p[None, :]))
    put("ones", np.ones((128, 128)))
    put("bd", (p[:, None] // 64 == p[None, :] // 64))
    put("causal", np.where(p[None, :] <= p[:, None], 0.0, NEG))
    q = p[:, None] + 128 * np.arange(4)[None, :]
    n = np.arange(32)
    ok = (n[None, None, :] * 16 + 31 <= q[:, :, None]) & (n < 31)[None, None, :]
    put("cmask", np.where(ok, 0.0, NEG))
    put("anyv", (q >= 31))
    sl = 2.0 ** -(np.arange(8) + 1.0)
    qa = np.zeros((128, 4, 8, 2))
    qa[..., 0] = sl[None, None, :]
    qa[..., 1] = -sl[None, None, :] * q[:, :, None]
    put("qaug", qa)
    ka = np.zeros((128, 4, 2))
    ka[..., 0] = q
    ka[..., 1] = 1.0
    put("kaug", ka)
    ca = np.zeros((128, 2))
    ca[:, 0] = np.where(p % 32 < 31, (p % 32) * 16 + 31, 0)
    ca[:, 1] = 1.0
    put("caug", ca)
    for m in (1, 2, 4, 8, 16, 32, 64):
        j, t = p[:, None] // m, p[None, :] // m
        put(f"lv{m}", (t % 2 == 1) & (j == t - 1))
    put("hsel", (p[:, None] // 64 == np.arange(2)[None, :]))
    inv = (np.float32(10000.0) ** (-np.arange(0, 32, 2, dtype=np.float32) / np.float32(32))).astype(np.float32)
    put("invf", np.broadcast_to(inv, (128, 16)))
    put("e4", np.broadcast_to(np.arange(4), (128, 4)))
    put("e16", np.broadcast_to(np.arange(16), (128, 16)))
    put("b7", np.broadcast_to(np.arange(7)[:, None], (128, 7, 16)))
    return np.concatenate(parts, 1), off


class Engine:

    def __init__(self, eng, sem):
        self.eng, self.sem, self.n, self.seen, self.queue = eng, sem, 0, {}, None

    def need(self, *tokens):
        for t in tokens:
            if t is not None and self.seen.get(t[0], 0) < t[2]:
                self.run(lambda sem=t[1], n=t[2]: self.eng.wait_ge(sem, n))
                self.seen[t[0]] = t[2]

    def run(self, f):
        if self.queue is None:
            f()
        else:
            self.queue.append(f)

    def mark(self, ins):
        self.n += 1
        ins.then_inc(self.sem, 1)
        return (id(self), self.sem, self.n)

    def later(self, f):
        self.n += 1
        self.run(lambda: f().then_inc(self.sem, 1))
        return (id(self), self.sem, self.n)

    @property
    def last(self):
        return (id(self), self.sem, self.n) if self.n else None

    def skip(self, n):
        self.eng.wait_ge(self.sem, n)
        if self.n > n:
            self.eng.sem_inc(self.sem, self.n - n)


class Queue:

    def __init__(self, engine, sems):
        self.engine, self.sems, self.n = engine, sems, 0

    def copy(self, dst, src, *tokens, **kw):
        return self.issue(lambda: self.engine.eng.dma_start(dst, src, **kw), *tokens)

    def gather(self, dst, src, rows, *tokens):
        at = bass.IndirectOffsetOnAxis(ap=rows, axis=0)
        return self.issue(lambda: self.engine.eng.indirect_dma_start(dst, None, src, at), *tokens)

    def scatter(self, dst, src, rows, *tokens):
        at = bass.IndirectOffsetOnAxis(ap=rows, axis=0)
        return self.issue(lambda: self.engine.eng.indirect_dma_start(dst, at, src, None), *tokens)

    def issue(self, start, *tokens):
        i = self.n % len(self.sems)
        self.engine.need(*tokens, self.token(self.n - len(self.sems)))
        self.engine.run(lambda: start().then_inc(self.sems[i], 16))
        self.n += 1
        return self.token(self.n - 1)

    def token(self, k):
        if k < 0:
            return None
        i = k % len(self.sems)
        return ((id(self), i), self.sems[i], 16 * (k // len(self.sems) + 1))

    def skip(self, n):
        for i in range(len(self.sems)):
            before, after = (len(range(i, k, len(self.sems))) for k in (n, self.n))
            if before:
                self.engine.eng.wait_ge(self.sems[i], 16 * before)
            if after > before:
                self.engine.eng.sem_inc(self.sems[i], 16 * (after - before))

    def outstanding(self):
        return [self.token(k) for k in range(max(0, self.n - len(self.sems)), self.n)]


class Slot:
    def __init__(self, ap):
        self.ap, self.free = ap, []


class Ring:
    def __init__(self, aps):
        self.slots, self.n = [Slot(a) for a in aps], 0

    def get(self):
        self.n += 1
        return self.slots[(self.n - 1) % len(self.slots)]


def pipe(items, *stages):
    for step in range(len(items) + len(stages) - 1):
        for s, stage in enumerate(stages):
            if 0 <= step - s < len(items):
                stage(items[step - s])


def build(nc, a, coff, out, xs_dram, tab_dram, ys_dram):
    with ExitStack() as ctx:
        sem = lambda name: ctx.enter_context(nc.semaphore(name))
        pe = Engine(nc.tensor, sem("s_pe"))
        ve = Engine(nc.vector, sem("s_ve"))
        ac = Engine(nc.scalar, sem("s_ac"))
        po = Engine(nc.gpsimd, sem("s_po"))
        sy = Engine(nc.sync, sem("s_sy"))
        wq = Queue(sy, [sem(f"s_w{i}") for i in range(12)])
        mq = Queue(po, [sem(f"s_m{i}") for i in range(24)])
        xq = Queue(po, [sem(f"s_x{i}") for i in range(8)])
        oq = Queue(sy, [sem(f"s_o{i}") for i in range(4)])
        pt_, vt, st, gt = nc.tensor, nc.vector, nc.scalar, nc.gpsimd

        ncst = sum(v[1] for v in coff.values())
        sb = lambda name, shape, dt=F32: ctx.enter_context(nc.sbuf_tensor(name, shape, dt))
        cst = sb("cst", [128, ncst])
        C = {k: cst[:, o:o + n] for k, (o, n) in coff.items()}
        identb = sb("identb", [128, 128], BF16)
        causb = sb("causb", [128, 128], BF16)
        cmaskb = sb("cmaskb", [128, 128], BF16)
        X = sb("X", [128, 4, 1024])
        HT = sb("HT", [128, 8, 512])
        NW = 4
        NBLK = 23
        Wt = sb("Wt", [128, NW, 4096])
        PR = sb("PR", [96, 128])
        PT = sb("PT", [128, 96])
        BR = sb("BR", [128, 28])
        SM = sb("SM", [128, 1024])
        ARN = 25130
        AR = sb("AR", [128, ARN])
        banks = [ctx.enter_context(nc.psum_tensor(f"pb{i}", [128, 512], F32)) for i in range(8)]
        SR = Ring([b[:, :] for b in banks[0:3]])
        TR = Ring([b[:, :] for b in banks[3:6]])
        OR = Ring([b[:, :] for b in banks[6:8]])
        WR = Ring([Wt[:, i, :] for i in range(NW)])

        class Place:

            def __init__(self, t, n, at=0):
                self.t, self.n, self.at = t, n, at

            def take(self, *shape):
                k = int(np.prod(shape))
                assert self.at + k <= self.n, (self.at, k, self.n)
                v = self.t[:, self.at:self.at + k]
                self.at += k
                if len(shape) == 2:
                    v = v.rearrange("p (a b) -> p a b", b=shape[1])
                if len(shape) == 3:
                    v = v.rearrange("p (a b c) -> p a b c", b=shape[1], c=shape[2])
                return v

        small = Place(SM, 1024)

        def barrier():
            toks = [e.last for e in (pe, ve, ac, po)] + mq.outstanding()
            for e in (pe, ve, ac, po):
                e.need(*toks)

        def mm(o, lhsT, rhs, start, stop, skip=False):
            return pt_.matmul(o, lhsT, rhs, start=start, stop=stop, skip_group_check=skip)

        def wload(src, k, cols, *more):
            s = WR.get()
            v = s.ap[:, 0:k * cols].rearrange("p (k n) -> p k n", n=cols)
            tok = wq.copy(v, src, *s.free)
            s.free = []
            return s, v, tok

        def wcols(w, c0, n, rows=1024):
            return w[0:rows, c0:c0 + n].rearrange("(k p) n -> p k n", p=128)

        t_x = wq.copy(X[:, :, :], a["x"][0].rearrange("(t p) d -> p t d", p=128))
        t_c = wq.copy(cst[:, :], a["consts"])
        t_m1 = ve.mark(vt.memset(PR[:, :], 1.0))
        rows = [("norm_mix_g", 0, 8), ("norm_ffn_g", 8, 8), ("g_pre_2", 16, 8), ("mu_shift_2", 24, 13),
                ("w0_2", 37, 4), ("a0_2", 41, 4), ("k_k_2", 45, 4), ("k_a_2", 49, 4), ("r_k_2", 53, 4),
                ("g_q_2", 57, 2), ("g_kv_2", 59, 1), ("fox_q_g", 60, 1), ("fox_k_g", 61, 1),
                ("nsa_q_g", 62, 1), ("nsa_k_g", 63, 1), ("cmp_k_pos", 64, 16), ("cmp_v_pos", 80, 16)]
        t_pr = []
        for name, r, n in rows:
            src = a[name]
            while len(src.shape) > 1:
                src = src.rearrange("a b -> (a b)") if len(src.shape) == 2 else src.rearrange("a b c -> (a b c)")
            w = src.shape[0] // n
            t_pr.append(mq.copy(PR[r:r + n, 0:w], src.rearrange("(r w) -> r w", w=w), t_m1))
        for name, o, n in (("b_forget", 0, 8), ("b_group", 8, 4), ("b_router", 12, 16)):
            t_pr.append(mq.copy(BR[:, o:o + n], a[name].to_broadcast([128, n])))
        t_br = t_pr[-3:]

        ve.need(t_c)
        ve.mark(vt.tensor_copy(identb[:, :], C["ident"]))
        ve.mark(vt.tensor_copy(causb[:, :], C["causal"]))
        t_cb = ve.mark(vt.tensor_copy(cmaskb[:, :], C["cmask"]))
        s = TR.get()
        pe.need(t_c, *t_pr)
        t = pe.mark(pt_.transpose(s.ap[:, 0:96], PR[:, :], C["ident"][0:96, 0:96]))
        ve.need(t)
        t_pt = ve.mark(vt.tensor_copy(PT[:, :], s.ap[:, 0:96]))
        s.free = [t_pt]
        ident = C["ident"]
        for e in (pe, ve, ac, po):
            e.need(t_c, t_cb, t_pt, *t_br)

        def rstd(dst, ss, n, scr, tok, s=1.0, eps=EPS):
            m, y = scr
            ve.need(tok)
            t = ve.mark(vt.tensor_scalar(m, ss, 1.0 / n, eps, ALU.mult, ALU.add))
            ac.need(t)
            t2 = ac.mark(st.activation(y, m, ACT.Ln))
            ac.need(t2)
            t3 = ac.mark(st.activation(y, y, ACT.Exp, scale=-0.5))
            ve.need(t3)
            t = ve.mark(vt.tensor_tensor(dst, y, y, ALU.mult))
            ve.need(t)
            t = ve.mark(vt.tensor_tensor(dst, dst, m, ALU.mult))
            ve.need(t)
            t = ve.mark(vt.tensor_scalar(dst, dst, -0.5 * s, 1.5 * s, ALU.mult, ALU.add))
            ve.need(t)
            return ve.mark(vt.tensor_tensor(dst, dst, y, ALU.mult))

        def bc(ap, n):
            return ap.unsqueeze(len(ap.shape)).to_broadcast([*ap.shape, n])

        def mid(ap, n):
            return ap.unsqueeze(1).to_broadcast([ap.shape[0], n, *ap.shape[1:]])

        def norm_turn(dst, gcol, scr, tokens, store=None):
            buf = scr.take(2, 1024)
            ss, rs, m, y = (small.take(4) for _ in range(4))
            ring = Ring([buf[:, i, :] for i in range(2)])
            toks = []
            for t in range(4):
                b = ring.get()
                ac.need(*tokens, *b.free)
                toks.append(ac.mark(st.activation(b.ap, X[:, t, :], ACT.Square, accum_out=ss[:, t:t + 1])))
                b.free = [toks[-1]]
            tr = rstd(rs, ss, 1024, (m, y), toks[-1])
            done = []

            def scale(t):
                b = ring.get()
                ve.need(tr, *b.free)
                tk = ve.mark(vt.tensor_scalar(b.ap, X[:, t, :], rs[:, t:t + 1], None, ALU.mult))
                state[t] = (b, tk)
                stored[t] = mq.copy(store[t * 128:(t + 1) * 128, :], b.ap, tk) if store is not None else None

            def turn(t):
                b, tk = state[t]
                pe.need(tk)
                for g in range(2):
                    s = TR.get()
                    pe.need(*s.free)
                    for j in range(4):
                        k = 4 * g + j
                        r = pt_.transpose(s.ap[:, j * 128:(j + 1) * 128], b.ap[:, k * 128:(k + 1) * 128], ident)
                    tp = pe.mark(r)
                    ve.need(tp)
                    r = ve.mark(vt.tensor_tensor(dst[:, 4 * g:4 * g + 4, t * 128:(t + 1) * 128],
                                                 s.ap.rearrange("p (k q) -> p k q", q=128),
                                                 bc(PT[:, gcol + 4 * g:gcol + 4 * g + 4], 128), ALU.mult))
                    s.free = [r]
                b.free = [tp, stored[t]]
                done.append(r)

            state, stored = {}, {}
            pipe(range(4), scale, turn)
            return done[-1]

        def proj(lT, t, nk, w, c0, n, ring, *tokens):
            s = ring.get()
            pe.need(*s.free, *tokens)
            for k in range(nk):
                r = mm(s.ap[:, 0:n], lT[:, k, t * 128:(t + 1) * 128], w[:, k, c0:c0 + n], k == 0, k == nk - 1)
            return s, pe.mark(r)

        ALLT = range(4)

        class HeadTurn:
            def __init__(self, scr, nh):
                self.sq = Ring([scr.take(nh * 64) for _ in range(2)])
                self.au = Ring([scr.take(nh, 66) for _ in range(2)])
                self.nh = nh
                self.sm = [small.take(nh) for _ in range(4)]

            def norm(self, ps, p0, tp, s, aug, atok):
                nh = self.nh
                q, u = self.sq.get(), self.au.get()
                ss, rs, m, y = self.sm
                ac.need(tp, *q.free)
                t1 = ac.mark(st.activation(q.ap, ps.ap[:, p0:p0 + nh * 64], ACT.Square))
                ve.need(t1)
                t2 = ve.mark(vt.reduce_sum(ss, q.ap.rearrange("p (h d) -> p h d", d=64), AX.X))
                q.free = [t2]
                tr = rstd(rs, ss, 64, (m, y), t2, s)
                ve.need(tr, *u.free)
                t3 = ve.mark(vt.tensor_tensor(u.ap[:, :, 0:64],
                                              ps.ap[:, p0:p0 + nh * 64].rearrange("p (h d) -> p h d", d=64),
                                              bc(rs, 64), ALU.mult))
                ps.free = [t3]
                ve.need(atok)
                for c, src in aug:
                    t3 = ve.mark(vt.tensor_copy(u.ap[:, :, 64 + c[0]:64 + c[1]], src))
                return u, t3

            def turn(self, u, tk, dst, t, gcol):
                pe.need(tk)
                for g in range(0, self.nh, 4):
                    n = min(4, self.nh - g)
                    s = TR.get()
                    pe.need(*s.free)
                    for j in range(n):
                        r = pt_.transpose(s.ap[0:66, j * 128:(j + 1) * 128], u.ap[:, g + j, :], ident)
                    tp = pe.mark(r)
                    ac.need(tp)
                    te = ac.mark(st.activation(dst[0:66, g:g + n, t * 128:(t + 1) * 128],
                                               s.ap[0:66, 0:n * 128].rearrange("p (h q) -> p h q", q=128),
                                               ACT.Copy, scale=PT[0:66, gcol:gcol + 1]))
                    s.free = [te]
                u.free = [tp]
                return te

        class Attend:
            def __init__(self, scr):
                self.P = Ring([scr.take(512) for _ in range(3)])
                self.PT = Ring([scr.take(512) for _ in range(3)])
                self.nm = Ring([small.take(8) for _ in range(2)])
                self.rs = Ring([small.take(8) for _ in range(2)])

            def run(self, qT, kT, V, kd, fin, toks):
                items = [dict(i=i, h=h) for i in ALLT for h in range(8)]

                def score(x):
                    i, h = x["i"], x["h"]
                    L = (i + 1) * 128
                    s = SR.get()
                    pe.need(*s.free, *toks)
                    mm(s.ap[:, 0:L], qT(h)[0:kd, i * 128:(i + 1) * 128], kT(h)[0:kd, 0:L], True, True)
                    tp = pe.mark(mm(s.ap[:, L - 128:L], identb[:, :], causb[:, :], False, True, True))
                    if h == 0:
                        self.m, self.r = self.nm.get(), self.rs.get()
                    nm, rs = self.m, self.r
                    ve.need(tp, *nm.free)
                    tm = ve.mark(vt.tensor_reduce(nm.ap[:, h:h + 1], s.ap[:, 0:L], AX.X, ALU.max, negate=True))
                    p = self.P.get()
                    ac.need(tm, *p.free, *rs.free)
                    x["e"] = ac.mark(st.activation(p.ap[:, 0:L], s.ap[:, 0:L], ACT.Exp, bias=nm.ap[:, h:h + 1],
                                                   accum_out=rs.ap[:, h:h + 1]))
                    s.free = [x["e"]]
                    x["p"], x["rs"], x["nm"] = p, rs, nm
                    if h == 7:
                        nm.free = [x["e"]]

                def turn(x):
                    i = x["i"]
                    L = (i + 1) * 128
                    s, p, q = TR.get(), x["p"], self.PT.get()
                    pe.need(x["e"], *s.free)
                    for j in range(i + 1):
                        r = pt_.transpose(s.ap[:, j * 128:(j + 1) * 128], p.ap[:, j * 128:(j + 1) * 128], ident)
                    tp = pe.mark(r)
                    p.free = [tp]
                    ve.need(tp, *q.free)
                    x["c"] = ve.mark(vt.tensor_copy(q.ap[:, 0:L], s.ap[:, 0:L]))
                    s.free = [x["c"]]
                    x["q"] = q

                def value(x):
                    i, h = x["i"], x["h"]
                    if h == 0:
                        self.o = OR.get()
                        pe.need(*self.o.free)
                    pe.need(x["c"])
                    for j in range(i + 1):
                        r = mm(self.o.ap[:, h * 64:(h + 1) * 64], x["q"].ap[:, j * 128:(j + 1) * 128],
                               V(h, j), j == 0, j == i)
                    tp = pe.mark(r)
                    x["q"].free = [tp]
                    if h == 7:
                        self.o.free = [fin(i, self.o, tp, x["rs"], x["e"])]

                pipe(items, score, turn, value)

        def divide(dst, o, tp, rs, te, scr, gate=None):
            ri = scr
            ve.need(tp, te)
            t = ve.mark(vt.reciprocal(ri, rs.ap))
            rs.free = [t]
            if gate is not None:
                ve.need(t)
                t = ve.mark(vt.tensor_tensor(ri, ri, gate, ALU.mult))
            ve.need(t)
            return ve.mark(vt.tensor_tensor(dst.rearrange("p (h d) -> p h d", d=64),
                                            o.ap.rearrange("p (h d) -> p h d", d=64), bc(ri, 64), ALU.mult))

        def turn4(src, dst, t, n, tok, gcol=None):
            s = TR.get()
            pe.need(tok, *s.free)
            for j in range(n):
                r = pt_.transpose(s.ap[:, j * 128:(j + 1) * 128], src[:, j * 128:(j + 1) * 128], ident)
            tp = pe.mark(r)
            if gcol is None:
                ac.need(tp)
                te = ac.mark(st.activation(dst[:, 0:n, t * 128:(t + 1) * 128],
                                           s.ap[:, 0:n * 128].rearrange("p (k q) -> p k q", q=128), ACT.Copy))
            else:
                ve.need(tp)
                for j in range(n):
                    te = ve.mark(vt.tensor_scalar(dst[:, j, t * 128:(t + 1) * 128], s.ap[:, j * 128:(j + 1) * 128],
                                                  PT[:, gcol + j:gcol + j + 1], None, ALU.mult))
            s.free = [te]
            return te, tp

        t_z = po.mark(gt.memset(AR[:, 20000:21024], 0.0))
        mq.copy(ys_dram[2048:NBLK * 128, :].rearrange("(b p) d -> p b d", p=128),
                AR[:, 20000:21024].unsqueeze(1).to_broadcast([128, NBLK - 16, 1024]), t_z)

        smark = small.at
        w = a["w_in"][0]
        ar = Place(AR, ARN)
        foxO = ar.take(4, 512)
        nsaO = ar.take(4, 512)
        base = ar.at
        t_h = norm_turn(HT[:, :, :], 0, Place(AR, ARN, base), [t_x])
        barrier()
        qT = ar.take(8, 512)
        kT = ar.take(8, 512)
        fv = ar.take(4, 512)
        gates = small.take(4, 24)
        cum = small.take(4, 8)
        lf = small.take(4, 8)
        tmp8 = small.take(4, 8)
        off8 = small.take(8)
        scr = Place(AR, ARN, ar.at)
        ht8 = HeadTurn(scr, 8)

        s0 = WR.get()
        v0 = s0.ap[:, 0:8 * 32].rearrange("p (k n) -> p k n", n=32)
        tw1 = wq.copy(v0[:, :, 0:8], wcols(w, 1536, 8), *s0.free)
        tw2 = wq.copy(v0[:, :, 8:32], wcols(w, 2824, 24))
        for t in ALLT:
            s, tp = proj(HT, t, 8, v0, 0, 32, SR, t_h, tw1, tw2)
            ve.need(tp)
            t1 = ve.mark(vt.tensor_tensor(lf[:, t, :], s.ap[:, 0:8], BR[:, 0:8], ALU.add))
            t2 = ve.mark(vt.tensor_copy(gates[:, t, :], s.ap[:, 8:32]))
            s.free = [t2]
        s0.free = [tp]
        ac.need(t1)
        t3 = ac.mark(st.activation(tmp8, lf, ACT.Abs))
        ac.need(t3)
        t3 = ac.mark(st.activation(tmp8, tmp8, ACT.Exp, scale=-1.0))
        ac.need(t3)
        t3 = ac.mark(st.activation(tmp8, tmp8, ACT.Ln, bias=1.0))
        ve.need(t3)
        t4 = ve.mark(vt.scalar_tensor_tensor(out=lf, in0=lf, scalar=0.0, in1=tmp8, op0=ALU.min, op1=ALU.subtract))
        ac.need(t2)
        t5 = ac.mark(st.activation(gates, gates, ACT.Exp, scale=-1.0))
        ve.need(t5)
        t5 = ve.mark(vt.tensor_scalar(gates, gates, 1.0, None, ALU.add))
        ve.need(t5)
        t_g = ve.mark(vt.reciprocal(gates, gates))
        s = OR.get()
        pe.need(t4, *s.free)
        for t in ALLT:
            for j in range(t + 1):
                r = mm(s.ap[:, t * 8:t * 8 + 8], C["tri"] if j == t else C["ones"], lf[:, j, :], j == 0, j == t)
        tp = pe.mark(r)
        ve.need(tp)
        t_cum = ve.mark(vt.tensor_copy(cum, s.ap[:, 0:32].rearrange("p (t h) -> p t h", h=8)))
        s.free = [t_cum]
        ones48 = C["ones"][:, 0:8].unsqueeze(2)

        def heads(wv, tw, dst, aug, gcol, s_, atok):
            st8 = {}

            def p_(t):
                ps, tp = proj(HT, t, 8, wv, 0, 512, SR, tw)
                st8[t] = ht8.norm(ps, 0, tp, s_, aug(t), atok)
                st8["pe"] = tp

            def t_(t):
                st8["e"] = ht8.turn(*st8[t], dst, t, gcol)

            pipe(ALLT, p_, t_)
            return st8["e"], st8["pe"]

        sw, wv, tw = wload(wcols(w, 0, 512), 8, 512)
        t_q, tp = heads(wv, tw, qT, lambda t: [((0, 1), ones48), ((1, 2), cum[:, t, :].unsqueeze(2))], 60, 0.125, t_cum)
        sw.free = [tp]
        ncum = small.take(4, 8)
        ve.need(t_cum)
        t_nc = ve.mark(vt.tensor_scalar(ncum, cum, -1.0, None, ALU.mult))
        sw, wv, tw = wload(wcols(w, 512, 512), 8, 512)
        t_k, tp = heads(wv, tw, kT, lambda t: [((0, 1), ncum[:, t, :].unsqueeze(2)), ((1, 2), ones48)], 61, 1.0, t_nc)
        sw.free = [tp]
        sw, wv, tw = wload(wcols(w, 1024, 512), 8, 512)
        for t in ALLT:
            ps, tp = proj(HT, t, 8, wv, 0, 512, SR, tw)
            ac.need(tp)
            t_v = ac.mark(st.copy(fv[:, t, :], ps.ap))
            ps.free = [t_v]
        sw.free = [tp]
        att = Attend(scr)
        ri8 = small.take(8)

        def fin(i, o, tp, rs, te):
            return divide(foxO[:, i, :], o, tp, rs, te, ri8)

        att.run(lambda h: qT[:, h, :], lambda h: kT[:, h, :], lambda h, j: fv[:, j, h * 64:(h + 1) * 64],
                66, fin, [t_q, t_k, t_v])
        barrier()

        ar.at = scr.at
        nq = qT
        kT2 = kT[:, 0:4, :]
        kcT = kT[:, 4, 0:64]
        kvT = kT[:, 5:7, :]
        vbd = kT[:, 7, :].rearrange("p (g n) -> p g n", n=256)
        vT2 = fv[:, :, 0:256]
        X2 = scr.take(4, 512)
        hidT = scr.take(4, 64)
        posb = small.take(4)
        kcn = small.take(66)
        kcs = [small.take(1) for _ in range(4)]
        sw, wv, tw = wload(wcols(w, 1544, 512), 8, 512)
        t_q, tp = heads(wv, tw, nq, lambda t: [((0, 2), C["qaug"].rearrange("p (t h c) -> p t h c", h=8, c=2)[:, t])],
                        62, 0.125, t_c)
        sw.free = [tp]
        sw, wv, tw = wload(wcols(w, 2056, 256), 8, 256)
        pe.need(tw)
        for c in range(2):
            s = SR.get()
            pe.need(*s.free)
            for k in range(8):
                r = mm(s.ap, wv[:, k, c * 128:(c + 1) * 128], HT[:, k, :], k == 0, k == 7)
            tp = pe.mark(r)
            ac.need(tp)
            tk = ac.mark(st.copy(kvT[:, c, :], s.ap))
            s.free = [tk]
        sw.free = [tp]
        t_z = po.mark(gt.memset(X2[:, :, 511:512], 0.0))
        tx2 = []
        for c in range(2):
            for g in range(2):
                tx2.append(mq.copy(X2[0:64, 2 * c + g, :], kvT[64 * g:64 * g + 64, c, :], tk, t_z))
                tx2.append(mq.copy(X2[64:128, 2 * c + g, 0:511], kvT[64 * g:64 * g + 64, c, 1:512]))
        t_vz = po.mark(gt.memset(vbd, 0.0))
        t_hz = po.mark(gt.memset(hidT, 0.0))
        sv, wv, tw = wload(wcols(w, 2312, 512), 8, 512)
        ht2 = HeadTurn(scr, 2)
        ht2.au = Ring([scr.take(2, 66) for _ in range(4)])
        kvs = Ring([scr.take(256) for _ in range(2)])
        kaug = C["kaug"].rearrange("p (t c) -> p t c", c=2)
        st2 = {}

        def p_(t):
            ps, tp = proj(HT, t, 8, wv, 0, 512, SR, tw)
            kk2 = kvs.get()
            ac.need(tp, *kk2.free)
            for j in range(2):
                ac.mark(st.copy(vT2[:, t, j * 128:(j + 1) * 128], ps.ap[:, 256 * j + 128:256 * j + 256]))
            te = ac.mark(st.copy(kk2.ap.rearrange("p (j n) -> p j n", n=128),
                                 ps.ap.rearrange("p (j n) -> p j n", n=256)[:, :, 0:128]))
            ps.free = [te]
            aug = [((0, 2), mid(kaug[:, t, :], 2))]
            u0 = ht2.norm(kk2, 0, te, 1.0, aug, t_c)
            u1 = ht2.norm(kk2, 128, te, 1.0, aug, t_c)
            st2[t] = (u0, u1)
            st2["pe"], st2["v"] = tp, te

        def t_(t):
            for j in range(2):
                st2["e"] = ht2.turn(*st2[t][j], kT2[:, 2 * j:2 * j + 2, :], t, 63)

        pipe(ALLT, p_, t_)
        sv.free = [st2["pe"]]
        for c, nm_ in enumerate(("k", "v")):
            s1, w1, tw1 = wload(a[f"cmp_{nm_}_w1"][0].rearrange("(j p) n -> p j n", p=128), 16, 256)
            s2, w2, tw2 = wload(a[f"cmp_{nm_}_w2"][0].rearrange("(j p) n -> p j n", p=128), 2, 64)
            xw = X2.rearrange("p c (n s) -> p c n s", s=16)
            for hf in range(2):
                s = OR.get()
                pe.need(*s.free, tw1, tw2, *tx2)
                for j in range(16):
                    mm(s.ap[:, 62:63], w1[:, j, hf * 128:(hf + 1) * 128], PT[:, 64 + 16 * c + j:65 + 16 * c + j],
                       j == 0, j == 15)
                for j in range(16):
                    n0, sft = (0, 2 * j) if j < 8 else (1, 2 * j - 16)
                    r = mm(s.ap[:, 0:62], w1[:, j, hf * 128:(hf + 1) * 128],
                           xw[:, 2 * c:2 * c + 2, n0:n0 + 31, sft], j == 0, j == 15)
                tp = pe.mark(r)
                ve.need(tp)
                tv = ve.mark(vt.tensor_copy(posb[:, 2 * c + hf:2 * c + hf + 1], s.ap[:, 62:63]))
                ac.need(tv, t_hz)
                th = ac.mark(st.activation(
                    hidT[:, 2 * c + hf, :].rearrange("p (g n) -> p g n", n=32)[:, :, 0:31],
                    s.ap[:, 0:62].rearrange("p (g n) -> p g n", n=31), ACT.Gelu_apprx_tanh,
                    bias=posb[:, 2 * c + hf:2 * c + hf + 1]))
                s.free = [th]
            s1.free = [tp]
            s = OR.get()
            pe.need(*s.free, th)
            if c == 0:
                for hf in range(2):
                    r = mm(s.ap[0:64, 0:64], hidT[:, hf, :], w2[:, hf, :], hf == 0, hf == 1)
                tp = pe.mark(r)
                ac.need(tp)
                t1 = ac.mark(st.activation(kcn[0:64, 0:64], s.ap[0:64, 0:64], ACT.Square,
                                           accum_out=kcs[0][0:64, :]))
                t1 = rstd(kcs[1][0:64, :], kcs[0][0:64, :], 64, (kcs[2][0:64, :], kcs[3][0:64, :]), t1)
                ve.need(t1)
                t1 = ve.mark(vt.tensor_scalar(kcn[0:64, 0:64], s.ap[0:64, 0:64], kcs[1][0:64, :], None, ALU.mult))
                t2 = ve.mark(vt.tensor_copy(kcn[0:64, 64:66], C["caug"][0:64, :]))
                s.free = [t1]
                s = TR.get()
                pe.need(t2, *s.free)
                tp = pe.mark(pt_.transpose(s.ap[0:66, 0:64], kcn[0:64, :], ident[0:64, 0:64]))
                ac.need(tp)
                t_kc = ac.mark(st.activation(kcT[0:66, :], s.ap[0:66, 0:64], ACT.Copy, scale=PT[0:66, 63:64]))
                s.free = [t_kc]
            else:
                pe.need(t_vz)
                for g in range(2):
                    for r4 in range(4):
                        for hf in range(2):
                            r = mm(s.ap[32 * r4:32 * r4 + 32, g * 64:g * 64 + 64],
                                   hidT[:, 2 + hf, g * 32:g * 32 + 32], w2[:, hf, :], hf == 0, hf == 1)
                tp = pe.mark(r)
                ve.need(tp, t_vz)
                for g in range(2):
                    for r4 in range(4):
                        t_vc = ve.mark(vt.tensor_copy(vbd[32 * r4:32 * r4 + 32, g, 64 * r4:64 * r4 + 64],
                                                      s.ap[32 * r4:32 * r4 + 32, g * 64:g * 64 + 64]))
                s.free = [t_vc]
            s2.free = [tp]

        ri8b = small.take(8)
        nm8, rs8 = small.take(8), small.take(8)
        anyg = small.take(8)
        pc, pcT = att.P, att.PT
        cm = cmaskb[:, :].rearrange("p (t n) -> p t n", n=32)
        e_prev = None
        for i in ALLT:
            s = SR.get()
            pe.need(*s.free, t_q, t_kc)
            mm(s.ap[:, 0:256], identb[:, :], mid(cm[:, i, :], 8), True, True)
            for h in range(8):
                r = mm(s.ap[:, h * 32:h * 32 + 32], nq[0:66, h, i * 128:(i + 1) * 128],
                       kcT[0:66, (h // 4) * 32:(h // 4) * 32 + 32], False, True, True)
            tp = pe.mark(r)
            sv8 = s.ap[:, 0:256].rearrange("p (h n) -> p h n", n=32)
            ve.need(tp, e_prev)
            t1 = ve.mark(vt.tensor_reduce(nm8, sv8, AX.X, ALU.max, negate=True))
            p = pc.get()
            pv = p.ap[:, 0:256].rearrange("p (h n) -> p h n", n=32)
            ve.need(t1, *p.free)
            t1 = ve.mark(vt.tensor_tensor(pv, sv8, bc(nm8, 32), ALU.add))
            s.free = [t1]
            ac.need(t1)
            t2 = ac.mark(st.activation(p.ap[:, 0:256], p.ap[:, 0:256], ACT.Exp))
            ve.need(t2)
            t3 = ve.mark(vt.reduce_sum(rs8, pv, AX.X))
            ve.need(t3)
            t3 = ve.mark(vt.reciprocal(ri8b, rs8))
            ve.need(t3)
            t3 = ve.mark(vt.tensor_tensor(ri8b, ri8b, gates[:, i, :].rearrange("p (h c) -> p h c", c=3)[:, :, 0], ALU.mult))
            ve.need(t3)
            t3 = ve.mark(vt.tensor_scalar(ri8b, ri8b, C["anyv"][:, i:i + 1], None, ALU.mult))
            s = TR.get()
            pe.need(t2, *s.free)
            for g in range(2):
                r = pt_.transpose(s.ap[:, g * 128:(g + 1) * 128], p.ap[:, g * 128:(g + 1) * 128], ident)
            tp = pe.mark(r)
            p.free = [tp, t3]
            q = pcT.get()
            ve.need(tp, *q.free)
            tc = ve.mark(vt.tensor_copy(q.ap[:, 0:256], s.ap[:, 0:256]))
            s.free = [tc]
            s = OR.get()
            pe.need(tc, t_vc, *s.free)
            for g in range(2):
                r = mm(s.ap[:, g * 256:(g + 1) * 256], q.ap[:, g * 128:(g + 1) * 128], vbd[:, g, :], True, True)
            tp = pe.mark(r)
            q.free = [tp]
            ve.need(tp, t3)
            e_prev = ve.mark(vt.tensor_tensor(nsaO[:, i, :].rearrange("p (h d) -> p h d", d=64),
                                              s.ap.rearrange("p (h d) -> p h d", d=64), bc(ri8b, 64), ALU.mult))
            s.free = [e_prev]

        tmpo = scr.take(512)
        for j in range(2):
            def fin2(i, o, tp, rs, te, j=j):
                g8 = gates[:, i, :].rearrange("p (h c) -> p h c", c=3)[:, :, 1 + j]
                if fin2.prev is not None:
                    ve.need(fin2.prev)
                t = divide(tmpo, o, tp, rs, te, ri8, g8)
                ve.need(t)
                fin2.prev = ve.mark(vt.tensor_tensor(nsaO[:, i, :], nsaO[:, i, :], tmpo, ALU.add))
                return t

            fin2.prev = None
            att.run(lambda h: nq[:, h, :], lambda h, j=j: kT2[:, 2 * j + h // 4, :],
                    lambda h, jt, j=j: vT2[:, jt, j * 128 + (h // 4) * 64:j * 128 + (h // 4) * 64 + 64],
                    66, fin2, [t_q, st2["e"], st2["v"]])
        barrier()

        def merge(lT, w_in, c_a, outs, oTs, mix, mixT, scr, bias=None):
            sg = Ring([scr.take(512) for _ in range(3)])
            tb = Ring([scr.take(512) for _ in range(2)])
            items = []
            for c in range(2):
                for b in range(2):
                    for t in ALLT:
                        items.append((c, b, t))
            cur = {}

            def go(x):
                c, b, t = x
                if t == 0:
                    cur["g"] = wload(wcols(w_in, c_a + 1024 * b + 512 * c, 512), 8, 512)
                    cur["u"] = wload(outs[b][:, 512 * c:512 * c + 512].rearrange("(k p) n -> p k n", p=128), 4, 512)
                sg_, gv, tg = cur["g"]
                su_, uv, tu = cur["u"]
                ps, tp = proj(lT, t, 8, gv, 0, 512, SR, tg)
                z = sg.get()
                if bias is not None:
                    ve.need(tp, *z.free)
                    tz = ve.mark(vt.tensor_tensor(z.ap, ps.ap, bias[:, 1024 * b + 512 * c:1024 * b + 512 * c + 512],
                                                  ALU.add))
                    ps.free = [tz]
                    ac.need(tz)
                    tz = ac.mark(st.activation(z.ap, z.ap, ACT.Sigmoid))
                else:
                    ac.need(tp, *z.free)
                    tz = ac.mark(st.activation(z.ap, ps.ap, ACT.Sigmoid))
                    ps.free = [tz]
                pu, tp2 = proj(oTs[b], t, 4, uv, 0, 512, OR, tu)
                ve.need(tp2, tz)
                m = mix[:, t, c * 512:(c + 1) * 512]
                if b == 0:
                    tm = ve.mark(vt.tensor_tensor(m, pu.ap, z.ap, ALU.mult))
                    pu.free = [tm]
                    z.free = [tm]
                    cur[(c, t)] = tm
                else:
                    y = tb.get()
                    ve.need(*y.free)
                    tm = ve.mark(vt.tensor_tensor(y.ap, pu.ap, z.ap, ALU.mult))
                    pu.free = [tm]
                    z.free = [tm]
                    ve.need(tm, cur[(c, t)])
                    tm = ve.mark(vt.tensor_tensor(m, m, y.ap, ALU.add))
                    y.free = [tm]
                    cur[(c, t)] = tm
                if t == 3:
                    sg_.free = [tp]
                    su_.free = [tp2]

            def tn(x):
                c, b, t = x
                if b == 1:
                    cur["t"], _ = turn4(mix[:, t, c * 512:(c + 1) * 512], mixT[:, 4 * c:4 * c + 4, :], t, 4, cur[(c, t)])

            pipe(items, go, tn)
            return cur["t"]

        ar = Place(AR, ARN, base)
        mix = ar.take(4, 1024)
        mixT = ar.take(8, 512)
        foT = ar.take(4, 512)
        noT = ar.take(4, 512)
        scr = Place(AR, ARN, ar.at)
        for t in ALLT:
            turn4(foxO[:, t, :], foT, t, 4, None)
            te, _ = turn4(nsaO[:, t, :], noT, t, 4, None)
        pe.need(te)
        tm = merge(HT, w, 2848, [a["w_fox_up"][0], a["w_nsa_up"][0]], [foT, noT], mix, mixT, scr)
        for c in range(2):
            sw, wv, tw = wload(wcols(a["w_out"][0], 512 * c, 512), 8, 512)
            for t in ALLT:
                ps, tp = proj(mixT, t, 8, wv, 0, 512, SR, tw, tm)
                ve.need(tp)
                xs = X[:, t, c * 512:(c + 1) * 512]
                tx = ve.mark(vt.tensor_tensor(xs, ps.ap, xs, ALU.add))
                ps.free = [tx]
            sw.free = [tp]
        barrier()

        small.at = smark
        ar = Place(AR, ARN)
        t_clear = [e.last for e in (pe, ve, ac, po)]
        t_h = norm_turn(HT[:, :, :], 8, Place(AR, ARN, 23000), [], xs_dram)
        zt = AR[:, 22900:22923].bitcast(U32)
        t_z = po.mark(gt.memset(zt, 0))
        tab_v = tab_dram.rearrange("(p b) a -> p (b a)", b=NBLK)
        t_tab = mq.copy(tab_v, zt, t_z)
        s0 = WR.get()
        v0 = s0.ap[:, 0:160].rearrange("p (k n) -> p k n", n=20)
        tw1 = wq.copy(v0[:, :, 0:4], a["w_group"][0].rearrange("(k p) n -> p k n", p=128), *s0.free)
        tw2 = wq.copy(v0[:, :, 4:20], a["w_router"][0].rearrange("(k p) n -> p k n", p=128))
        lg = small.take(4, 20)
        for t in ALLT:
            s, tp = proj(HT, t, 8, v0, 0, 20, SR, t_h, tw1, tw2)
            ve.need(tp)
            tl = ve.mark(vt.tensor_tensor(lg[:, t, :], s.ap[:, 0:20], BR[:, 8:28], ALU.add))
            s.free = [tl]
        s0.free = [tp]

        def vop(f, *tokens):
            ve.need(ve.last, *tokens)
            return ve.mark(f())

        m1 = small.take(4)
        g1 = small.take(4, 4)
        oh = small.take(4, 4)
        pg = small.take(4)
        e4 = mid(C["e4"], 4)

        def first_max(dst, src, mx, scr4, sc1):
            vop(lambda: vt.reduce_max(mx, src, AX.X))
            vop(lambda: vt.tensor_tensor(scr4, src, bc(mx, 4), ALU.is_ge))
            vop(lambda: vt.tensor_scalar(scr4, scr4, -100.0, 100.0, ALU.mult, ALU.add))
            vop(lambda: vt.tensor_tensor(scr4, scr4, e4, ALU.add))
            vop(lambda: vt.tensor_reduce(sc1, scr4, AX.X, ALU.min))
            return vop(lambda: vt.tensor_tensor(dst, e4, bc(sc1, 4), ALU.is_equal))

        f4, f1 = small.take(4, 4), small.take(4)
        gl = lg[:, :, 0:4]
        first_max(oh, gl, m1, f4, f1)
        t1 = vop(lambda: vt.tensor_tensor(g1, gl, bc(m1, 4), ALU.subtract))
        ac.need(t1)
        t1 = ac.mark(st.activation(g1, g1, ACT.Exp))
        vop(lambda: vt.reduce_sum(pg, g1, AX.X), t1)
        vop(lambda: vt.reciprocal(pg, pg))
        em = small.take(4, 4, 4)
        ein = small.take(4, 4)
        elg = lg[:, :, 4:20]
        for g in range(4):
            vop(lambda: vt.tensor_tensor(em[:, :, g, :], elg[:, :, 4 * g:4 * g + 4], bc(oh[:, :, g], 4), ALU.mult))
        vop(lambda: vt.reduce_sum(ein, em.rearrange("p t g j -> p t j g"), AX.X))
        vop(lambda: vt.reduce_max(m1, ein, AX.X))
        t1 = vop(lambda: vt.tensor_tensor(ein, ein, bc(m1, 4), ALU.subtract))
        ac.need(t1)
        t1 = ac.mark(st.activation(ein, ein, ACT.Exp))
        ve.need(t1)
        o1, o2, e2 = small.take(4, 4), small.take(4, 4), small.take(4, 4)
        p1, p2, ps_ = small.take(4), small.take(4), small.take(4)
        first_max(o1, ein, p1, f4, f1)
        vop(lambda: vt.tensor_scalar(e2, o1, -2.0, None, ALU.mult))
        vop(lambda: vt.tensor_tensor(e2, ein, e2, ALU.add))
        first_max(o2, e2, p2, f4, f1)
        vop(lambda: vt.tensor_tensor(ps_, p1, p2, ALU.add))
        vop(lambda: vt.reciprocal(ps_, ps_))
        vop(lambda: vt.tensor_tensor(ps_, ps_, pg, ALU.mult))
        vop(lambda: vt.tensor_tensor(p1, p1, ps_, ALU.mult))
        vop(lambda: vt.tensor_tensor(p2, p2, ps_, ALU.mult))
        M1, M2, MM = (small.take(4, 16) for _ in range(3))
        for g in range(4):
            vop(lambda: vt.tensor_tensor(M1[:, :, 4 * g:4 * g + 4], o1, bc(oh[:, :, g], 4), ALU.mult))
            vop(lambda: vt.tensor_tensor(M2[:, :, 4 * g:4 * g + 4], o2, bc(oh[:, :, g], 4), ALU.mult))
        t1 = vop(lambda: vt.tensor_tensor(MM, M1, M2, ALU.add))
        s = OR.get()
        pe.need(t1, *s.free)
        for t in ALLT:
            for j in range(t + 1):
                mm(s.ap[:, 16 * t:16 * t + 16], C["stri"] if j == t else C["ones"], MM[:, j, :], j == 0, j == t)
        for j in ALLT:
            r = mm(s.ap[:, 64:80], C["ones"], MM[:, j, :], j == 0, j == 3)
        tp = pe.mark(r)
        PO, CN = small.take(4, 16), small.take(16)
        vop(lambda: vt.tensor_copy(PO, s.ap[:, 0:64].rearrange("p (t e) -> p t e", e=16)), tp)
        t1 = vop(lambda: vt.tensor_copy(CN, s.ap[:, 64:80]))
        s.free = [t1]
        nov, ovi, ovb, ones16 = small.take(16), small.take(16), small.take(16), C["ones"][:, 0:16]
        vop(lambda: vt.tensor_scalar(nov, CN, 128.0, None, ALU.is_gt))
        for c in (256.0, 384.0):
            vop(lambda: vt.scalar_tensor_tensor(out=nov, in0=CN, scalar=c, in1=nov, op0=ALU.is_gt, op1=ALU.add))
        vop(lambda: vt.tensor_tensor_scan(ovi, ones16, nov, 0.0, ALU.mult, ALU.add))
        vop(lambda: vt.tensor_tensor(ovb, ovi, nov, ALU.subtract))
        e7 = small.take(7, 16)
        ctl = small.take(8)
        vop(lambda: vt.tensor_tensor(e7, mid(ovi, 7), C["b7"].rearrange("p (b e) -> p b e", e=16), ALU.is_le))
        vop(lambda: vt.reduce_sum(ctl[:, 1:8], e7, AX.X))
        vop(lambda: vt.tensor_scalar(ctl[:, 1:8], ctl[:, 1:8], 15.0, None, ALU.min))
        vop(lambda: vt.tensor_copy(ctl[:, 0:1], ovi[:, 15:16]))
        ctli = small.take(8).bitcast(I32)
        t_ctl = vop(lambda: vt.tensor_copy(ctli, ctl))
        q_, F_, BK = (small.take(4, 16) for _ in range(3))
        vop(lambda: vt.tensor_scalar(F_, PO, 128.0, None, ALU.is_ge))
        vop(lambda: vt.scalar_tensor_tensor(out=q_, in0=PO, scalar=256.0, in1=F_, op0=ALU.is_ge, op1=ALU.add))
        vop(lambda: vt.scalar_tensor_tensor(out=q_, in0=PO, scalar=384.0, in1=q_, op0=ALU.is_ge, op1=ALU.add))
        vop(lambda: vt.tensor_tensor(ovb, ovb, C["e16"], ALU.subtract))
        vop(lambda: vt.tensor_scalar(ovb, ovb, 15.0, None, ALU.add))
        vop(lambda: vt.tensor_tensor(BK, F_, mid(ovb, 4), ALU.mult))
        vop(lambda: vt.tensor_tensor(BK, BK, mid(C["e16"], 4), ALU.add))
        vop(lambda: vt.tensor_tensor(BK, BK, q_, ALU.add))
        vop(lambda: vt.scalar_tensor_tensor(out=PO, in0=q_, scalar=-128.0, in1=PO, op0=ALU.mult, op1=ALU.add))
        RY, RT_ = F_, q_
        vop(lambda: vt.scalar_tensor_tensor(out=RY, in0=BK, scalar=128.0, in1=PO, op0=ALU.mult, op1=ALU.add))
        vop(lambda: vt.scalar_tensor_tensor(out=RT_, in0=PO, scalar=float(NBLK), in1=BK, op0=ALU.mult, op1=ALU.add))
        rows_ = small.take(4, 4)
        for j, (R_, M_) in enumerate(((RT_, M1), (RT_, M2), (RY, M1), (RY, M2))):
            vop(lambda: vt.tensor_tensor(MM, R_, M_, ALU.mult))
            vop(lambda: vt.reduce_sum(rows_[:, j, :], MM, AX.X))
        rowi = small.take(16).bitcast(U32).rearrange("p (j t) -> p j t", t=4)
        toki = small.take(4).bitcast(U32)
        vop(lambda: vt.tensor_copy(toki, kaug[:, :, 0]))
        t1 = vop(lambda: vt.tensor_copy(rowi, rows_))
        t_sc = [mq.scatter(tab_dram, toki[:, t:t + 1], rowi[:, j, t:t + 1], t1, t_tab) for j in range(2) for t in ALLT]
        slots = small.take(NBLK).bitcast(U32)
        t_sl = mq.copy(slots, tab_v, *t_sc)

        barrier()
        EW = Ring([])
        EW.slots = WR.slots + [Slot(ar.take(4096)) for _ in range(3)]
        EW.n = WR.n % NW
        order = [(WR.n + i) % NW for i in range(NW)]
        EW.slots = [WR.slots[i] for i in order] + EW.slots[NW:]
        EW.n = 0
        Gr = Ring([ar.take(1024) for _ in range(3)])
        XTr = Ring([ar.take(8, 128) for _ in range(2)])
        Yr = Ring([ar.take(1024) for _ in range(2)])
        sil = Ring([ar.take(512) for _ in range(2)])
        hb = Ring([ar.take(512) for _ in range(2)])
        hTr = Ring([ar.take(4, 128) for _ in range(2)])
        for r_ in EW.slots[NW:]:
            r_.free = list(t_clear)

        def eload(src, k, n):
            s = EW.get()
            v = s.ap[:, 0:k * n].rearrange("p (k n) -> p k n", n=n)
            tok = wq.copy(v, src.rearrange("(k p) n -> p k n", p=128), *s.free)
            s.free = []
            return s, v, tok

        bst, ty = {}, []

        def expert(name, b, ev):
            return a[name][0, b] if ev is None else a[name][0][bass.ds(ev[b - 16], 1)].rearrange("a k n -> (a k) n")

        def fetch(x):
            b, ev = x
            g = Gr.get()
            bst[b] = [g, (mq if ev is None else xq).gather(g.ap, xs_dram, slots[:, b:b + 1], t_sl, *g.free)]

        def q_mm(o, l, r, start, stop):
            f = lambda: pt_.matmul(o, l, r, start=start, stop=stop)
            return pe.later(f) if stop else pe.run(f)

        def q_turn(o, i, last):
            f = lambda: pt_.transpose(o, i, ident)
            return pe.later(f) if last else pe.run(f)

        def q_mult(o, x, y):
            return ve.later(lambda: vt.tensor_tensor(o, x, y, ALU.mult))

        def q_act(o, x, func):
            return ac.later(lambda: st.activation(o, x, func))

        def turn_x(x):
            b, ev = x
            g, tg = bst[b]
            xt_ = XTr.get()
            for hf in range(2):
                s = TR.get()
                pe.need(tg, *s.free)
                for j in range(4):
                    k = 4 * hf + j
                    tp = q_turn(s.ap[:, j * 128:(j + 1) * 128], g.ap[:, k * 128:(k + 1) * 128], j == 3)
                ve.need(tp, *xt_.free)
                te = q_mult(xt_.ap[:, 4 * hf:4 * hf + 4, :], s.ap.rearrange("p (k q) -> p k q", q=128),
                            bc(PT[:, 8 + 4 * hf:12 + 4 * hf], 128))
                s.free = [te]
            g.free = [tp]
            bst[b] = [xt_, te]

        def gate_up(x):
            b, ev = x
            xt_, te = bst[b]
            pss = []
            for name in ("w_gate", "w_up"):
                sl, wv_, tw_ = eload(expert(name, b, ev), 8, 512)
                s = SR.get()
                pe.need(*s.free, tw_, te)
                for k in range(8):
                    tp = q_mm(s.ap, xt_.ap[:, k, :], wv_[:, k, :], k == 0, k == 7)
                pss.append((s, tp))
                sl.free = [pe.last]
            (s1, tp1), (s2, tp2) = pss
            xt_.free = [tp2]
            z, h = sil.get(), hb.get()
            ac.need(tp1, *z.free)
            tz = q_act(z.ap, s1.ap, ACT.Silu)
            s1.free = [tz]
            ve.need(tz, tp2, *h.free)
            th = q_mult(h.ap, s2.ap, z.ap)
            s2.free = [th]
            z.free = [th]
            bst[b] = [h, th]

        def down(x):
            b, ev = x
            h, th = bst[b]
            s = TR.get()
            ht_, y = hTr.get(), Yr.get()
            pe.need(th, *s.free)
            for j in range(4):
                tp = q_turn(s.ap[:, j * 128:(j + 1) * 128], h.ap[:, j * 128:(j + 1) * 128], j == 3)
            h.free = [tp]
            ac.need(tp, *ht_.free)
            te = q_act(ht_.ap, s.ap.rearrange("p (k q) -> p k q", q=128), ACT.Copy)
            s.free = [te]
            sl, wv_, tw_ = eload(expert("w_down", b, ev), 4, 1024)
            for c in range(2):
                s = OR.get()
                pe.need(*s.free, tw_, te)
                for f in range(4):
                    tp = q_mm(s.ap, ht_.ap[:, f, :], wv_[:, f, c * 512:(c + 1) * 512], f == 0, f == 3)
                ac.need(tp, *y.free)
                tc = q_act(y.ap[:, c * 512:(c + 1) * 512], s.ap, ACT.Copy)
                s.free = [tc]
            ht_.free = [tp]
            sl.free = [tp]
            y.free = [(mq if ev is None else xq).copy(ys_dram[b * 128:(b + 1) * 128, :], y.ap, tc)]

        pipe([(b, None) for b in range(16)], fetch, turn_x, gate_up, down)

        barrier()
        sy.need(*[e.last for e in (pe, ve, ac, po)], *mq.outstanding())
        engs = (pe, ve, ac, po, sy)
        for e in engs:
            e.need(t_ctl)
        before = [(e, e.n, dict(e.seen)) for e in engs]
        wbefore = wq.n
        vals = {}
        for e in engs:
            vals[e] = e.eng.value_load(ctli[0:1, 0:1], min_val=0, max_val=7)
        ev = [sy.eng.value_load(ctli[0:1, 1 + b:2 + b], min_val=0, max_val=15) for b in range(7)]
        for e in engs:
            e.queue = []
        pipe([(b, ev) for b in range(16, NBLK)], fetch, turn_x, gate_up, down)
        po.need(*xq.outstanding())
        po.later(lambda: gt.memset(ctl, 0.0))
        for e, n, seen in before:
            todo, e.queue = e.queue, None
            with e.eng.If(vals[e] > 0):
                for f in todo:
                    f()
            with e.eng.Else():
                if e is not sy:
                    e.skip(n)
                else:
                    wq.skip(wbefore)
            e.seen = seen
        barrier()
        g2 = Ring([ar.t[:, 4096 * i:4096 * i + 1024] for i in range(4)])
        for t in ALLT:
            for j, pw in ((0, p1), (1, p2)):
                g = g2.get()
                tg = mq.gather(g.ap, ys_dram, rowi[:, 2 + j, t:t + 1], *g.free)
                g.free = [vop(lambda: vt.scalar_tensor_tensor(out=X[:, t, :], in0=g.ap, scalar=pw[:, t:t + 1],
                                                              in1=X[:, t, :], op0=ALU.mult, op1=ALU.add), tg)]
        WR.slots = [WR.slots[i] for i in order]
        WR.n = 0
        barrier()

        small.at = smark
        w = a["w_in_2"]
        t_h = norm_turn(HT[:, :, :], 16, Place(AR, ARN, 0), [])
        xv = xs_dram.rearrange("(t p) d -> p t d", p=128)
        mq.copy(xv, X[:, :, :])
        barrier()
        ar = Place(AR, ARN)
        oA = ar.take(4, 512)
        oB = ar.take(4, 512)
        base = ar.at

        qT = ar.take(8, 512)
        kT = ar.take(8, 512)
        fv = ar.take(4, 512)
        cT = ar.take(3, 512)
        kpe = ar.take(4, 32)
        cosb = ar.take(4, 16)
        sinb = ar.take(4, 16)
        scr = Place(AR, ARN, ar.at)
        posr = small.take(4).bitcast(I32)
        posf = small.take(4)
        tpi = mq.copy(posr, a["positions_2"][0].rearrange("(t p) -> p t", p=128), allow_slow_non_contiguous=True)
        vop(lambda: vt.tensor_copy(posf, posr), tpi)
        ang, kk_, rr = scr.take(4, 16), scr.take(4, 16), scr.take(4, 16)
        for t in ALLT:
            vop(lambda: vt.tensor_scalar(ang[:, t, :], C["invf"], posf[:, t:t + 1], None, ALU.mult))
        MAGIC = 12582912.0
        c1 = float(np.float32(6.28125))
        c2 = float(np.float32(TWO_PI - 6.28125))
        c3 = float(np.float32(TWO_PI - 6.28125 - float(np.float32(TWO_PI - 6.28125))))
        hp = float(np.float32(np.pi / 2))
        PIF = 3.1415925
        for dst, q0, ph in ((sinb, 0.0, 0.0), (cosb, 0.25, hp)):
            vop(lambda: vt.tensor_scalar(kk_, ang, float(1.0 / TWO_PI), q0, ALU.mult, ALU.add))
            vop(lambda: vt.tensor_scalar(kk_, kk_, MAGIC, None, ALU.add))
            vop(lambda: vt.tensor_scalar(kk_, kk_, -MAGIC, None, ALU.add))
            vop(lambda: vt.scalar_tensor_tensor(out=rr, in0=kk_, scalar=-c1, in1=ang, op0=ALU.mult, op1=ALU.add))
            vop(lambda: vt.scalar_tensor_tensor(out=rr, in0=kk_, scalar=-c2, in1=rr, op0=ALU.mult, op1=ALU.add))
            vop(lambda: vt.scalar_tensor_tensor(out=rr, in0=kk_, scalar=-c3, in1=rr, op0=ALU.mult, op1=ALU.add))
            vop(lambda: vt.tensor_scalar(rr, rr, ph, PIF, ALU.add, ALU.min))
            t1 = vop(lambda: vt.tensor_scalar(rr, rr, -PIF, None, ALU.max))
            ac.need(t1)
            t1 = ac.mark(st.activation(dst, rr, ACT.Sin))
            ve.need(t1)

        sw, wv, tw = wload(wcols(w, 2176, 416), 8, 416)
        cb = Ring([scr.take(384) for _ in range(2)])
        sqb = scr.take(384)
        sc = [small.take(1) for _ in range(8)]
        for t in ALLT:
            ps, tp = proj(HT, t, 8, wv, 0, 416, SR, tw)
            b = cb.get()
            ve.need(tp)
            tkp = ve.mark(vt.tensor_copy(kpe[:, t, :], ps.ap[:, 384:416]))
            lo = 0
            for n, o, k4 in ((256, 0, 0), (128, 256, 4)):
                ac.need(tp, ve.last)
                t1 = ac.mark(st.activation(sqb[:, o:o + n], ps.ap[:, o:o + n], ACT.Square, accum_out=sc[k4]))
                t1 = rstd(sc[k4 + 1], sc[k4], n, (sc[k4 + 2], sc[k4 + 3]), t1)
                ve.need(t1, *b.free)
                t1 = ve.mark(vt.tensor_scalar(b.ap[:, o:o + n], ps.ap[:, o:o + n], sc[k4 + 1], None, ALU.mult))
            ps.free = [t1, tkp]
            tcT, tpp = turn4(b.ap, cT, t, 3, t1, 57)
            b.free = [tpp]
        sw.free = [tp]
        c3_, s3_ = cosb, sinb
        ra = Ring([scr.take(8, 32) for _ in range(2)])

        def rope(dst, src, t, nh, scr_, tok):
            c, s = mid(cosb[:, t, :], nh), mid(sinb[:, t, :], nh)
            u = scr_
            ve.need(tok)
            ve.mark(vt.tensor_tensor(u[:, 0:nh, 0:16], src[:, :, 16:32], s, ALU.mult))
            t1 = ve.mark(vt.tensor_tensor(u[:, 0:nh, 16:32], src[:, :, 0:16], s, ALU.mult))
            ve.mark(vt.tensor_tensor(dst[:, :, 0:16], src[:, :, 0:16], c, ALU.mult))
            t2 = ve.mark(vt.tensor_tensor(dst[:, :, 16:32], src[:, :, 16:32], c, ALU.mult))
            ve.need(t1, t2)
            ve.mark(vt.tensor_tensor(dst[:, :, 0:16], dst[:, :, 0:16], u[:, 0:nh, 0:16], ALU.subtract))
            return ve.mark(vt.tensor_tensor(dst[:, :, 16:32], dst[:, :, 16:32], u[:, 0:nh, 16:32], ALU.add))

        kpr = scr.take(4, 32)
        for t in ALLT:
            tkr = rope(kpr[:, t:t + 1, :], kpe[:, t:t + 1, :], t, 1, ra.get().ap, tkp)
            ve.need(tkr)
        s1, wq_, tw1 = wload(a["w_uq_2"].rearrange("(k p) n -> p k n", p=128), 2, 768)
        s2, wk_, tw2 = wload(a["w_ukv_2"].rearrange("(k p) n -> p k n", p=128), 1, 1024)
        qb = Ring([scr.take(8, 96) for _ in range(2)])
        msc = 1.0 / float(np.sqrt(96.0))
        qp = scr.take(8, 32)
        stm = {}

        def turn_h(u, tk, dst, t):
            pe.need(tk)
            for g in range(2):
                s = TR.get()
                pe.need(*s.free)
                for j in range(4):
                    r = pt_.transpose(s.ap[0:96, j * 128:(j + 1) * 128], u.ap[:, 4 * g + j, :], ident)
                tp = pe.mark(r)
                ac.need(tp)
                te = ac.mark(st.activation(dst[0:96, 4 * g:4 * g + 4, t * 128:(t + 1) * 128],
                                           s.ap[0:96, :].rearrange("p (h q) -> p h q", q=128), ACT.Copy))
                s.free = [te]
            u.free = [tp]
            return te

        def mq_(t):
            u = qb.get()
            ve.need(*u.free)
            qt = {}
            for hf in range(2):
                ps, tp = proj(cT, t, 2, wq_, 384 * hf, 384, SR, tw1, tcT)
                v = ps.ap[:, 0:384].rearrange("p (h d) -> p h d", d=96)
                ve.need(tp)
                t1 = ve.mark(vt.tensor_scalar(u.ap[:, 4 * hf:4 * hf + 4, 0:64], v[:, :, 0:64], msc, None, ALU.mult))
                t2 = ve.mark(vt.tensor_scalar(qp[:, 4 * hf:4 * hf + 4, :], v[:, :, 64:96], msc, None, ALU.mult))
                ps.free = [t2]
            t3 = rope(u.ap[:, :, 64:96], qp, t, 8, ra.get().ap, t2)
            stm[("q", t)] = (u, t3)
            stm["pe"] = tp

        def mk_(t):
            u = qb.get()
            ve.need(*u.free)
            for hf in range(2):
                s = SR.get()
                pe.need(*s.free, tw2, tcT)
                tp = pe.mark(mm(s.ap, cT[:, 2, t * 128:(t + 1) * 128], wk_[:, 0, 512 * hf:512 * hf + 512], True, True))
                v = s.ap.rearrange("p (h d) -> p h d", d=128)
                ve.need(tp)
                t1 = ve.mark(vt.tensor_copy(u.ap[:, 4 * hf:4 * hf + 4, 0:64], v[:, :, 0:64]))
                ac.need(tp, t1)
                t2 = ac.mark(st.copy(fv[:, t, 256 * hf:256 * hf + 256].rearrange("p (h d) -> p h d", d=64),
                                     v[:, :, 64:128]))
                s.free = [t2]
            t3 = ve.mark(vt.tensor_copy(u.ap[:, :, 64:96], mid(kpr[:, t, :], 8)))
            stm[("k", t)] = (u, t3)
            stm["pe"], stm["v"] = tp, t2

        for t in ALLT:
            mq_(t)
            mk_(t)
            stm["e"] = turn_h(*stm[("q", t)], qT, t)
            stm["e"] = turn_h(*stm[("k", t)], kT, t)
        s1.free = [stm["pe"]]
        s2.free = [stm["pe"]]
        att = Attend(scr)
        ri8 = small.take(8)

        def fin3(i, o, tp, rs, te):
            return divide(oB[:, i, :], o, tp, rs, te, ri8)

        att.run(lambda h: qT[:, h, :], lambda h: kT[:, h, :], lambda h, j: fv[:, j, h * 64:(h + 1) * 64],
                96, fin3, [stm["e"], stm["v"]])
        barrier()

        ar = Place(AR, ARN, base)
        rT, kkT, vT, cumT = (ar.take(4, 512) for _ in range(4))
        aT = ar.take(4, 512)
        wa = ar.take(512)
        scr = Place(AR, ARN, ar.at)
        raw = Ring([scr.take(513) for _ in range(2)])
        dif = Ring([scr.take(512) for _ in range(2)])
        for r_ in raw.slots:
            r_.free = [po.mark(gt.memset(r_.ap[:, 0:1], 0.0))]
        dst = [rT, kkT, vT]
        tf = {}
        for n in range(13):
            if n % 4 == 0:
                wd_ = min(512, 1664 - 128 * n)
                sw, wv, tw = wload(wcols(w, 128 * n, wd_), 8, wd_)
            s = SR.get()
            pe.need(*s.free, tw)
            for k in range(8):
                r = mm(s.ap, wv[:, k, (n % 4) * 128:(n % 4) * 128 + 128], HT[:, k, :], k == 0, k == 7)
            tp = pe.mark(r)
            if n % 4 == 3 or n == 12:
                sw.free = [tp]
            b, d = raw.get(), dif.get()
            ac.need(tp, *b.free)
            t1 = ac.mark(st.copy(b.ap[:, 1:513], s.ap))
            s.free = [t1]
            ve.need(t1, *d.free, *b.free)
            t2 = ve.mark(vt.tensor_tensor(d.ap, b.ap[:, 0:512], b.ap[:, 1:513], ALU.subtract))
            o = dst[n // 4][:, n % 4, :] if n < 12 else wa
            ve.need(t2)
            t3 = ve.mark(vt.scalar_tensor_tensor(out=o, in0=d.ap, scalar=PT[:, 24 + n:25 + n], in1=b.ap[:, 1:513],
                                                 op0=ALU.mult, op1=ALU.add))
            b.free, d.free = [t3], [t3]
        t_f = t3
        s1, wl, tw1 = WR.get(), None, None
        wl = s1.ap[:, 0:512]
        tw1 = wq.copy(wl[0:64, :], a["w_decay_up_2"], *s1.free)
        tw2 = wq.copy(wl[64:128, :], a["w_iclr_up_2"])
        ac.need(t_f)
        t1 = ac.mark(st.activation(wa[0:64, :], wa[0:64, :], ACT.Tanh))
        for n in range(4):
            for j, (p0, col, d_) in enumerate(((0, 37, cumT), (64, 41, aT))):
                s = OR.get()
                pe.need(*s.free, t1, tw1, tw2)
                tp = pe.mark(mm(s.ap, wl[p0:p0 + 64, n * 128:(n + 1) * 128], wa[p0:p0 + 64, :], True, True))
                ac.need(tp)
                t2 = ac.mark(st.activation(d_[:, n, :], s.ap, ACT.Sigmoid, bias=PT[:, col + n:col + n + 1]))
                s.free = [t2]
        s1.free = [tp]
        t_sg = t2
        be = scr.take(4, 512)
        bufs = Ring([scr.take(512) for _ in range(2)])
        rkb = small.take(4)
        kap = kkT
        al = ar_al = None
        kn_at = scr.at
        kn = scr.take(4, 512)
        sel = small.take(4, 2)
        for n in range(4):
            ve.need(ve.last)
            ve.mark(vt.tensor_scalar(sel[:, n, :], C["hsel"], PT[:, 53 + n:54 + n], None, ALU.mult))
        dia = scr.take(4, 8)
        for n in range(4):
            b = bufs.get()
            t1 = vop(lambda: vt.tensor_scalar(kn[:, n, :], kkT[:, n, :], PT[:, 45 + n:46 + n], None, ALU.mult))
            ac.need(t1, *b.free)
            t2 = ac.mark(st.activation(b.ap, kn[:, n, :], ACT.Square))
            s = OR.get()
            pe.need(t2, *s.free)
            tp = pe.mark(mm(s.ap, C["bd"], b.ap, True, True))
            ve.need(tp)
            m_ = b.ap
            t3 = vop(lambda: vt.tensor_scalar(m_, s.ap, 1e-24, None, ALU.max))
            s.free = [t3]
            b2 = bufs.get()
            y_ = b2.ap
            ac.need(t3)
            t4 = ac.mark(st.activation(y_, m_, ACT.Sqrt, scale=float(2.0 ** 40)))
            vop(lambda: vt.reciprocal(y_, y_), t4)
            vop(lambda: vt.tensor_scalar(y_, y_, float(2.0 ** 20), None, ALU.mult))
            vop(lambda: vt.tensor_tensor(m_, m_, y_, ALU.mult))
            vop(lambda: vt.tensor_tensor(m_, m_, y_, ALU.mult))
            vop(lambda: vt.tensor_scalar(m_, m_, -0.5, 1.5, ALU.mult, ALU.add))
            vop(lambda: vt.tensor_tensor(y_, y_, m_, ALU.mult))
            vop(lambda: vt.tensor_tensor(kn[:, n, :], kn[:, n, :], y_, ALU.mult))
            vop(lambda: vt.tensor_tensor(be[:, n, :], kn[:, n, :], aT[:, n, :], ALU.mult), t_sg)
            vop(lambda: vt.tensor_scalar(m_, aT[:, n, :], 1.0, PT[:, 49 + n:50 + n], ALU.subtract, ALU.mult))
            t5 = vop(lambda: vt.scalar_tensor_tensor(out=kkT[:, n, :], in0=m_, scalar=1.0, in1=kkT[:, n, :],
                                                     op0=ALU.add, op1=ALU.mult))
            t6 = vop(lambda: vt.tensor_tensor(m_, rT[:, n, :], kkT[:, n, :], ALU.mult))
            s = OR.get()
            pe.need(t6, *s.free)
            for t in ALLT:
                r = mm(s.ap[:, 2 * t:2 * t + 2], m_[:, t * 128:(t + 1) * 128], sel[:, n, :], True, True)
            tp = pe.mark(r)
            b.free = [tp]
            t7 = vop(lambda: vt.tensor_copy(dia[:, :, 2 * n:2 * n + 2],
                                            s.ap[:, 0:8].rearrange("p (t c) -> p t c", c=2)), tp)
            s.free = [t7]
            b2.free = [t7]
        scn = bufs.get().ap
        on = bufs.get().ap
        po.need(*[x for b_ in bufs.slots for x in b_.free])
        to = po.mark(gt.memset(on, 1.0))
        dmid = small.take(4, 4)
        dend = small.take(4, 4)
        for n in range(4):
            for c in ALLT:
                vop(lambda: vt.tensor_tensor_scan(scn[:, c * 128:(c + 1) * 128], on[:, 0:128],
                                                  cumT[:, n, c * 128:(c + 1) * 128], 0.0, ALU.mult, ALU.add), to)
            for c in ALLT:
                vop(lambda: vt.tensor_copy(dmid[:, n, c:c + 1], scn[:, c * 128 + 63:c * 128 + 64]))
            t1 = vop(lambda: vt.tensor_tensor(scn.rearrange("p (c q) -> p c q", q=128),
                                              scn.rearrange("p (c q) -> p c q", q=128),
                                              bc(dmid[:, n, :], 128), ALU.subtract))
            t2 = vop(lambda: vt.tensor_tensor(aT[:, n, :], scn, cumT[:, n, :], ALU.subtract))
            ac.need(t2)
            t3 = ac.mark(st.activation(aT[:, n, :], aT[:, n, :], ACT.Exp, scale=-DECAY))
            t4 = ac.mark(st.activation(cumT[:, n, :], scn, ACT.Exp, scale=-DECAY))
            t5 = ac.mark(st.activation(scn, scn, ACT.Exp, scale=DECAY))
            vop(lambda: vt.scalar_tensor_tensor(out=kn[:, n, :], in0=kn[:, n, :], scalar=-1.0, in1=aT[:, n, :],
                                                op0=ALU.mult, op1=ALU.mult), t3)
            vop(lambda: vt.tensor_copy(dend[:, n, :], cumT[:, n, :].rearrange("p (c q) -> p c q", q=128)[:, :, 127]), t4)
            vop(lambda: vt.tensor_tensor(rT[:, n, :], rT[:, n, :], cumT[:, n, :], ALU.mult))
            vop(lambda: vt.tensor_tensor(be[:, n, :], be[:, n, :], scn, ALU.mult), t5)
            vop(lambda: vt.tensor_tensor(kkT[:, n, :], kkT[:, n, :], scn, ALU.mult))
        t1 = ve.last
        ac.need(t1)
        t_dm = ac.mark(st.activation(dmid, dmid, ACT.Exp, scale=-DECAY))
        barrier()

        alT, beT, kaT = kn, be, kkT
        scr2 = Place(AR, ARN, scr.at)
        vTM = ar_v = aT
        beTM = cumT
        kaTM = scr2.take(4, 512)
        for src, d_ in ((vT, vTM), (beT, beTM), (kaT, kaTM)):
            for n in range(4):
                s = TR.get()
                pe.need(*s.free)
                for t in ALLT:
                    r = pt_.transpose(s.ap[:, t * 128:(t + 1) * 128], src[:, n, t * 128:(t + 1) * 128], ident)
                tp = pe.mark(r)
                ac.need(tp)
                te = ac.mark(st.copy(d_[:, :, n * 128:(n + 1) * 128], s.ap.rearrange("p (t c) -> p t c", c=128)))
                s.free = [te]
        barrier()
        fr = Place(X[:, :, :].rearrange("p a b -> p (a b)"), 4096)
        w8 = lambda: fr.take(8, 128)
        LT, AK, RB, RK = vT.rearrange("p a b -> p (a b)")[:, 0:1024].rearrange("p (h t) -> p h t", t=128), w8(), \
            vT.rearrange("p a b -> p (a b)")[:, 1024:2048].rearrange("p (h t) -> p h t", t=128), w8()
        raws = Place(AR, ARN, ar.at - 512)
        T0 = raws.take(8, 128)
        TT0 = raws.take(8, 128)
        MS = w8()
        UU = w8()
        fr = Place(AR, ARN, scr2.at)
        S0 = bufs.slots[0].ap.rearrange("p (a b) -> p a b", b=128)
        SA = bufs.slots[1].ap
        RHS = fr.take(512)
        for z in (LT, AK, RB, RK):
            po.mark(gt.memset(z, 0.0))
        t_z = po.mark(gt.memset(S0, 0.0))
        ys = oA
        stri = C["stri"].bitcast(U32)
        tri = C["tri"].bitcast(U32)

        def two(dst, f):
            res = []
            for par in range(2):
                s = SR.get()
                pe.need(*s.free)
                for j in range(4):
                    l_, r_ = f(2 * j + par)
                    r = mm(s.ap[:, j * 128:(j + 1) * 128], l_, r_, True, True)
                res.append((s, pe.mark(r)))
            return res

        t_s = t_z
        for c in ALLT:
            cs = slice(c * 128, (c + 1) * 128)

            def hT(x, h):
                return x[64 * (h % 2):64 * (h % 2) + 64, h // 2, cs]

            for dst_, lx, rx, mk in ((LT, beT, alT, stri), (AK, kaT, alT, stri), (RB, beT, rT, tri), (RK, kaT, rT, tri)):
                for par, (s, tp) in enumerate(two(dst_, lambda h: (hT(lx, h), hT(rx, h)))):
                    v = dst_.rearrange("p (a b) t -> p a b t", b=2)[:, :, par, :]
                    ve.need(tp, t_z, pe.last)
                    te = ve.mark(vt.copy_predicated(v, mid(mk, 4), s.ap.rearrange("p (a t) -> p a t", t=128)))
                    s.free = [te]
            t1 = vop(lambda: vt.tensor_tensor(TT0, LT, mid(C["lv1"], 8), ALU.mult))
            t1 = vop(lambda: vt.tensor_tensor(TT0, TT0, mid(ident, 8), ALU.add))
            for g in range(2):
                s = TR.get()
                pe.need(*s.free, t1)
                for j in range(4):
                    r = pt_.transpose(s.ap[:, j * 128:(j + 1) * 128], TT0[:, 4 * g + j, :], ident)
                tp = pe.mark(r)
                ac.need(tp, pe.last)
                te = ac.mark(st.copy(T0[:, 4 * g:4 * g + 4, :], s.ap.rearrange("p (h t) -> p h t", t=128)))
                s.free = [te]
            tT = te
            tTT = t1
            for m in (2, 4, 8, 16, 32, 64):
                po.need(ve.last, pe.last)
                tM = po.mark(gt.tensor_tensor(MS, LT, mid(C[f"lv{m}"], 8), ALU.mult))
                for g in range(2):
                    s = SR.get()
                    pe.need(*s.free, tM, tT, tTT)
                    for j in range(4):
                        r = mm(s.ap[:, j * 128:(j + 1) * 128], MS[:, 4 * g + j, :], T0[:, 4 * g + j, :], True, True)
                    tp = pe.mark(r)
                    ac.need(tp)
                    tU = ac.mark(st.copy(UU[:, 4 * g:4 * g + 4, :], s.ap.rearrange("p (h t) -> p h t", t=128)))
                    s.free = [tU]
                nxt = []
                for g in range(2):
                    pe.need(tU)
                    for kind in range(2):
                        if kind == 0 and m == 64:
                            continue
                        s = TR.get() if kind else SR.get()
                        pe.need(*s.free)
                        for j in range(4):
                            h = 4 * g + j
                            if kind == 0:
                                r = mm(s.ap[:, j * 128:(j + 1) * 128], TT0[:, h, :], UU[:, h, :], True, True)
                            else:
                                r = mm(s.ap[:, j * 128:(j + 1) * 128], UU[:, h, :], TT0[:, h, :], True, True)
                        nxt.append((g, kind, s, pe.mark(r)))
                for g, kind, s, tp in nxt:
                    d_ = (T0, TT0)[kind][:, 4 * g:4 * g + 4, :]
                    ve.need(pe.last)
                    te = ve.mark(vt.tensor_tensor(d_, s.ap.rearrange("p (h t) -> p h t", t=128), d_, ALU.add))
                    s.free = [te]
                tT = tTT = te
            if c == 0:
                t_s0 = t_z
            ve.need(t_s, t_dm)
            for n in range(4):
                t_s0 = ve.mark(vt.tensor_scalar(S0[:, n, :], S0[:, n, :], dmid[:, n, c:c + 1], None, ALU.mult))
            s = OR.get()
            pe.need(*s.free, t_s0, tT)
            for n in range(4):
                mm(s.ap[:, n * 128:(n + 1) * 128], alT[:, n, cs], S0[:, n, :], n == 0, True, True)
            for h in range(8):
                r = mm(s.ap[:, h * 64:(h + 1) * 64], AK[:, h, :], vTM[:, c, h * 64:(h + 1) * 64], False, True, True)
            tp = pe.mark(r)
            ac.need(tp)
            t1 = ac.mark(st.copy(RHS, s.ap))
            s.free = [t1]
            s = OR.get()
            pe.need(*s.free, t1)
            for h in range(8):
                r = mm(s.ap[:, h * 64:(h + 1) * 64], TT0[:, h, :], RHS[:, h * 64:(h + 1) * 64], True, True)
            tp = pe.mark(r)
            ac.need(tp)
            t1 = ac.mark(st.copy(SA, s.ap))
            s.free = [t1]
            s = OR.get()
            pe.need(*s.free, t1)
            for n in range(4):
                mm(s.ap[:, n * 128:(n + 1) * 128], rT[:, n, cs], S0[:, n, :], n == 0, True, True)
            for h in range(8):
                mm(s.ap[:, h * 64:(h + 1) * 64], RB[:, h, :], SA[:, h * 64:(h + 1) * 64], False, True, True)
                r = mm(s.ap[:, h * 64:(h + 1) * 64], RK[:, h, :], vTM[:, c, h * 64:(h + 1) * 64], False, True, True)
            tp = pe.mark(r)
            ac.need(tp)
            t1 = ac.mark(st.copy(ys[:, c, :], s.ap))
            s.free = [t1]
            s = SR.get()
            pe.need(*s.free)
            for n in range(4):
                mm(s.ap[:, n * 128:(n + 1) * 128], beTM[:, c, n * 128:(n + 1) * 128], SA[:, n * 128:(n + 1) * 128],
                   True, False)
                r = mm(s.ap[:, n * 128:(n + 1) * 128], kaTM[:, c, n * 128:(n + 1) * 128],
                       vTM[:, c, n * 128:(n + 1) * 128], False, True)
            tp = pe.mark(r)
            ve.need(tp)
            for par in range(2):
                q = slice(64 * par, 64 * par + 64)
                sv_ = s.ap[q, :].rearrange("p (n v) -> p n v", v=128)[:, :, 64 * par:64 * par + 64]
                S_ = S0[q, :, 64 * par:64 * par + 64]
                vop(lambda: vt.tensor_tensor(S_, sv_, S_, ALU.add))
                t_s = vop(lambda: vt.tensor_tensor(S_, S_, bc(dend[q, :, c], 64), ALU.mult))
            s.free = [ve.last]
        barrier()

        mq.copy(X[:, :, :], xv)

        ar = Place(AR, ARN, base)
        vTM_ = vTM
        nf = Place(AR, ARN, scr2.at)
        gnb = nf.take(1024)
        bgb = rT.rearrange("p a b -> p (a b)")
        gpb = be.rearrange("p a b -> p (a b)")[:, 0:1024]
        tg = [mq.copy(gnb[:, 0:512], a["gn_gain_2"].unsqueeze(0).to_broadcast([128, 512])),
              mq.copy(gnb[:, 512:1024], a["gn_bias_2"].unsqueeze(0).to_broadcast([128, 512])),
              mq.copy(bgb, a["b_gate_2"].unsqueeze(0).to_broadcast([128, 2048])),
              mq.copy(gpb, a["g_post_2"].unsqueeze(0).to_broadcast([128, 1024]))]
        ve.need(*tg)
        v8 = lambda x: x.rearrange("p (h d) -> p h d", d=64)
        t8 = [b_.ap for b_ in bufs.slots]
        mu8, va8, rs8, m8, y8 = (small.take(8) for _ in range(5))
        for t in ALLT:
            y = v8(ys[:, t, :])
            vop(lambda: vt.reduce_sum(mu8, y, AX.X))
            vop(lambda: vt.tensor_scalar(mu8, mu8, 1.0 / 64, None, ALU.mult))
            t1 = vop(lambda: vt.tensor_tensor(y, y, bc(mu8, 64), ALU.subtract))
            ac.need(t1)
            t2 = ac.mark(st.activation(t8[0], ys[:, t, :], ACT.Square))
            t3 = vop(lambda: vt.reduce_sum(va8, v8(t8[0]), AX.X), t2)
            rstd(rs8, va8, 64, (m8, y8), t3, 1.0, GN_EPS)
            vop(lambda: vt.tensor_tensor(y, y, bc(rs8, 64), ALU.mult))
            vop(lambda: vt.tensor_tensor(ys[:, t, :], ys[:, t, :], gnb[:, 0:512], ALU.mult))
            vop(lambda: vt.tensor_tensor(ys[:, t, :], ys[:, t, :], gnb[:, 512:1024], ALU.add))
            vop(lambda: vt.tensor_tensor(v8(t8[1]), v8(vTM[:, t, :]), bc(dia[:, t, :], 64), ALU.mult))
            vop(lambda: vt.tensor_tensor(ys[:, t, :], ys[:, t, :], t8[1], ALU.add))
        for c0, o_ in ((1664, oA), (2592, oB)):
            sw, wv, tw = wload(wcols(w, c0, 512), 8, 512)
            for t in ALLT:
                ps, tp = proj(HT, t, 8, wv, 0, 512, SR, tw)
                ac.need(tp, ve.last)
                t1 = ac.mark(st.activation(t8[t % 2], ps.ap, ACT.Silu))
                ps.free = [t1]
                vop(lambda: vt.tensor_tensor(o_[:, t, :], o_[:, t, :], t8[t % 2], ALU.mult), t1)
            sw.free = [tp]
        barrier()
        oAT, oBT = kkT, vT
        for t in ALLT:
            turn4(oA[:, t, :], oAT, t, 4, None)
            te, _ = turn4(oB[:, t, :], oBT, t, 4, None)
        pe.need(te)
        mx = AR[:, base + 3 * 2048:base + 5 * 2048].rearrange("p (a b) -> p a b", b=1024)
        mxT = AR[:, kn_at:kn_at + 4096].rearrange("p (a b) -> p a b", b=512)
        mscr = Place(AR, base + 5 * 2048 + 512 + 2050, base + 5 * 2048)
        tm = merge(HT, w, 3104, [a["w_out_a_2"], a["w_out_b_2"]], [oAT, oBT], mx, mxT, mscr, bgb)
        barrier()
        yo = mx
        for c in range(2):
            sw, wv, tw = wload(wcols(a["w_o_2"], 512 * c, 512), 8, 512)
            for t in ALLT:
                ps, tp = proj(mxT, t, 8, wv, 0, 512, SR, tw, tm)
                ac.need(tp)
                t1 = ac.mark(st.copy(yo[:, t, c * 512:(c + 1) * 512], ps.ap))
                ps.free = [t1]
            sw.free = [tp]
        ss, rs, m, y = (small.take(4) for _ in range(4))
        junk = HT[:, 0:2, :].rearrange("p a b -> p (a b)")
        barrier()
        for t in ALLT:
            ac.need(ac.last)
            t1 = ac.mark(st.activation(junk, yo[:, t, :], ACT.Square, accum_out=ss[:, t:t + 1]))
        rstd(rs, ss, 1024, (m, y), t1)
        outv = out[0].rearrange("(t p) d -> p t d", p=128)
        for t in ALLT:
            vop(lambda: vt.scalar_tensor_tensor(out=yo[:, t, :], in0=yo[:, t, :], scalar=rs[:, t:t + 1], in1=gpb,
                                                op0=ALU.mult, op1=ALU.mult))
            t2 = vop(lambda: vt.tensor_tensor(yo[:, t, :], yo[:, t, :], X[:, t, :], ALU.add))
            oq.copy(outv[:, t, :], yo[:, t, :], t2)
        sy.need(*oq.outstanding())


_INS = ["x", "norm_mix_g", "w_in", "b_forget", "fox_q_g", "fox_k_g", "nsa_q_g", "nsa_k_g", "cmp_k_w1", "cmp_k_w2",
        "cmp_k_pos", "cmp_v_w1", "cmp_v_w2", "cmp_v_pos", "w_fox_up", "w_nsa_up", "w_out", "norm_ffn_g", "w_group",
        "b_group", "w_router", "b_router", "w_gate", "w_up", "w_down", "positions_2", "g_pre_2", "w_in_2",
        "b_gate_2", "mu_shift_2", "w0_2", "w_decay_up_2", "a0_2", "w_iclr_up_2", "k_k_2", "k_a_2", "r_k_2",
        "gn_gain_2", "gn_bias_2", "w_out_a_2", "g_q_2", "w_uq_2", "g_kv_2", "w_ukv_2", "w_out_b_2", "w_o_2",
        "g_post_2"]


def kernel(**inputs):
    import numpy as _np
    import concourse.bacc as _bacc
    from concourse import mybir as _mybir
    from concourse.bass_utils import run_bass_kernel_spmd as _run

    nc = _bacc.Bacc("TRN2", target_bir_lowering=False, num_devices=1)
    consts, coff = constants()
    arrays, args = {}, {}
    for name in _INS:
        arrays[f"in_{name}_dram"] = _np.ascontiguousarray(inputs[name])
    arrays["in_consts_dram"] = consts
    for key, arr in arrays.items():
        args[key[3:-5]] = nc.dram_tensor(key, arr.shape, _mybir.dt.from_np(arr.dtype), kind="ExternalInput").ap()
    out = nc.dram_tensor("out_0_dram", (1, 512, 1024), _mybir.dt.float32, kind="ExternalOutput").ap()
    spill = nc.dram_tensor("spill", (512, 1024), _mybir.dt.float32, kind="Internal").ap()
    tab = nc.dram_tensor("tab", (23 * 128, 1), _mybir.dt.uint32, kind="Internal").ap()
    ys = nc.dram_tensor("ys", (23 * 128, 1024), _mybir.dt.float32, kind="Internal").ap()
    build(nc, args, coff, out, spill, tab, ys)
    r = _run(nc, [arrays], core_ids=[0])
    return r.results[0]["out_0_dram"]
```

```python
from contextlib import ExitStack

import numpy as np

import concourse.bass as bass
from concourse import mybir

F32 = mybir.dt.float32
BF16 = mybir.dt.bfloat16
U32 = mybir.dt.uint32
I32 = mybir.dt.int32
ALU = mybir.AluOpType
ACT = mybir.ActivationFunctionType
AX = mybir.AxisListType

EPS = 1e-6
GN_EPS = 64e-5
NEG = -1e30
DECAY = 0.6065306597
TWO_PI = 2.0 * np.pi


def constants():
    p = np.arange(128)
    parts, off = [], {}

    def put(name, a):
        a = np.asarray(a, np.float32).reshape(128, -1)
        off[name] = (sum(x.shape[1] for x in parts), a.shape[1])
        parts.append(a)

    put("ident", np.eye(128))
    put("tri", (p[:, None] <= p[None, :]))
    put("stri", (p[:, None] < p[None, :]))
    put("ones", np.ones((128, 128)))
    put("causal", np.where(p[None, :] <= p[:, None], 0.0, NEG))
    q = p[:, None] + 128 * np.arange(4)[None, :]
    n = np.arange(32)
    ok = (n[None, None, :] * 16 + 31 <= q[:, :, None]) & (n < 31)[None, None, :]
    put("cmask", np.where(ok, 0.0, NEG))
    put("anyv", (q >= 31))
    sl = 2.0 ** -(np.arange(8) + 1.0)
    qa = np.zeros((128, 4, 8, 2))
    qa[..., 0] = sl[None, None, :]
    qa[..., 1] = -sl[None, None, :] * q[:, :, None]
    put("qaug", qa)
    ka = np.zeros((128, 4, 2))
    ka[..., 0] = q
    ka[..., 1] = 1.0
    put("kaug", ka)
    ca = np.zeros((128, 2))
    ca[:, 0] = np.where(p % 32 < 31, (p % 32) * 16 + 31, 0)
    ca[:, 1] = 1.0
    put("caug", ca)
    put("lv1", (p[None, :] % 2 == 1) & (p[:, None] == p[None, :] - 1))
    for m in (2, 4, 8, 16, 32, 64):
        even = p[(p // m) % 2 == 0]
        put(f"um{m}", (p[:, None] // m == even[None, :] // m + 1))
    h8 = 2 * np.arange(4)[None, :, None] + (p // 64)[:, None, None] == np.arange(8)[None, None, :]
    put("hs8", h8)
    hb = np.zeros((128, 4, 128))
    hb[0:8] = h8.transpose(2, 1, 0)
    put("hb8", hb)
    put("hsel", (p[:, None] // 64 == np.arange(2)[None, :]))
    inv = (np.float32(10000.0) ** (-np.arange(0, 32, 2, dtype=np.float32) / np.float32(32))).astype(np.float32)
    put("invf", np.broadcast_to(inv, (128, 16)))
    put("e4", np.broadcast_to(np.arange(4), (128, 4)))
    put("io", np.broadcast_to(np.arange(128), (128, 128)))
    put("e16", np.broadcast_to(np.arange(16), (128, 16)))
    put("b7", np.broadcast_to(np.arange(7)[:, None], (128, 7, 16)))
    return np.concatenate(parts, 1), off


class Engine:

    def __init__(self, eng, sem):
        self.eng, self.sem, self.n, self.seen, self.queue = eng, sem, 0, {}, None

    def need(self, *tokens):
        for t in tokens:
            if t is not None and self.seen.get(t[0], 0) < t[2]:
                self.run(lambda sem=t[1], n=t[2]: self.eng.wait_ge(sem, n))
                self.seen[t[0]] = t[2]

    def run(self, f):
        if self.queue is None:
            f()
        else:
            self.queue.append(f)

    def mark(self, ins):
        self.n += 1
        ins.then_inc(self.sem, 1)
        return (id(self), self.sem, self.n)

    def later(self, f):
        self.n += 1
        self.run(lambda: f().then_inc(self.sem, 1))
        return (id(self), self.sem, self.n)

    @property
    def last(self):
        return (id(self), self.sem, self.n) if self.n else None

    def skip(self, n):
        self.eng.wait_ge(self.sem, n)
        if self.n > n:
            self.eng.sem_inc(self.sem, self.n - n)


class Queue:

    def __init__(self, engine, sems):
        self.engine, self.sems, self.n = engine, sems, 0

    def copy(self, dst, src, *tokens, **kw):
        return self.issue(lambda: self.engine.eng.dma_start(dst, src, **kw), *tokens)

    def gather(self, dst, src, rows, *tokens):
        at = bass.IndirectOffsetOnAxis(ap=rows, axis=0)
        return self.issue(lambda: self.engine.eng.indirect_dma_start(dst, None, src, at), *tokens)

    def scatter(self, dst, src, rows, *tokens):
        at = bass.IndirectOffsetOnAxis(ap=rows, axis=0)
        return self.issue(lambda: self.engine.eng.indirect_dma_start(dst, at, src, None), *tokens)

    def issue(self, start, *tokens):
        i = self.n % len(self.sems)
        self.engine.need(*tokens, self.token(self.n - len(self.sems)))
        self.engine.run(lambda: start().then_inc(self.sems[i], 16))
        self.n += 1
        return self.token(self.n - 1)

    def token(self, k):
        if k < 0:
            return None
        i = k % len(self.sems)
        return ((id(self), i), self.sems[i], 16 * (k // len(self.sems) + 1))

    def skip(self, n):
        for i in range(len(self.sems)):
            before, after = (len(range(i, k, len(self.sems))) for k in (n, self.n))
            if before:
                self.engine.eng.wait_ge(self.sems[i], 16 * before)
            if after > before:
                self.engine.eng.sem_inc(self.sems[i], 16 * (after - before))

    def outstanding(self):
        return [self.token(k) for k in range(max(0, self.n - len(self.sems)), self.n)]


class Slot:
    def __init__(self, ap):
        self.ap, self.free = ap, []


class Ring:
    def __init__(self, aps):
        self.slots, self.n = [Slot(a) for a in aps], 0

    def get(self):
        self.n += 1
        return self.slots[(self.n - 1) % len(self.slots)]


def weave(first, second, every=1):
    a, b = True, True
    n = 0
    while a or b:
        if a:
            a = next(first, None) is not None
        n += 1
        if b and (n % every == 0 or not a):
            b = next(second, None) is not None


def steps(items, *stages):
    for step in range(len(items) + len(stages) - 1):
        for s, stage in enumerate(stages):
            if stage is not None and 0 <= step - s < len(items):
                stage(items[step - s])
        yield 1


def pipe(items, *stages):
    for _ in steps(items, *stages):
        pass


def build(nc, a, coff, out, xs_dram, ys_dram):
    with ExitStack() as ctx:
        sem = lambda name: ctx.enter_context(nc.semaphore(name))
        pe = Engine(nc.tensor, sem("s_pe"))
        ve = Engine(nc.vector, sem("s_ve"))
        ac = Engine(nc.scalar, sem("s_ac"))
        po = Engine(nc.gpsimd, sem("s_po"))
        sy = Engine(nc.sync, sem("s_sy"))
        wq = Queue(sy, [sem(f"s_w{i}") for i in range(12)])
        mq = Queue(po, [sem(f"s_m{i}") for i in range(24)])
        xq = Queue(po, [sem(f"s_x{i}") for i in range(8)])
        oq = Queue(sy, [sem(f"s_o{i}") for i in range(4)])
        pt_, vt, st, gt = nc.tensor, nc.vector, nc.scalar, nc.gpsimd

        ncst = sum(v[1] for v in coff.values())
        sb = lambda name, shape, dt=F32: ctx.enter_context(nc.sbuf_tensor(name, shape, dt))
        cst = sb("cst", [128, ncst])
        C = {k: cst[:, o:o + n] for k, (o, n) in coff.items()}
        identb = sb("identb", [128, 128], BF16)
        causb = sb("causb", [128, 128], BF16)
        cmaskb = sb("cmaskb", [128, 128], BF16)
        X = sb("X", [128, 4, 1024])
        HT = sb("HT", [128, 8, 512])
        NW = 3
        NBLK = 23
        Wt = sb("Wt", [128, NW, 4096])
        PR = sb("PR", [96, 128])
        PT = sb("PT", [128, 96])
        BR = sb("BR", [128, 28])
        SM = sb("SM", [128, 1024])
        ARN = 29050
        AR = sb("AR", [128, ARN])
        banks = [ctx.enter_context(nc.psum_tensor(f"pb{i}", [128, 512], F32)) for i in range(8)]
        SR = Ring([b[:, :] for b in banks[0:3]])
        TR = Ring([b[:, :] for b in banks[3:6]])
        OR = Ring([b[:, :] for b in banks[6:8]])
        WR = Ring([Wt[:, i, :] for i in range(NW)])

        class Place:

            def __init__(self, t, n, at=0):
                self.t, self.n, self.at = t, n, at

            def take(self, *shape):
                k = int(np.prod(shape))
                assert self.at + k <= self.n, (self.at, k, self.n)
                v = self.t[:, self.at:self.at + k]
                self.at += k
                if len(shape) == 2:
                    v = v.rearrange("p (a b) -> p a b", b=shape[1])
                if len(shape) == 3:
                    v = v.rearrange("p (a b c) -> p a b c", b=shape[1], c=shape[2])
                return v

        small = Place(SM, 992)
        small_c = Place(SM, 1024, 992)

        def barrier():
            toks = [e.last for e in (pe, ve, ac, po)] + mq.outstanding()
            for e in (pe, ve, ac, po):
                e.need(*toks)

        def mm(o, lhsT, rhs, start, stop, skip=False):
            return pt_.matmul(o, lhsT, rhs, start=start, stop=stop, skip_group_check=skip)

        def wload(src, k, cols, *more):
            s = WR.get()
            v = s.ap[:, 0:k * cols].rearrange("p (k n) -> p k n", n=cols)
            tok = wq.copy(v, src, *s.free)
            s.free = []
            return s, v, tok

        def wcols(w, c0, n, rows=1024):
            return w[0:rows, c0:c0 + n].rearrange("(k p) n -> p k n", p=128)

        t_x = [wq.copy(X[:, t, :], a["x"][0, t * 128:(t + 1) * 128, :]) for t in range(4)]
        t_c = wq.copy(cst[:, :], a["consts"])
        w = a["w_in"][0]
        s0 = WR.get()
        v0 = s0.ap[:, 0:8 * 32].rearrange("p (k n) -> p k n", n=32)
        tw1 = wq.copy(v0[:, :, 0:8], wcols(w, 1536, 8), *s0.free)
        tw2 = wq.copy(v0[:, :, 8:32], wcols(w, 2824, 24))
        t_m1 = ve.mark(vt.memset(PR[:, :], 1.0))
        rows = [("norm_mix_g", 0, 8), ("norm_ffn_g", 8, 8), ("g_pre_2", 16, 8), ("mu_shift_2", 24, 13),
                ("w0_2", 37, 4), ("a0_2", 41, 4), ("k_k_2", 45, 4), ("k_a_2", 49, 4), ("r_k_2", 53, 4),
                ("g_q_2", 57, 2), ("g_kv_2", 59, 1), ("fox_q_g", 60, 1), ("fox_k_g", 61, 1),
                ("nsa_q_g", 62, 1), ("nsa_k_g", 63, 1), ("cmp_k_pos", 64, 16), ("cmp_v_pos", 80, 16)]
        t_pr = []
        for name, r, n in rows:
            src = a[name]
            while len(src.shape) > 1:
                src = src.rearrange("a b -> (a b)") if len(src.shape) == 2 else src.rearrange("a b c -> (a b c)")
            width = src.shape[0] // n
            q = mq if len(t_pr) % 2 else wq
            t_pr.append(q.copy(PR[r:r + n, 0:width], src.rearrange("(r w) -> r w", w=width), t_m1))
        for name, o, n in (("b_forget", 0, 8), ("b_group", 8, 4), ("b_router", 12, 16)):
            t_pr.append(mq.copy(BR[:, o:o + n], a[name].to_broadcast([128, n])))
        t_br = t_pr[-3:]

        ve.need(t_c)
        ve.mark(vt.tensor_copy(identb[:, :], C["ident"]))
        ve.mark(vt.tensor_copy(causb[:, :], C["causal"]))
        t_cb = ve.mark(vt.tensor_copy(cmaskb[:, :], C["cmask"]))
        s = TR.get()
        pe.need(t_c, *t_pr)
        t = pe.mark(pt_.transpose(s.ap[:, 0:96], PR[:, :], C["ident"][0:96, 0:96]))
        ve.need(t)
        t_pt = ve.mark(vt.tensor_copy(PT[:, :], s.ap[:, 0:96]))
        s.free = [t_pt]
        ident = C["ident"]
        for e in (pe, ve, ac, po):
            e.need(t_c, t_cb, t_pt, *t_br)

        def rstd(dst, ss, n, scr, tok, s=1.0, eps=EPS):
            m, y = scr
            ve.need(tok)
            t = ve.mark(vt.tensor_scalar(m, ss, 1.0 / n, eps, ALU.mult, ALU.add))
            ac.need(t)
            t2 = ac.mark(st.activation(y, m, ACT.Ln))
            ac.need(t2)
            t3 = ac.mark(st.activation(y, y, ACT.Exp, scale=-0.5))
            ve.need(t3)
            t = ve.mark(vt.tensor_tensor(dst, y, y, ALU.mult))
            ve.need(t)
            t = ve.mark(vt.tensor_tensor(dst, dst, m, ALU.mult))
            ve.need(t)
            t = ve.mark(vt.tensor_scalar(dst, dst, -0.5 * s, 1.5 * s, ALU.mult, ALU.add))
            ve.need(t)
            return ve.mark(vt.tensor_tensor(dst, dst, y, ALU.mult))

        def bc(ap, n):
            return ap.unsqueeze(len(ap.shape)).to_broadcast([*ap.shape, n])

        def mid(ap, n):
            return ap.unsqueeze(1).to_broadcast([ap.shape[0], n, *ap.shape[1:]])

        def norm_turn(dst, gcol, scr, make, use, store=None):
            buf = scr.take(2, 1024)
            ss, rs, m, y = (scr.take(4) for _ in range(4))
            ring = Ring([buf[:, i, :] for i in range(2)])
            done = []
            state, stored = {}, {}

            def scale(t):
                tokens = make(t)
                b = ring.get()
                ac.need(*tokens, *b.free)
                tk = ac.mark(st.activation(b.ap, X[:, t, :], ACT.Square, accum_out=ss[:, t:t + 1]))
                c = slice(t, t + 1)
                tr = rstd(rs[:, c], ss[:, c], 1024, (m[:, c], y[:, c]), tk)
                ve.need(tr, *tokens)
                tk = ve.mark(vt.tensor_scalar(b.ap, X[:, t, :], rs[:, t:t + 1], None, ALU.mult))
                state[t] = (b, tk)
                stored[t] = mq.copy(store[t * 128:(t + 1) * 128, :], b.ap, tk) if store is not None else None

            def turn(t):
                b, tk = state[t]
                pe.need(tk)
                for g in range(2):
                    s = TR.get()
                    pe.need(*s.free)
                    for j in range(4):
                        k = 4 * g + j
                        r = pt_.transpose(s.ap[:, j * 128:(j + 1) * 128], b.ap[:, k * 128:(k + 1) * 128], ident)
                    tp = pe.mark(r)
                    ve.need(tp)
                    r = ve.mark(vt.tensor_tensor(dst[:, 4 * g:4 * g + 4, t * 128:(t + 1) * 128],
                                                 s.ap.rearrange("p (k q) -> p k q", q=128),
                                                 bc(PT[:, gcol + 4 * g:gcol + 4 * g + 4], 128), ALU.mult))
                    s.free = [r]
                b.free = [tp, stored[t]]
                done.append(r)

            pipe(range(4), scale, turn, None, lambda t: use(t, done[t]))
            return done[-1]

        def proj(lT, t, nk, w, c0, n, ring, *tokens):
            s = ring.get()
            pe.need(*s.free, *tokens)
            for k in range(nk):
                r = mm(s.ap[:, 0:n], lT[:, k, t * 128:(t + 1) * 128], w[:, k, c0:c0 + n], k == 0, k == nk - 1)
            return s, pe.mark(r)

        ALLT = range(4)

        class HeadTurn:
            def __init__(self, scr, nh):
                self.sq = Ring([scr.take(nh * 64) for _ in range(2)])
                self.au = Ring([scr.take(nh, 66) for _ in range(2)])
                self.nh = nh
                self.sm = [small.take(nh) for _ in range(4)]

            def norm(self, ps, p0, tp, s, aug, atok):
                nh = self.nh
                q, u = self.sq.get(), self.au.get()
                ss, rs, m, y = self.sm
                ac.need(tp, *q.free)
                t1 = ac.mark(st.activation(q.ap, ps.ap[:, p0:p0 + nh * 64], ACT.Square))
                ve.need(t1)
                t2 = ve.mark(vt.reduce_sum(ss, q.ap.rearrange("p (h d) -> p h d", d=64), AX.X))
                q.free = [t2]
                tr = rstd(rs, ss, 64, (m, y), t2, s)
                ve.need(tr, *u.free)
                t3 = ve.mark(vt.tensor_tensor(u.ap[:, :, 0:64],
                                              ps.ap[:, p0:p0 + nh * 64].rearrange("p (h d) -> p h d", d=64),
                                              bc(rs, 64), ALU.mult))
                ps.free = [t3]
                ve.need(atok)
                for c, src in aug:
                    t3 = ve.mark(vt.tensor_copy(u.ap[:, :, 64 + c[0]:64 + c[1]], src))
                return u, t3

            def turn(self, u, tk, dst, t, gcol):
                pe.need(tk)
                for g in range(0, self.nh, 4):
                    n = min(4, self.nh - g)
                    s = TR.get()
                    pe.need(*s.free)
                    for j in range(n):
                        r = pt_.transpose(s.ap[0:66, j * 128:(j + 1) * 128], u.ap[:, g + j, :], ident)
                    tp = pe.mark(r)
                    ac.need(tp)
                    te = ac.mark(st.activation(dst[0:66, g:g + n, t * 128:(t + 1) * 128],
                                               s.ap[0:66, 0:n * 128].rearrange("p (h q) -> p h q", q=128),
                                               ACT.Copy, scale=PT[0:66, gcol:gcol + 1]))
                    s.free = [te]
                u.free = [tp]
                return te

        class Attend:
            def __init__(self, scr):
                self.P = Ring([scr.take(512) for _ in range(3)])
                self.PT = Ring([scr.take(512) for _ in range(3)])
                self.nm = Ring([small.take(8) for _ in range(4)])
                self.rs = Ring([small.take(8) for _ in range(4)])
                self.o, self.m, self.r = {}, {}, {}

            def run(self, *args):
                for _ in self.steps(*args):
                    pass

            def steps(self, qT, kT, V, kd, fin, toks):
                items = [dict(i=i, h=h) for pair in ((3, 0), (2, 1)) for h in range(8) for i in pair]

                def score(x):
                    i, h = x["i"], x["h"]
                    L = (i + 1) * 128
                    s = SR.get()
                    pe.need(*s.free, *toks)
                    mm(s.ap[:, 0:L], qT(h)[0:kd, i * 128:(i + 1) * 128], kT(h)[0:kd, 0:L], True, True)
                    tp = pe.mark(mm(s.ap[:, L - 128:L], identb[:, :], causb[:, :], False, True, True))
                    if h == 0:
                        self.m[i], self.r[i] = self.nm.get(), self.rs.get()
                    nm, rs = self.m[i], self.r[i]
                    ve.need(tp, *nm.free)
                    tm = ve.mark(vt.tensor_reduce(nm.ap[:, h:h + 1], s.ap[:, 0:L], AX.X, ALU.max, negate=True))
                    p = self.P.get()
                    ac.need(tm, *p.free, *rs.free)
                    x["e"] = ac.mark(st.activation(p.ap[:, 0:L], s.ap[:, 0:L], ACT.Exp, bias=nm.ap[:, h:h + 1],
                                                   accum_out=rs.ap[:, h:h + 1]))
                    s.free = [x["e"]]
                    x["p"], x["rs"], x["nm"] = p, rs, nm
                    if h == 7:
                        nm.free = [x["e"]]

                def turn(x):
                    i = x["i"]
                    L = (i + 1) * 128
                    s, p, q = TR.get(), x["p"], self.PT.get()
                    pe.need(x["e"], *s.free)
                    for j in range(i + 1):
                        r = pt_.transpose(s.ap[:, j * 128:(j + 1) * 128], p.ap[:, j * 128:(j + 1) * 128], ident)
                    tp = pe.mark(r)
                    p.free = [tp]
                    ve.need(tp, *q.free)
                    x["c"] = ve.mark(vt.tensor_copy(q.ap[:, 0:L], s.ap[:, 0:L]))
                    s.free = [x["c"]]
                    x["q"] = q

                def value(x):
                    i, h = x["i"], x["h"]
                    if h == 0:
                        self.o[i] = OR.get()
                        pe.need(*self.o[i].free)
                    pe.need(x["c"])
                    for j in range(i + 1):
                        r = mm(self.o[i].ap[:, h * 64:(h + 1) * 64], x["q"].ap[:, j * 128:(j + 1) * 128],
                               V(h, j), j == 0, j == i)
                    tp = pe.mark(r)
                    x["q"].free = [tp]
                    if h == 7:
                        self.o[i].free = [fin(i, self.o[i], tp, x["rs"], x["e"])]

                yield from steps(items, score, None, turn, value)

        def divide(dst, o, tp, rs, te, scr, gate=None):
            ri = scr
            ve.need(tp, te, ve.last)
            t = ve.mark(vt.reciprocal(ri, rs.ap))
            rs.free = [t]
            if gate is not None:
                ve.need(t)
                t = ve.mark(vt.tensor_tensor(ri, ri, gate, ALU.mult))
            ve.need(t)
            return ve.mark(vt.tensor_tensor(dst.rearrange("p (h d) -> p h d", d=64),
                                            o.ap.rearrange("p (h d) -> p h d", d=64), bc(ri, 64), ALU.mult))

        def turn4(src, dst, t, n, tok, gcol=None):
            s = TR.get()
            pe.need(tok, *s.free)
            for j in range(n):
                r = pt_.transpose(s.ap[:, j * 128:(j + 1) * 128], src[:, j * 128:(j + 1) * 128], ident)
            tp = pe.mark(r)
            if gcol is None:
                ac.need(tp)
                te = ac.mark(st.activation(dst[:, 0:n, t * 128:(t + 1) * 128],
                                           s.ap[:, 0:n * 128].rearrange("p (k q) -> p k q", q=128), ACT.Copy))
            else:
                ve.need(tp)
                for j in range(n):
                    te = ve.mark(vt.tensor_scalar(dst[:, j, t * 128:(t + 1) * 128], s.ap[:, j * 128:(j + 1) * 128],
                                                  PT[:, gcol + j:gcol + j + 1], None, ALU.mult))
            s.free = [te]
            return te, tp

        t_z = po.mark(gt.memset(AR[:, 20000:21024], 0.0))
        mq.copy(ys_dram[2048:NBLK * 128, :].rearrange("(b p) d -> p b d", p=128),
                AR[:, 20000:21024].unsqueeze(1).to_broadcast([128, NBLK - 16, 1024]), t_z)

        smark = small.at
        w = a["w_in"][0]
        ar = Place(AR, ARN)
        foxO = ar.take(4, 512)
        nsaO = ar.take(4, 512)
        base = ar.at
        qT = ar.take(8, 512)
        kT = ar.take(8, 512)
        fv = ar.take(4, 512)
        gates = small.take(4, 24)
        cum = small.take(4, 8)
        lf = small.take(4, 8)
        tmp8 = small.take(4, 8)
        off8 = small.take(8)
        s_v, w_v, t_wv = wload(wcols(w, 1024, 512), 8, 512)

        def fox_v(t, tok=None):
            ps, tp = proj(HT, t, 8, w_v, 0, 512, SR, t_wv, tok)
            ac.need(tp)
            ps.free = [ac.mark(st.copy(fv[:, t, :], ps.ap))]
            s_v.free = [tp]
            return ps.free[0]

        t_h = norm_turn(HT[:, :, :], 0, Place(AR, ARN, ar.at), lambda t: [t_x[t]],
                        lambda t, tok: fox_v(t, tok) if t < 2 else None)
        barrier()
        scr = Place(AR, ARN, ar.at)
        ht8 = HeadTurn(scr, 8)

        for t in ALLT:
            s, tp = proj(HT, t, 8, v0, 0, 32, SR, t_h, tw1, tw2)
            ve.need(tp)
            t1 = ve.mark(vt.tensor_tensor(lf[:, t, :], s.ap[:, 0:8], BR[:, 0:8], ALU.add))
            t2 = ve.mark(vt.tensor_copy(gates[:, t, :], s.ap[:, 8:32]))
            s.free = [t2]
        s0.free = [tp]
        ac.need(t1)
        t3 = ac.mark(st.activation(tmp8, lf, ACT.Abs))
        ac.need(t3)
        t3 = ac.mark(st.activation(tmp8, tmp8, ACT.Exp, scale=-1.0))
        ac.need(t3)
        t3 = ac.mark(st.activation(tmp8, tmp8, ACT.Ln, bias=1.0))
        ve.need(t3)
        t4 = ve.mark(vt.scalar_tensor_tensor(out=lf, in0=lf, scalar=0.0, in1=tmp8, op0=ALU.min, op1=ALU.subtract))
        ac.need(t2)
        t5 = ac.mark(st.activation(gates, gates, ACT.Exp, scale=-1.0))
        ve.need(t5)
        t5 = ve.mark(vt.tensor_scalar(gates, gates, 1.0, None, ALU.add))
        ve.need(t5)
        t_g = ve.mark(vt.reciprocal(gates, gates))
        fox_v(2)
        s = OR.get()
        pe.need(t4, *s.free)
        for t in ALLT:
            for j in range(t + 1):
                r = mm(s.ap[:, t * 8:t * 8 + 8], C["tri"] if j == t else C["ones"], lf[:, j, :], j == 0, j == t)
        tp = pe.mark(r)
        ve.need(tp)
        t_cum = ve.mark(vt.tensor_copy(cum, s.ap[:, 0:32].rearrange("p (t h) -> p t h", h=8)))
        s.free = [t_cum]
        ones48 = C["ones"][:, 0:8].unsqueeze(2)

        def heads(wv, tw, dst, aug, gcol, s_, atok):
            st8 = {}

            def p_(t):
                ps, tp = proj(HT, t, 8, wv, 0, 512, SR, tw)
                st8[t] = ht8.norm(ps, 0, tp, s_, aug(t), atok)
                st8["pe"] = tp

            def t_(t):
                st8["e"] = ht8.turn(*st8[t], dst, t, gcol)

            pipe(ALLT, p_, t_)
            return st8["e"], st8["pe"]

        sw, wv, tw = wload(wcols(w, 0, 512), 8, 512)
        t_q, tp = heads(wv, tw, qT, lambda t: [((0, 1), ones48), ((1, 2), cum[:, t, :].unsqueeze(2))], 60, 0.125, t_cum)
        sw.free = [tp]
        ncum = small.take(4, 8)
        ve.need(t_cum)
        t_nc = ve.mark(vt.tensor_scalar(ncum, cum, -1.0, None, ALU.mult))
        sw, wv, tw = wload(wcols(w, 512, 512), 8, 512)
        t_k, tp = heads(wv, tw, kT, lambda t: [((0, 1), ncum[:, t, :].unsqueeze(2)), ((1, 2), ones48)], 61, 1.0, t_nc)
        sw.free = [tp]
        t_v = fox_v(3)
        att = Attend(scr)
        ri8 = small.take(8)

        def fin(i, o, tp, rs, te):
            return divide(foxO[:, i, :], o, tp, rs, te, ri8)

        att.run(lambda h: qT[:, h, :], lambda h: kT[:, h, :], lambda h, j: fv[:, j, h * 64:(h + 1) * 64],
                66, fin, [t_q, t_k, t_v])
        barrier()

        ar.at = scr.at
        nq = qT
        kT2 = kT[:, 0:4, :]
        kcT = kT[:, 4, 0:64]
        kvT = kT[:, 5:7, :]
        vbd = kT[:, 7, :].rearrange("p (g n) -> p g n", n=256)
        vT2 = fv[:, :, 0:256]
        X2 = scr.take(4, 512)
        hidT = scr.take(4, 64)
        kcn = small.take(66)
        kcs = [small.take(1) for _ in range(4)]
        sw, wv, tw = wload(wcols(w, 1544, 512), 8, 512)
        t_q, tp = heads(wv, tw, nq, lambda t: [((0, 2), C["qaug"].rearrange("p (t h c) -> p t h c", h=8, c=2)[:, t])],
                        62, 0.125, t_c)
        sw.free = [tp]
        sv, wv, tw = wload(wcols(w, 2312, 512), 8, 512)
        ht2 = HeadTurn(scr, 2)
        ht2.au = Ring([scr.take(2, 66) for _ in range(4)])
        kvs = Ring([scr.take(256) for _ in range(2)])
        kaug = C["kaug"].rearrange("p (t c) -> p t c", c=2)
        st2 = {}

        def p_(t):
            ps, tp = proj(HT, t, 8, wv, 0, 512, SR, tw)
            kk2 = kvs.get()
            ac.need(tp, *kk2.free)
            for j in range(2):
                ac.mark(st.copy(vT2[:, t, j * 128:(j + 1) * 128], ps.ap[:, 256 * j + 128:256 * j + 256]))
            te = ac.mark(st.copy(kk2.ap.rearrange("p (j n) -> p j n", n=128),
                                 ps.ap.rearrange("p (j n) -> p j n", n=256)[:, :, 0:128]))
            ps.free = [te]
            aug = [((0, 2), mid(kaug[:, t, :], 2))]
            u0 = ht2.norm(kk2, 0, te, 1.0, aug, t_c)
            u1 = ht2.norm(kk2, 128, te, 1.0, aug, t_c)
            st2[t] = (u0, u1)
            st2["pe"], st2["v"] = tp, te

        def t_(t):
            for j in range(2):
                st2["e"] = ht2.turn(*st2[t][j], kT2[:, 2 * j:2 * j + 2, :], t, 63)

        pipe(ALLT, p_, t_)
        sv.free = [st2["pe"]]
        sw, wv, tw = wload(wcols(w, 2056, 256), 8, 256)
        pe.need(tw)
        for c in range(2):
            s = SR.get()
            pe.need(*s.free)
            for k in range(8):
                r = mm(s.ap, wv[:, k, c * 128:(c + 1) * 128], HT[:, k, :], k == 0, k == 7)
            tp = pe.mark(r)
            ac.need(tp)
            tk = ac.mark(st.copy(kvT[:, c, :], s.ap))
            s.free = [tk]
        sw.free = [tp]
        t_z = po.mark(gt.memset(X2[:, :, 511:512], 0.0))
        tx2 = []
        for c in range(2):
            for g in range(2):
                tx2.append(mq.copy(X2[0:64, 2 * c + g, :], kvT[64 * g:64 * g + 64, c, :], tk, t_z))
                tx2.append(mq.copy(X2[64:128, 2 * c + g, 0:511], kvT[64 * g:64 * g + 64, c, 1:512]))
        t_vz = po.mark(gt.memset(vbd, 0.0))
        t_hz = po.mark(gt.memset(hidT, 0.0))
        tmpo, tmpc = scr.take(512), scr.take(512)
        pc = Ring([scr.take(256) for _ in range(2)])
        pcT = Ring([scr.take(256) for _ in range(2)])
        last = {}

        hid = scr.take(256)
        win = [scr.take(16, 62) for _ in range(2)]

        def compressed():
            t_w = []
            for c in range(2):
                for g in range(2):
                    for h in range(2):
                        xw = X2[:, 2 * c + g, :].rearrange("p (n s two) -> p s n two", s=8, two=2)[:, :, h:h + 31, 0]
                        ve.need(*tx2)
                        o = 64 + 16 * c + 8 * h
                        t_w.append(ve.mark(vt.tensor_tensor(win[c][:, 8 * h:8 * h + 8, 31 * g:31 * g + 31], xw,
                                                            bc(PT[:, o:o + 8], 31), ALU.add)))
                yield 1
            th = None
            for c, nm_ in enumerate(("k", "v")):
                s1, w1, tw1 = wload(a[f"cmp_{nm_}_w1"][0].rearrange("(j p) n -> p j n", p=128), 16, 256)
                s2, w2, tw2 = wload(a[f"cmp_{nm_}_w2"][0].rearrange("(j p) n -> p j n", p=128), 2, 64)
                s = SR.get()
                pe.need(*s.free, tw1, tw2, *t_w)
                for j in range(16):
                    r = mm(s.ap[0:62, 0:256], win[c][:, j, :], w1[:, j, :], j == 0, j == 15)
                    if j == 7:
                        yield 1
                s1.free = [pe.mark(r)]
                ac.need(*s1.free, th)
                th = ac.mark(st.activation(hid[0:62, :], s.ap[0:62, 0:256], ACT.Gelu_apprx_tanh))
                s.free = [th]
                yield 1
                s = TR.get()
                pe.need(th, *s.free)
                for hf in range(2):
                    r = pt_.transpose(s.ap[:, 64 * hf:64 * hf + 62], hid[0:62, 128 * hf:128 * hf + 128],
                                      ident[0:62, 0:62])
                tp = pe.mark(r)
                ac.need(tp, t_hz)
                for hf in range(2):
                    th = ac.mark(st.copy(hidT[:, 2 * c + hf, :].rearrange("p (g n) -> p g n", n=32)[:, :, 0:31],
                                         s.ap[:, 64 * hf:64 * hf + 62].rearrange("p (g n) -> p g n", n=31)))
                s.free = [th]
                yield 1
                s = SR.get()
                pe.need(*s.free, th)
                if c == 0:
                    for hf in range(2):
                        r = mm(s.ap[0:64, 0:64], hidT[:, hf, :], w2[:, hf, :], hf == 0, hf == 1)
                    tp = pe.mark(r)
                    ac.need(tp)
                    t1 = ac.mark(st.activation(kcn[0:64, 0:64], s.ap[0:64, 0:64], ACT.Square,
                                               accum_out=kcs[0][0:64, :]))
                    t1 = rstd(kcs[1][0:64, :], kcs[0][0:64, :], 64, (kcs[2][0:64, :], kcs[3][0:64, :]), t1)
                    ve.need(t1)
                    t1 = ve.mark(vt.tensor_scalar(kcn[0:64, 0:64], s.ap[0:64, 0:64], kcs[1][0:64, :], None, ALU.mult))
                    t2 = ve.mark(vt.tensor_copy(kcn[0:64, 64:66], C["caug"][0:64, :]))
                    s.free = [t1]
                    yield 1
                    s = TR.get()
                    pe.need(t2, *s.free)
                    tp = pe.mark(pt_.transpose(s.ap[0:66, 0:64], kcn[0:64, :], ident[0:64, 0:64]))
                    ac.need(tp)
                    t_kc = ac.mark(st.activation(kcT[0:66, :], s.ap[0:66, 0:64], ACT.Copy, scale=PT[0:66, 63:64]))
                    s.free = [t_kc]
                else:
                    pe.need(t_vz)
                    for g in range(2):
                        for r4 in range(4):
                            for hf in range(2):
                                r = mm(s.ap[32 * r4:32 * r4 + 32, g * 64:g * 64 + 64],
                                       hidT[:, 2 + hf, g * 32:g * 32 + 32], w2[:, hf, :], hf == 0, hf == 1)
                    tp = pe.mark(r)
                    ve.need(tp, t_vz)
                    for g in range(2):
                        for r4 in range(4):
                            t_vc = ve.mark(vt.tensor_copy(vbd[32 * r4:32 * r4 + 32, g, 64 * r4:64 * r4 + 64],
                                                          s.ap[32 * r4:32 * r4 + 32, g * 64:g * 64 + 64]))
                    s.free = [t_vc]
                s2.free = [tp]
                yield 1

            ri8b = small.take(8)
            nm8, rs8 = small.take(8), small.take(8)
            anyg = small.take(8)
            cm = cmaskb[:, :].rearrange("p (t n) -> p t n", n=32)
            e_prev = tc3 = None
            for i in ALLT:
                s = SR.get()
                pe.need(*s.free, t_q, t_kc)
                mm(s.ap[:, 0:256], identb[:, :], mid(cm[:, i, :], 8), True, True)
                for h in range(8):
                    r = mm(s.ap[:, h * 32:h * 32 + 32], nq[0:66, h, i * 128:(i + 1) * 128],
                           kcT[0:66, (h // 4) * 32:(h // 4) * 32 + 32], False, True, True)
                tp = pe.mark(r)
                sv8 = s.ap[:, 0:256].rearrange("p (h n) -> p h n", n=32)
                ve.need(tp, e_prev)
                t1 = ve.mark(vt.tensor_reduce(nm8, sv8, AX.X, ALU.max, negate=True))
                p = pc.get()
                pv = p.ap[:, 0:256].rearrange("p (h n) -> p h n", n=32)
                ve.need(t1, *p.free)
                t1 = ve.mark(vt.tensor_tensor(pv, sv8, bc(nm8, 32), ALU.add))
                s.free = [t1]
                ac.need(t1)
                t2 = ac.mark(st.activation(p.ap[:, 0:256], p.ap[:, 0:256], ACT.Exp))
                ve.need(t2)
                t3 = ve.mark(vt.reduce_sum(rs8, pv, AX.X))
                ve.need(t3)
                t3 = ve.mark(vt.reciprocal(ri8b, rs8))
                ve.need(t3)
                t3 = ve.mark(vt.tensor_tensor(ri8b, ri8b, gates[:, i, :].rearrange("p (h c) -> p h c", c=3)[:, :, 0], ALU.mult))
                ve.need(t3)
                t3 = ve.mark(vt.tensor_scalar(ri8b, ri8b, C["anyv"][:, i:i + 1], None, ALU.mult))
                yield 1
                s = TR.get()
                pe.need(t2, *s.free)
                for g in range(2):
                    r = pt_.transpose(s.ap[:, g * 128:(g + 1) * 128], p.ap[:, g * 128:(g + 1) * 128], ident)
                tp = pe.mark(r)
                p.free = [tp, t3]
                q = pcT.get()
                ve.need(tp, *q.free)
                tc = ve.mark(vt.tensor_copy(q.ap[:, 0:256], s.ap[:, 0:256]))
                s.free = [tc]
                yield 1
                s = SR.get()
                pe.need(tc, t_vc, *s.free)
                for g in range(2):
                    r = mm(s.ap[:, g * 256:(g + 1) * 256], q.ap[:, g * 128:(g + 1) * 128], vbd[:, g, :], True, True)
                tp = pe.mark(r)
                q.free = [tp]
                ve.need(tp, t3, tc3)
                e_prev = ve.mark(vt.tensor_tensor(tmpc.rearrange("p (h d) -> p h d", d=64),
                                                  s.ap.rearrange("p (h d) -> p h d", d=64), bc(ri8b, 64), ALU.mult))
                s.free = [e_prev]
                ve.need(e_prev, last[i])
                last[i] = tc3 = ve.mark(vt.tensor_tensor(nsaO[:, i, :], nsaO[:, i, :], tmpc, ALU.add))
                yield 1

        def local(j):
            def fin2(i, o, tp, rs, te):
                g8 = gates[:, i, :].rearrange("p (h c) -> p h c", c=3)[:, :, 1 + j]
                if j == 0:
                    last[i] = divide(nsaO[:, i, :], o, tp, rs, te, ri8, g8)
                    return last[i]
                ve.need(za_["t"])
                t = divide(tmpo, o, tp, rs, te, ri8, g8)
                ve.need(t, last[i])
                last[i] = za_["t"] = ve.mark(vt.tensor_tensor(nsaO[:, i, :], nsaO[:, i, :], tmpo, ALU.add))
                return t

            za_ = {"t": None}
            return att.steps(lambda h: nq[:, h, :], lambda h: kT2[:, 2 * j + h // 4, :],
                             lambda h, jt: vT2[:, jt, j * 128 + (h // 4) * 64:j * 128 + (h // 4) * 64 + 64],
                             66, fin2, [t_q, st2["e"], st2["v"]])

        def both():
            yield from local(0)
            yield from local(1)

        def after(n, g):
            for _ in range(n):
                yield 1
            yield from g

        weave(both(), after(40, compressed()))
        barrier()

        def merge(lT, w_in, c_a, outs, oTs, mix, mixT, scr, bias=None):
            sg = Ring([scr.take(512) for _ in range(3)])
            tb = Ring([scr.take(512) for _ in range(2)])
            items = []
            for c in range(2):
                for b in range(2):
                    for t in ALLT:
                        items.append((c, b, t))
            cur = {}

            def go(x):
                c, b, t = x
                if t == 0:
                    cur["g"] = wload(wcols(w_in, c_a + 1024 * b + 512 * c, 512), 8, 512)
                    cur["u"] = wload(outs[b][:, 512 * c:512 * c + 512].rearrange("(k p) n -> p k n", p=128), 4, 512)
                sg_, gv, tg = cur["g"]
                su_, uv, tu = cur["u"]
                ps, tp = proj(lT, t, 8, gv, 0, 512, SR, tg)
                z = sg.get()
                if bias is not None:
                    ve.need(tp, *z.free)
                    tz = ve.mark(vt.tensor_tensor(z.ap, ps.ap, bias[:, 1024 * b + 512 * c:1024 * b + 512 * c + 512],
                                                  ALU.add))
                    ps.free = [tz]
                    ac.need(tz)
                    tz = ac.mark(st.activation(z.ap, z.ap, ACT.Sigmoid))
                else:
                    ac.need(tp, *z.free)
                    tz = ac.mark(st.activation(z.ap, ps.ap, ACT.Sigmoid))
                    ps.free = [tz]
                pu, tp2 = proj(oTs[b], t, 4, uv, 0, 512, OR, tu)
                ve.need(tp2, tz)
                m = mix[:, t, c * 512:(c + 1) * 512]
                if b == 0:
                    tm = ve.mark(vt.tensor_tensor(m, pu.ap, z.ap, ALU.mult))
                    pu.free = [tm]
                    z.free = [tm]
                    cur[(c, t)] = tm
                else:
                    y = tb.get()
                    ve.need(*y.free)
                    tm = ve.mark(vt.tensor_tensor(y.ap, pu.ap, z.ap, ALU.mult))
                    pu.free = [tm]
                    z.free = [tm]
                    ve.need(tm, cur[(c, t)])
                    tm = ve.mark(vt.tensor_tensor(m, m, y.ap, ALU.add))
                    y.free = [tm]
                    cur[(c, t)] = tm
                if t == 3:
                    sg_.free = [tp]
                    su_.free = [tp2]

            def tn(x):
                c, b, t = x
                if b == 1:
                    cur["t"], _ = turn4(mix[:, t, c * 512:(c + 1) * 512], mixT[:, 4 * c:4 * c + 4, :], t, 4, cur[(c, t)])

            pipe(items, go, tn)
            return cur["t"]

        ar = Place(AR, ARN, base)
        mix = ar.take(4, 1024)
        mixT = ar.take(8, 512)
        foT = ar.take(4, 512)
        noT = ar.take(4, 512)
        scr = Place(AR, ARN, ar.at)
        for t in ALLT:
            turn4(foxO[:, t, :], foT, t, 4, None)
            te, _ = turn4(nsaO[:, t, :], noT, t, 4, None)
        pe.need(te)
        tm = merge(HT, w, 2848, [a["w_fox_up"][0], a["w_nsa_up"][0]], [foT, noT], mix, mixT, scr)
        def w_out(t):
            ps, tp = proj(mixT, t, 8, wo_[1], 0, 512, SR, wo_[2], tm)
            ve.need(tp)
            xs = X[:, t, c * 512:(c + 1) * 512]
            tx = ve.mark(vt.tensor_tensor(xs, ps.ap, xs, ALU.add))
            ps.free = [tx]
            wo_[0].free = [tp]
            return [tx]

        c, wo_ = 0, wload(wcols(a["w_out"][0], 0, 512), 8, 512)
        for t in ALLT:
            w_out(t)
        s0 = WR.get()
        v0 = s0.ap[:, 0:160].rearrange("p (k n) -> p k n", n=20)
        tw1 = wq.copy(v0[:, :, 0:4], a["w_group"][0].rearrange("(k p) n -> p k n", p=128), *s0.free)
        tw2 = wq.copy(v0[:, :, 4:20], a["w_router"][0].rearrange("(k p) n -> p k n", p=128))
        c, wo_ = 1, wload(wcols(a["w_out"][0], 512, 512), 8, 512)

        ar = Place(AR, ARN)
        small.at = smark
        lg = small.take(4, 20)

        def logits(t, tok):
            s, tp = proj(HT, t, 8, v0, 0, 20, SR, tok, tw1, tw2)
            ve.need(tp)
            s.free = [ve.mark(vt.tensor_tensor(lg[:, t, :], s.ap[:, 0:20], BR[:, 8:28], ALU.add))]
            s0.free = [tp]

        norm_turn(HT[:, :, :], 8, Place(AR, ARN, 23000), w_out, logits, xs_dram)
        t_clear = [e.last for e in (pe, ve, ac, po)]
        po.need(*t_clear)
        ve.need(*t_clear)
        ac.need(*t_clear)

        def vop(f, *tokens):
            ve.need(ve.last, *tokens)
            return ve.mark(f())

        m1 = small.take(4)
        g1 = small.take(4, 4)
        oh = small.take(4, 4)
        pg = small.take(4)
        e4 = mid(C["e4"], 4)

        def first_max(dst, src, mx, scr4, sc1):
            vop(lambda: vt.reduce_max(mx, src, AX.X))
            vop(lambda: vt.tensor_tensor(scr4, src, bc(mx, 4), ALU.is_ge))
            vop(lambda: vt.tensor_scalar(scr4, scr4, -100.0, 100.0, ALU.mult, ALU.add))
            vop(lambda: vt.tensor_tensor(scr4, scr4, e4, ALU.add))
            vop(lambda: vt.tensor_reduce(sc1, scr4, AX.X, ALU.min))
            return vop(lambda: vt.tensor_tensor(dst, e4, bc(sc1, 4), ALU.is_equal))

        f4, f1 = small.take(4, 4), small.take(4)
        gl = lg[:, :, 0:4]
        first_max(oh, gl, m1, f4, f1)
        t1 = vop(lambda: vt.tensor_tensor(g1, gl, bc(m1, 4), ALU.subtract))
        ac.need(t1)
        t1 = ac.mark(st.activation(g1, g1, ACT.Exp))
        vop(lambda: vt.reduce_sum(pg, g1, AX.X), t1)
        vop(lambda: vt.reciprocal(pg, pg))
        em = small.take(4, 4, 4)
        ein = small.take(4, 4)
        elg = lg[:, :, 4:20]
        for g in range(4):
            vop(lambda: vt.tensor_tensor(em[:, :, g, :], elg[:, :, 4 * g:4 * g + 4], bc(oh[:, :, g], 4), ALU.mult))
        vop(lambda: vt.reduce_sum(ein, em.rearrange("p t g j -> p t j g"), AX.X))
        vop(lambda: vt.reduce_max(m1, ein, AX.X))
        t1 = vop(lambda: vt.tensor_tensor(ein, ein, bc(m1, 4), ALU.subtract))
        ac.need(t1)
        t1 = ac.mark(st.activation(ein, ein, ACT.Exp))
        ve.need(t1)
        o1, o2, e2 = small.take(4, 4), small.take(4, 4), small.take(4, 4)
        p1, p2, ps_ = small.take(4), small.take(4), small.take(4)
        first_max(o1, ein, p1, f4, f1)
        vop(lambda: vt.tensor_scalar(e2, o1, -2.0, None, ALU.mult))
        vop(lambda: vt.tensor_tensor(e2, ein, e2, ALU.add))
        first_max(o2, e2, p2, f4, f1)
        vop(lambda: vt.tensor_tensor(ps_, p1, p2, ALU.add))
        vop(lambda: vt.reciprocal(ps_, ps_))
        vop(lambda: vt.tensor_tensor(ps_, ps_, pg, ALU.mult))
        vop(lambda: vt.tensor_tensor(p1, p1, ps_, ALU.mult))
        vop(lambda: vt.tensor_tensor(p2, p2, ps_, ALU.mult))
        M1, M2, MM = (small.take(4, 16) for _ in range(3))
        for g in range(4):
            vop(lambda: vt.tensor_tensor(M1[:, :, 4 * g:4 * g + 4], o1, bc(oh[:, :, g], 4), ALU.mult))
            vop(lambda: vt.tensor_tensor(M2[:, :, 4 * g:4 * g + 4], o2, bc(oh[:, :, g], 4), ALU.mult))
        t1 = vop(lambda: vt.tensor_tensor(MM, M1, M2, ALU.add))
        s = OR.get()
        pe.need(t1, *s.free)
        for t in ALLT:
            for j in range(t + 1):
                mm(s.ap[:, 16 * t:16 * t + 16], C["stri"] if j == t else C["ones"], MM[:, j, :], j == 0, j == t)
        for j in ALLT:
            r = mm(s.ap[:, 64:80], C["ones"], MM[:, j, :], j == 0, j == 3)
        tp = pe.mark(r)
        PO, CN = small.take(4, 16), small.take(16)
        vop(lambda: vt.tensor_copy(PO, s.ap[:, 0:64].rearrange("p (t e) -> p t e", e=16)), tp)
        t1 = vop(lambda: vt.tensor_copy(CN, s.ap[:, 64:80]))
        s.free = [t1]
        nov, ovi, ovb, ones16 = small.take(16), small.take(16), small.take(16), C["ones"][:, 0:16]
        vop(lambda: vt.tensor_scalar(nov, CN, 128.0, None, ALU.is_gt))
        for c in (256.0, 384.0):
            vop(lambda: vt.scalar_tensor_tensor(out=nov, in0=CN, scalar=c, in1=nov, op0=ALU.is_gt, op1=ALU.add))
        vop(lambda: vt.tensor_tensor_scan(ovi, ones16, nov, 0.0, ALU.mult, ALU.add))
        vop(lambda: vt.tensor_tensor(ovb, ovi, nov, ALU.subtract))
        e7 = small.take(7, 16)
        ctl = small.take(8)
        vop(lambda: vt.tensor_tensor(e7, mid(ovi, 7), C["b7"].rearrange("p (b e) -> p b e", e=16), ALU.is_le))
        vop(lambda: vt.reduce_sum(ctl[:, 1:8], e7, AX.X))
        vop(lambda: vt.tensor_scalar(ctl[:, 1:8], ctl[:, 1:8], 15.0, None, ALU.min))
        vop(lambda: vt.tensor_copy(ctl[:, 0:1], ovi[:, 15:16]))
        ctli = small.take(8).bitcast(I32)
        t_ctl = vop(lambda: vt.tensor_copy(ctli, ctl))
        q_, F_, BK = (small.take(4, 16) for _ in range(3))
        vop(lambda: vt.tensor_scalar(F_, PO, 128.0, None, ALU.is_ge))
        vop(lambda: vt.scalar_tensor_tensor(out=q_, in0=PO, scalar=256.0, in1=F_, op0=ALU.is_ge, op1=ALU.add))
        vop(lambda: vt.scalar_tensor_tensor(out=q_, in0=PO, scalar=384.0, in1=q_, op0=ALU.is_ge, op1=ALU.add))
        vop(lambda: vt.tensor_tensor(ovb, ovb, C["e16"], ALU.subtract))
        vop(lambda: vt.tensor_scalar(ovb, ovb, 15.0, None, ALU.add))
        vop(lambda: vt.tensor_tensor(BK, F_, mid(ovb, 4), ALU.mult))
        vop(lambda: vt.tensor_tensor(BK, BK, mid(C["e16"], 4), ALU.add))
        vop(lambda: vt.tensor_tensor(BK, BK, q_, ALU.add))
        vop(lambda: vt.scalar_tensor_tensor(out=PO, in0=q_, scalar=-128.0, in1=PO, op0=ALU.mult, op1=ALU.add))
        pb = small.take(4, 4)
        for j, (R_, M_) in enumerate(((PO, M1), (PO, M2), (BK, M1), (BK, M2))):
            vop(lambda: vt.tensor_tensor(MM, R_, M_, ALU.mult))
            t1 = vop(lambda: vt.reduce_sum(pb[:, j, :], MM, AX.X))
        op_ = Place(AR, ARN, 25200)
        ohp, ohb = op_.take(8, 128), op_.take(8, NBLK)
        s = OR.get()
        pe.need(*s.free)
        ve.need(t1)
        for j in range(2):
            for t in ALLT:
                i = 4 * j + t
                ve.mark(vt.tensor_scalar(ohb[:, i, :], C["io"][:, 0:NBLK], pb[:, 2 + j, t:t + 1], kaug[:, t, 0:1],
                                         ALU.is_equal, ALU.mult))
                t2 = ve.mark(vt.tensor_scalar(ohp[:, i, :], C["io"], pb[:, j, t:t + 1], None, ALU.is_equal))
                pe.need(t2)
                r = mm(s.ap[:, 0:NBLK], ohp[:, i, :], ohb[:, i, :], i == 0, i == 7)
        tp = pe.mark(r)
        slots = small.take(NBLK).bitcast(U32)
        t_sl = vop(lambda: vt.tensor_copy(slots, s.ap[:, 0:NBLK]), tp)
        s.free = [t_sl]
        rowf = small.take(2, 4)
        rowi = small.take(8).bitcast(U32).rearrange("p (j t) -> p j t", t=4)
        vop(lambda: vt.scalar_tensor_tensor(out=rowf, in0=pb[:, 2:4, :], scalar=128.0, in1=pb[:, 0:2, :],
                                            op0=ALU.mult, op1=ALU.add))
        vop(lambda: vt.tensor_copy(rowi, rowf))

        barrier()
        EW = Ring([])
        EW.slots = WR.slots + [Slot(ar.take(4096)) for _ in range(3)]
        EW.n = WR.n % NW
        order = [(WR.n + i) % NW for i in range(NW)]
        EW.slots = [WR.slots[i] for i in order] + EW.slots[NW:]
        EW.n = 0
        Gr = Ring([ar.take(1024) for _ in range(3)])
        XTr = Ring([ar.take(8, 128) for _ in range(2)])
        Yr = Ring([ar.take(1024) for _ in range(2)])
        sil = Ring([ar.take(512) for _ in range(2)])
        hb = Ring([ar.take(512) for _ in range(2)])
        hTr = Ring([ar.take(4, 128) for _ in range(2)])
        for r_ in EW.slots[NW:]:
            r_.free = list(t_clear)

        def eload(src, k, n):
            s = EW.get()
            v = s.ap[:, 0:k * n].rearrange("p (k n) -> p k n", n=n)
            tok = wq.copy(v, src.rearrange("(k p) n -> p k n", p=128), *s.free)
            s.free = []
            return s, v, tok

        bst, ty = {}, []

        def expert(name, b, ev):
            return a[name][0, b] if ev is None else a[name][0][bass.ds(ev[b - 16], 1)].rearrange("a k n -> (a k) n")

        def fetch(x):
            b, ev = x
            g = Gr.get()
            bst[b] = [g, (mq if ev is None else xq).gather(g.ap, xs_dram, slots[:, b:b + 1], t_sl, *g.free)]

        def q_mm(o, l, r, start, stop):
            f = lambda: pt_.matmul(o, l, r, start=start, stop=stop)
            return pe.later(f) if stop else pe.run(f)

        def q_turn(o, i, last):
            f = lambda: pt_.transpose(o, i, ident)
            return pe.later(f) if last else pe.run(f)

        def q_mult(o, x, y):
            return ve.later(lambda: vt.tensor_tensor(o, x, y, ALU.mult))

        def q_act(o, x, func):
            return ac.later(lambda: st.activation(o, x, func))

        def turn_x(x):
            b, ev = x
            g, tg = bst[b]
            xt_ = XTr.get()
            for hf in range(2):
                s = TR.get()
                pe.need(tg, *s.free)
                for j in range(4):
                    k = 4 * hf + j
                    tp = q_turn(s.ap[:, j * 128:(j + 1) * 128], g.ap[:, k * 128:(k + 1) * 128], j == 3)
                ve.need(tp, *xt_.free)
                te = q_mult(xt_.ap[:, 4 * hf:4 * hf + 4, :], s.ap.rearrange("p (k q) -> p k q", q=128),
                            bc(PT[:, 8 + 4 * hf:12 + 4 * hf], 128))
                s.free = [te]
            g.free = [tp]
            bst[b] = [xt_, te]

        def gate_up(x):
            b, ev = x
            xt_, te = bst[b]
            pss = []
            for name in ("w_gate", "w_up"):
                sl, wv_, tw_ = eload(expert(name, b, ev), 8, 512)
                s = SR.get()
                pe.need(*s.free, tw_, te)
                for k in range(8):
                    tp = q_mm(s.ap, xt_.ap[:, k, :], wv_[:, k, :], k == 0, k == 7)
                pss.append((s, tp))
                sl.free = [pe.last]
            (s1, tp1), (s2, tp2) = pss
            xt_.free = [tp2]
            z, h = sil.get(), hb.get()
            ac.need(tp1, *z.free)
            tz = q_act(z.ap, s1.ap, ACT.Silu)
            s1.free = [tz]
            ve.need(tz, tp2, *h.free)
            th = q_mult(h.ap, s2.ap, z.ap)
            s2.free = [th]
            z.free = [th]
            bst[b] = [h, th]

        def down(x):
            b, ev = x
            h, th = bst[b]
            s = TR.get()
            ht_, y = hTr.get(), Yr.get()
            pe.need(th, *s.free)
            for j in range(4):
                tp = q_turn(s.ap[:, j * 128:(j + 1) * 128], h.ap[:, j * 128:(j + 1) * 128], j == 3)
            h.free = [tp]
            ac.need(tp, *ht_.free)
            te = q_act(ht_.ap, s.ap.rearrange("p (k q) -> p k q", q=128), ACT.Copy)
            s.free = [te]
            sl, wv_, tw_ = eload(expert("w_down", b, ev), 4, 1024)
            for c in range(2):
                s = OR.get()
                pe.need(*s.free, tw_, te)
                for f in range(4):
                    tp = q_mm(s.ap, ht_.ap[:, f, :], wv_[:, f, c * 512:(c + 1) * 512], f == 0, f == 3)
                ac.need(tp, *y.free)
                tc = q_act(y.ap[:, c * 512:(c + 1) * 512], s.ap, ACT.Copy)
                s.free = [tc]
            ht_.free = [tp]
            sl.free = [tp]
            y.free = [(mq if ev is None else xq).copy(ys_dram[b * 128:(b + 1) * 128, :], y.ap, tc)]

        pipe([(b, None) for b in range(16)], fetch, turn_x, gate_up, down)

        barrier()
        sy.need(*[e.last for e in (pe, ve, ac, po)], *mq.outstanding())
        engs = (pe, ve, ac, po, sy)
        for e in engs:
            e.need(t_ctl)
        before = [(e, e.n, dict(e.seen)) for e in engs]
        wbefore = wq.n
        vals = {}
        for e in engs:
            vals[e] = e.eng.value_load(ctli[0:1, 0:1], min_val=0, max_val=7)
        ev = [sy.eng.value_load(ctli[0:1, 1 + b:2 + b], min_val=0, max_val=15) for b in range(7)]
        for e in engs:
            e.queue = []
        pipe([(b, ev) for b in range(16, NBLK)], fetch, turn_x, gate_up, down)
        po.need(*xq.outstanding())
        po.later(lambda: gt.memset(ctl, 0.0))
        for e, n, seen in before:
            todo, e.queue = e.queue, None
            with e.eng.If(vals[e] > 0):
                for f in todo:
                    f()
            with e.eng.Else():
                if e is not sy:
                    e.skip(n)
                else:
                    wq.skip(wbefore)
            e.seen = seen
        barrier()
        g2 = [[ar.t[:, 4096 + 1024 * (2 * t + j):5120 + 1024 * (2 * t + j)] for j in range(2)] for t in ALLT]
        t_g2 = [[mq.gather(g2[t][j], ys_dram, rowi[:, j, t:t + 1]) for j in range(2)] for t in ALLT]
        WR.slots = [WR.slots[i] for i in order]
        WR.n = 0
        xv = xs_dram.rearrange("(t p) d -> p t d", p=128)

        def add_rows(t):
            for j, pw in ((0, p1), (1, p2)):
                r = vop(lambda: vt.scalar_tensor_tensor(out=X[:, t, :], in0=g2[t][j], scalar=pw[:, t:t + 1],
                                                        in1=X[:, t, :], op0=ALU.mult, op1=ALU.add), t_g2[t][j])
            return [r]

        w = a["w_in_2"]
        ar = Place(AR, ARN)
        oA = ar.take(4, 512)
        oB = ar.take(4, 512)
        base = ar.at

        qT = ar.take(8, 512)
        kT = ar.take(8, 512)
        fv = ar.take(4, 512)
        cT = ar.take(3, 512)
        cosb = ar.take(4, 16)
        sinb = ar.take(4, 16)
        scr = Place(AR, ARN, ar.at)
        posr = scr.take(4).bitcast(I32)
        posf = scr.take(4)
        tpi = mq.copy(posr, a["positions_2"][0].rearrange("(t p) -> p t", p=128), allow_slow_non_contiguous=True)
        ang, kk_, rr = scr.take(4, 16), scr.take(4, 16), scr.take(4, 16)
        sw, wv, tw = wload(wcols(w, 2176, 416), 8, 416)
        cb = scr.take(4, 416)
        sqb = scr.take(256)
        ss8, mm8, yy8, rr8 = (small_c.take(2, 4) for _ in range(4))

        def latent(t, tok):
            ps, tp = proj(HT, t, 8, wv, 0, 416, SR, tw, tok)
            ac.need(tp)
            t1 = ac.mark(st.copy(cb[:, t, :], ps.ap[:, 0:416]))
            ps.free = [t1]
            for k_, (n, o) in enumerate(((256, 0), (128, 256))):
                ac.need(t1)
                t1 = ac.mark(st.activation(sqb[:, 0:n], cb[:, t, o:o + n], ACT.Square, accum_out=ss8[:, k_, t:t + 1]))
            sw.free = [tp]

        norm_turn(HT[:, :, :], 16, Place(AR, ARN, 20000), add_rows, latent)
        small.at = smark
        barrier()
        mq.copy(xv, X[:, :, :])
        tkp = t1 = ac.last
        vop(lambda: vt.tensor_scalar(ss8[:, 1, :], ss8[:, 1, :], 2.0, None, ALU.mult), t1)
        tr = rstd(rr8, ss8, 256, (mm8, yy8), ve.last)

        def cscale(t):
            ve.need(tr)
            for k_, (n, o) in enumerate(((256, 0), (128, 256))):
                tcs[t] = ve.mark(vt.tensor_scalar(cb[:, t, o:o + n], cb[:, t, o:o + n], rr8[:, k_, t:t + 1], None,
                                                  ALU.mult))

        tcs = {}

        def cturn(t):
            tcs["e"], _ = turn4(cb[:, t, :], cT, t, 3, tcs[t], 57)

        pipe(ALLT, cscale, cturn)
        tcT = tcs["e"]
        vop(lambda: vt.tensor_copy(posf, posr), tpi)
        for t in ALLT:
            vop(lambda: vt.tensor_scalar(ang[:, t, :], C["invf"], posf[:, t:t + 1], None, ALU.mult))
        MAGIC = 12582912.0
        c1 = float(np.float32(6.28125))
        c2 = float(np.float32(TWO_PI - 6.28125))
        c3 = float(np.float32(TWO_PI - 6.28125 - float(np.float32(TWO_PI - 6.28125))))
        hp = float(np.float32(np.pi / 2))
        PIF = 3.1415925
        for dst, q0, ph in ((sinb, 0.0, 0.0), (cosb, 0.25, hp)):
            vop(lambda: vt.tensor_scalar(kk_, ang, float(1.0 / TWO_PI), q0, ALU.mult, ALU.add))
            vop(lambda: vt.tensor_scalar(kk_, kk_, MAGIC, None, ALU.add))
            vop(lambda: vt.tensor_scalar(kk_, kk_, -MAGIC, None, ALU.add))
            vop(lambda: vt.scalar_tensor_tensor(out=rr, in0=kk_, scalar=-c1, in1=ang, op0=ALU.mult, op1=ALU.add))
            vop(lambda: vt.scalar_tensor_tensor(out=rr, in0=kk_, scalar=-c2, in1=rr, op0=ALU.mult, op1=ALU.add))
            vop(lambda: vt.scalar_tensor_tensor(out=rr, in0=kk_, scalar=-c3, in1=rr, op0=ALU.mult, op1=ALU.add))
            vop(lambda: vt.tensor_scalar(rr, rr, ph, PIF, ALU.add, ALU.min))
            t1 = vop(lambda: vt.tensor_scalar(rr, rr, -PIF, None, ALU.max))
            ac.need(t1)
            t1 = ac.mark(st.activation(dst, rr, ACT.Sin))
            ve.need(t1)
        ra = Ring([scr.take(8, 32) for _ in range(2)])

        def rope(dst, src, t, nh, scr_, tok):
            c, s = mid(cosb[:, t, :], nh), mid(sinb[:, t, :], nh)
            u = scr_
            ve.need(tok)
            ve.mark(vt.tensor_tensor(u[:, 0:nh, 0:16], src[:, :, 16:32], s, ALU.mult))
            t1 = ve.mark(vt.tensor_tensor(u[:, 0:nh, 16:32], src[:, :, 0:16], s, ALU.mult))
            ve.mark(vt.tensor_tensor(dst[:, :, 0:16], src[:, :, 0:16], c, ALU.mult))
            t2 = ve.mark(vt.tensor_tensor(dst[:, :, 16:32], src[:, :, 16:32], c, ALU.mult))
            ve.need(t1, t2)
            ve.mark(vt.tensor_tensor(dst[:, :, 0:16], dst[:, :, 0:16], u[:, 0:nh, 0:16], ALU.subtract))
            return ve.mark(vt.tensor_tensor(dst[:, :, 16:32], dst[:, :, 16:32], u[:, 0:nh, 16:32], ALU.add))

        kpr = scr.take(4, 32)
        for t in ALLT:
            tkr = rope(kpr[:, t:t + 1, :], cb[:, t:t + 1, 384:416], t, 1, ra.get().ap, tkp)
            ve.need(tkr)
        s1, wq_, tw1 = wload(a["w_uq_2"].rearrange("(k p) n -> p k n", p=128), 2, 768)
        s2, wk_, tw2 = wload(a["w_ukv_2"].rearrange("(k p) n -> p k n", p=128), 1, 1024)
        qb = Ring([scr.take(8, 96) for _ in range(4)])
        msc = 1.0 / float(np.sqrt(96.0))
        qp = scr.take(8, 32)
        stm = {}

        def turn_h(u, tk, dst, t):
            pe.need(tk)
            for g in range(2):
                s = TR.get()
                pe.need(*s.free)
                for j in range(4):
                    r = pt_.transpose(s.ap[0:96, j * 128:(j + 1) * 128], u.ap[:, 4 * g + j, :], ident)
                tp = pe.mark(r)
                ac.need(tp)
                te = ac.mark(st.activation(dst[0:96, 4 * g:4 * g + 4, t * 128:(t + 1) * 128],
                                           s.ap[0:96, :].rearrange("p (h q) -> p h q", q=128), ACT.Copy))
                s.free = [te]
            u.free = [tp]
            return te

        def mq_(t):
            u = qb.get()
            ve.need(*u.free)
            qt = {}
            for hf in range(2):
                ps, tp = proj(cT, t, 2, wq_, 384 * hf, 384, SR, tw1, tcT)
                v = ps.ap[:, 0:384].rearrange("p (h d) -> p h d", d=96)
                ve.need(tp)
                t1 = ve.mark(vt.tensor_scalar(u.ap[:, 4 * hf:4 * hf + 4, 0:64], v[:, :, 0:64], msc, None, ALU.mult))
                t2 = ve.mark(vt.tensor_scalar(qp[:, 4 * hf:4 * hf + 4, :], v[:, :, 64:96], msc, None, ALU.mult))
                ps.free = [t2]
            t3 = rope(u.ap[:, :, 64:96], qp, t, 8, ra.get().ap, t2)
            stm[("q", t)] = (u, t3)
            stm["pe"] = tp

        def mk_(t):
            u = qb.get()
            ve.need(*u.free)
            for hf in range(2):
                s = SR.get()
                pe.need(*s.free, tw2, tcT)
                tp = pe.mark(mm(s.ap, cT[:, 2, t * 128:(t + 1) * 128], wk_[:, 0, 512 * hf:512 * hf + 512], True, True))
                v = s.ap.rearrange("p (h d) -> p h d", d=128)
                ve.need(tp)
                t1 = ve.mark(vt.tensor_copy(u.ap[:, 4 * hf:4 * hf + 4, 0:64], v[:, :, 0:64]))
                ac.need(tp, t1)
                t2 = ac.mark(st.copy(fv[:, t, 256 * hf:256 * hf + 256].rearrange("p (h d) -> p h d", d=64),
                                     v[:, :, 64:128]))
                s.free = [t2]
            t3 = ve.mark(vt.tensor_copy(u.ap[:, :, 64:96], mid(kpr[:, t, :], 8)))
            stm[("k", t)] = (u, t3)
            stm["pe"], stm["v"] = tp, t2

        def tq_(t):
            turn_h(*stm[("q", t)], qT, t)
            stm["e"] = turn_h(*stm[("k", t)], kT, t)

        pipe(ALLT, lambda t: (mq_(t), mk_(t)), tq_)
        s1.free = [stm["pe"]]
        s2.free = [stm["pe"]]
        att = Attend(scr)
        ri8 = small.take(8)

        def fin3(i, o, tp, rs, te):
            return divide(oB[:, i, :], o, tp, rs, te, ri8)

        att.run(lambda h: qT[:, h, :], lambda h: kT[:, h, :], lambda h, j: fv[:, j, h * 64:(h + 1) * 64],
                96, fin3, [stm["e"], stm["v"]])
        barrier()

        ar = Place(AR, ARN, base)
        rT, kaT, vT, cumT, aT, beT, alT = (ar.take(4, 512) for _ in range(7))
        oBT = ar.take(4, 512)
        wa = ar.take(512)
        mis_at = ar.at
        raw = Ring([ar.take(513) for _ in range(2)])
        dif = Ring([ar.take(512) for _ in range(2)])
        bufs = Ring([ar.take(512) for _ in range(2)])
        dia = ar.take(4, 8)
        tail = Place(AR, ARN, ar.at)
        nrm = tail.take(3, 512)
        res = tail.take(512)
        scs = Ring([tail.take(512) for _ in range(2)])
        for r_ in raw.slots:
            r_.free = [po.mark(gt.memset(r_.ap[:, 0:1], 0.0))]
        po.need(po.mark(gt.memset(res, 1.0)))
        t_res = po.mark(gt.memset(res.rearrange("p (c q) -> p c q", q=128)[:, :, 0:1], 0.0))

        def feature(wv, c0, n, dst, tw):
            s = SR.get()
            pe.need(*s.free, tw)
            for k in range(8):
                r = mm(s.ap, wv[:, k, c0:c0 + 128], HT[:, k, :], k == 0, k == 7)
            tp = pe.mark(r)
            b, d = raw.get(), dif.get()
            ac.need(tp, *b.free)
            t1 = ac.mark(st.copy(b.ap[:, 1:513], s.ap))
            s.free = [t1]
            ve.need(t1, *d.free, *b.free)
            t2 = ve.mark(vt.tensor_tensor(d.ap, b.ap[:, 0:512], b.ap[:, 1:513], ALU.subtract))
            ve.need(t2)
            t3 = ve.mark(vt.scalar_tensor_tensor(out=dst, in0=d.ap, scalar=PT[:, 24 + n:25 + n], in1=b.ap[:, 1:513],
                                                 op0=ALU.mult, op1=ALU.add))
            b.free, d.free = [t3], [t3]
            return t3, tp

        sw, wv, tw = wload(wcols(w, 2592, 512), 8, 512)
        for t in ALLT:
            ps, tp = proj(HT, t, 8, wv, 0, 512, SR, tw)
            b = scs.get()
            ac.need(tp, *b.free)
            t1 = ac.mark(st.activation(b.ap, ps.ap, ACT.Silu))
            ps.free = [t1]
            ve.need(t1)
            t1 = ve.mark(vt.tensor_tensor(oB[:, t, :], oB[:, t, :], b.ap, ALU.mult))
            b.free = [t1]
        sw.free = [tp]
        t_ob = t1

        sw, wv, tw = wload(wcols(w, 1536, 128), 8, 128)
        t_f, tp = feature(wv, 0, 12, wa, tw)
        sw.free = [tp]
        for t in ALLT:
            t_obt, _ = turn4(oB[:, t, :], oBT, t, 4, t_ob)
        s1 = WR.get()
        wl = s1.ap[:, 0:512]
        tw1 = wq.copy(wl[0:64, :], a["w_decay_up_2"], *s1.free)
        tw2 = wq.copy(wl[64:128, :], a["w_iclr_up_2"])
        ac.need(t_f)
        t1 = ac.mark(st.activation(wa[0:64, :], wa[0:64, :], ACT.Tanh))
        sw, wv, tw = wload(wcols(w, 512, 512), 8, 512)
        t_k = {}
        for n in range(2):
            t_k[n], tp = feature(wv, 128 * n, 4 + n, kaT[:, n, :], tw)
        for n in range(4):
            for j, (p0, col, d_) in enumerate(((0, 37, cumT), (64, 41, aT))):
                s = OR.get()
                pe.need(*s.free, t1, tw1, tw2)
                tp = pe.mark(mm(s.ap, wl[p0:p0 + 64, n * 128:(n + 1) * 128], wa[p0:p0 + 64, :], True, True))
                ac.need(tp)
                t_sg = ac.mark(st.activation(d_[:, n, :], s.ap, ACT.Sigmoid, bias=PT[:, col + n:col + n + 1]))
                s.free = [t_sg]
        s1.free = [tp]
        for n in range(2, 4):
            t_k[n], tp = feature(wv, 128 * n, 4 + n, kaT[:, n, :], tw)
        sw.free = [tp]
        sel = small.take(4, 2)
        for n in range(4):
            ve.mark(vt.tensor_scalar(sel[:, n, :], C["hsel"], PT[:, 53 + n:54 + n], None, ALU.mult))
        sn = OR.get()
        hs8 = C["hs8"].rearrange("p (n h) -> p n h", h=8)
        hb8 = C["hb8"].rearrange("p (n q) -> p n q", q=128)
        t_kn = []
        for n in range(4):
            t_kn.append(vop(lambda: vt.tensor_scalar(alT[:, n, :], kaT[:, n, :], PT[:, 45 + n:46 + n], None, ALU.mult)))
            b = bufs.get()
            ac.need(t_kn[n], *b.free)
            t2 = ac.mark(st.activation(b.ap, alT[:, n, :], ACT.Square))
            pe.need(t2, *sn.free)
            tp = pe.mark(mm(sn.ap[0:8, :], hs8[:, n, :], b.ap, n == 0, n == 3))
            b.free = [tp]
        sr_, wr_, twr = wload(wcols(w, 0, 512), 8, 512)
        sv_, wv_, twv = wload(wcols(w, 1024, 512), 8, 512)
        t_r, t_v = {}, {}
        t_r[0], tp2 = feature(wr_, 0, 0, rT[:, 0, :], twr)
        m_, y_, q_ = nrm[0:8, 0, :], nrm[0:8, 1, :], nrm[0:8, 2, :]
        t3 = vop(lambda: vt.tensor_scalar(m_, sn.ap[0:8, :], 1e-24, None, ALU.max), tp)
        sn.free = [t3]
        ac.need(t3)
        t4 = ac.mark(st.activation(y_, m_, ACT.Sqrt, scale=float(2.0 ** 40)))
        t_v[0], tp2 = feature(wv_, 0, 8, vT[:, 0, :], twv)
        vop(lambda: vt.reciprocal(y_, y_), t4)
        vop(lambda: vt.tensor_scalar(y_, y_, float(2.0 ** 20), None, ALU.mult))
        vop(lambda: vt.tensor_tensor(q_, m_, y_, ALU.mult))
        vop(lambda: vt.tensor_tensor(q_, q_, y_, ALU.mult))
        vop(lambda: vt.tensor_scalar(q_, q_, -0.5, 1.5, ALU.mult, ALU.add))
        t_y = vop(lambda: vt.tensor_tensor(y_, y_, q_, ALU.mult))
        dmid = small.take(4, 4)
        dend = small.take(4, 4)
        done = {}

        def chain(n):
            if n > 0:
                t_r[n], tp = feature(wr_, 128 * n, n, rT[:, n, :], twr)
                t_v[n], tq = feature(wv_, 128 * n, 8 + n, vT[:, n, :], twv)
                if n == 3:
                    sr_.free, sv_.free = [tp], [tq]
            s = OR.get()
            pe.need(t_y, *s.free)
            tp = pe.mark(mm(s.ap, hb8[0:8, n, :], y_, True, True))
            kn, be, k_, r_, cm_ = alT[:, n, :], beT[:, n, :], kaT[:, n, :], rT[:, n, :], cumT[:, n, :]
            t1 = vop(lambda: vt.tensor_tensor(kn, s.ap, kn, ALU.mult), tp)
            s.free = [t1]
            vop(lambda: vt.tensor_tensor(be, kn, aT[:, n, :], ALU.mult), t_sg)
            b = bufs.get()
            vop(lambda: vt.tensor_scalar(b.ap, aT[:, n, :], 1.0, PT[:, 49 + n:50 + n], ALU.subtract, ALU.mult), *b.free)
            vop(lambda: vt.scalar_tensor_tensor(out=k_, in0=b.ap, scalar=1.0, in1=k_, op0=ALU.add, op1=ALU.mult))
            t6 = vop(lambda: vt.tensor_tensor(b.ap, r_, k_, ALU.mult))
            b2 = scs.get()
            c_ = b2.ap
            c4 = c_.rearrange("p (c q) -> p c q", q=128)
            vop(lambda: vt.tensor_tensor_scan(c_, res, cm_, 0.0, ALU.mult, ALU.add), t_res, *b2.free)
            vop(lambda: vt.tensor_copy(dmid[:, n, :], c4[:, :, 63]))
            vop(lambda: vt.tensor_tensor(c4, c4, bc(dmid[:, n, :], 128), ALU.subtract))
            t2 = vop(lambda: vt.tensor_tensor(aT[:, n, :], c_, cm_, ALU.subtract))
            ac.need(t2)
            t3 = ac.mark(st.activation(aT[:, n, :], aT[:, n, :], ACT.Exp, scale=-DECAY))
            t4 = ac.mark(st.activation(cm_, c_, ACT.Exp, scale=-DECAY))
            t5 = ac.mark(st.activation(c_, c_, ACT.Exp, scale=DECAY))
            s = TR.get()
            pe.need(t6, *s.free)
            for t in ALLT:
                r = mm(s.ap[:, 2 * t:2 * t + 2], b.ap[:, t * 128:(t + 1) * 128], sel[:, n, :], True, True)
            tp = pe.mark(r)
            b.free = [tp]
            done[n] = (b2, c_, t3, t4, t5, s, tp)

        def apply(n):
            b2, c_, t3, t4, t5, s, tp = done[n]
            t7 = vop(lambda: vt.tensor_copy(dia[:, :, 2 * n:2 * n + 2], s.ap[:, 0:8].rearrange("p (t c) -> p t c", c=2)),
                     tp)
            s.free = [t7]
            vop(lambda: vt.scalar_tensor_tensor(out=alT[:, n, :], in0=alT[:, n, :], scalar=-1.0, in1=aT[:, n, :],
                                                op0=ALU.mult, op1=ALU.mult), t3)
            vop(lambda: vt.tensor_copy(dend[:, n, :], cumT[:, n, :].rearrange("p (c q) -> p c q", q=128)[:, :, 127]), t4)
            vop(lambda: vt.tensor_tensor(rT[:, n, :], rT[:, n, :], cumT[:, n, :], ALU.mult))
            vop(lambda: vt.tensor_tensor(beT[:, n, :], beT[:, n, :], c_, ALU.mult), t5)
            b2.free = [vop(lambda: vt.tensor_tensor(kaT[:, n, :], kaT[:, n, :], c_, ALU.mult))]

        pipe(range(4), chain, apply)
        ac.need(ve.last)
        t_dm = ac.mark(st.activation(dmid, dmid, ACT.Exp, scale=-DECAY))
        barrier()

        vTM = aT
        for n in range(4):
            s = TR.get()
            pe.need(*s.free)
            for t in ALLT:
                r = pt_.transpose(s.ap[:, t * 128:(t + 1) * 128], vT[:, n, t * 128:(t + 1) * 128], ident)
            tp = pe.mark(r)
            ac.need(tp)
            t_vt = ac.mark(st.copy(vTM[:, :, n * 128:(n + 1) * 128], s.ap.rearrange("p (t c) -> p t c", c=128)))
            s.free = [t_vt]
        xp = Place(X[:, :, :].rearrange("p a b -> p (a b)"), 4096)
        LT, AK, RB, RK = (xp.take(8, 128) for _ in range(4))
        vp = Place(vT.rearrange("p a b -> p (a b)"), 2048)
        T0, TT0 = vp.take(8, 128), vp.take(8, 128)
        cp = Place(cumT.rearrange("p a b -> p (a b)"), 2048)
        beTM, kaTM, S0, SA = cp.take(512), cp.take(512), cp.take(4, 128), cp.take(512)
        mp = Place(AR, mis_at + 2050 + 1024, mis_at - 512)
        UU, RHS, YB, YQ = mp.take(8, 64), mp.take(512), mp.take(512), mp.take(512)
        sgr = Ring([mp.take(512) for _ in range(2)])
        yb1 = mp.take(512)
        obp = Place(oB.rearrange("p a b -> p (a b)"), 2048)
        gnb = obp.take(1024)
        bgr = Ring([obp.take(512) for _ in range(2)])
        tail = Place(AR, ARN, tail.at - 5 * 512 - 512)
        mx = tail.take(4, 1024)
        bgate = a["b_gate_2"].unsqueeze(0)
        t_gn = [mq.copy(gnb[:, 0:512], a["gn_gain_2"].unsqueeze(0).to_broadcast([128, 512])),
                mq.copy(gnb[:, 512:1024], a["gn_bias_2"].unsqueeze(0).to_broadcast([128, 512]))]
        for z in (LT, AK, RB, RK):
            po.mark(gt.memset(z, 0.0))
        t_z = po.mark(gt.memset(S0, 0.0))
        ve.need(t_z, t_vt, *t_gn)
        pe.need(t_z, t_vt)
        stri, tri = C["stri"].bitcast(U32), C["tri"].bitcast(U32)
        v8 = lambda x: x.rearrange("p (h d) -> p h d", d=64)
        mu8, va8, rs8, m8, y8 = (small.take(8) for _ in range(5))
        za, gw = {}, {}
        oAT = oBT

        def gate_part(c, t, gv, tg, bg, tb_):
            s = OR.get()
            pe.need(*s.free, tg)
            for k in range(8):
                r = mm(s.ap, HT[:, k, t * 128:(t + 1) * 128], gv[:, k, :], k == 0, k == 7)
                if k % 2 and k < 7:
                    yield 1
            za["pg"] = tp = pe.mark(r)
            z = sgr.get()
            ve.need(tp, tb_, *z.free)
            tz = ve.mark(vt.tensor_tensor(z.ap, s.ap, bg, ALU.add))
            s.free = [tz]
            ac.need(tz)
            za["z", c] = z, ac.mark(st.activation(z.ap, z.ap, ACT.Sigmoid))
            yield 1

        def up_part(lT, br, c, t, uv, tu):
            z, tz = za["z", c]
            s = OR.get()
            pe.need(*s.free, tu)
            for k in range(4):
                r = mm(s.ap, lT[:, k, t * 128:(t + 1) * 128], uv[:, k, :], k == 0, k == 3)
                if k == 1:
                    yield 1
            za["pu"] = tp = pe.mark(r)
            m = mx[:, t, c * 512:(c + 1) * 512]
            ve.need(tp, tz)
            if br == 1:
                tm = ve.mark(vt.tensor_tensor(m, s.ap, z.ap, ALU.mult))
            else:
                ve.need(za.get("y1"))
                tm = ve.mark(vt.tensor_tensor(yb1, s.ap, z.ap, ALU.mult))
                ve.need(tm)
                za["y1"] = tm = ve.mark(vt.tensor_tensor(m, m, yb1, ALU.add))
            s.free = [tm]
            z.free = [tm]
            za[(br, c, t)] = tm
            yield 1

        def gate_branch(lT, br, wo):
            for c in range(2):
                sg_, gv, tg = wload(wcols(w, 3104 + 1024 * br + 512 * c, 512), 8, 512)
                su_, uv, tu = wload(wo[:, 512 * c:512 * c + 512].rearrange("(k p) n -> p k n", p=128), 4, 512)
                bg = bgr.get()
                o = 1024 * br + 512 * c
                tb_ = mq.copy(bg.ap, bgate[:, o:o + 512].to_broadcast([128, 512]), *bg.free)
                for t in ALLT:
                    yield from gate_part(c, t, gv, tg, bg.ap, tb_)
                    yield from up_part(lT, br, c, t, uv, tu)
                bg.free = [za[(br, c, 3)]]
                sg_.free, su_.free = [za["pg"]], [za["pu"]]

        def dense():
            sw, wv, tw = wload(wcols(w, 1664, 512), 8, 512)
            for t in ALLT:
                s = OR.get()
                pe.need(*s.free, tw)
                for k in range(8):
                    r = mm(s.ap, HT[:, k, t * 128:(t + 1) * 128], wv[:, k, :], k == 0, k == 7)
                    if k % 2 and k < 7:
                        yield 1
                tp = pe.mark(r)
                ac.need(tp)
                za[t] = ac.mark(st.activation(oA[:, t, :], s.ap, ACT.Silu))
                s.free = [za[t]]
                yield 1
            sw.free = [tp]
            yield from gate_branch(oBT, 1, a["w_out_b_2"])
            for c in range(2):
                gw[c] = wload(wcols(w, 3104 + 512 * c, 512), 8, 512)
                bg = bgr.get()
                gw["b", c] = bg.ap, mq.copy(bg.ap, bgate[:, 512 * c:512 * c + 512].to_broadcast([128, 512]), *bg.free)
            su_, uv, tu = wload(a["w_out_a_2"].rearrange("(k p) n -> p k n", p=128), 4, 1024)
            for t in ALLT:
                for c in range(2):
                    sg_, gv, tg = gw[c]
                    yield from gate_part(c, t, gv, tg, *gw["b", c])
                    sg_.free = [za["pg"]]
                while ("o", t) not in za:
                    yield 1
                te, _ = turn4(oA[:, t, :], oAT, t, 4, za[("o", t)])
                yield 1
                pe.need(te)
                for c in range(2):
                    yield from up_part(oAT, 0, c, t, uv[:, :, 512 * c:512 * c + 512], tu)
            su_.free = [za["pu"]]

        def chunks():
            t_s = t_z
            t_ka = t_yb = None
            for c in ALLT:
                cs = slice(c * 128, (c + 1) * 128)

                def hT(x, h):
                    return x[64 * (h % 2):64 * (h % 2) + 64, h // 2, cs]

                for src, d_ in ((beT, beTM), (kaT, kaTM)):
                    s = TR.get()
                    pe.need(*s.free)
                    for n in range(4):
                        r = pt_.transpose(s.ap[:, n * 128:(n + 1) * 128], src[:, n, cs], ident)
                    tp = pe.mark(r)
                    ac.need(tp, t_ka)
                    te = ac.mark(st.copy(d_, s.ap))
                    s.free = [te]
                t_tm = te
                yield 1
                for dst_, lx, rx, mk in ((LT, beT, alT, stri), (AK, kaT, alT, stri), (RB, beT, rT, tri),
                                         (RK, kaT, rT, tri)):
                    for par in range(2):
                        s = SR.get()
                        pe.need(*s.free)
                        for j in range(4):
                            h = 2 * j + par
                            r = mm(s.ap[:, j * 128:(j + 1) * 128], hT(lx, h), hT(rx, h), True, True)
                        tp = pe.mark(r)
                        v = dst_.rearrange("p (a b) t -> p a b t", b=2)[:, :, par, :]
                        ve.need(tp, t_ka)
                        te = ve.mark(vt.copy_predicated(v, mid(mk, 4), s.ap.rearrange("p (a t) -> p a t", t=128)))
                        s.free = [te]
                    if dst_ is LT:
                        t1 = vop(lambda: vt.tensor_tensor(TT0, LT, mid(C["lv1"], 8), ALU.mult))
                        t_tt = vop(lambda: vt.tensor_tensor(TT0, TT0, mid(ident, 8), ALU.add))
                    yield 1
                t_g = te
                tT, tTT = [None, None], [t_tt, t_tt]
                for g in range(2):
                    s = TR.get()
                    pe.need(*s.free, t_tt)
                    for j in range(4):
                        r = pt_.transpose(s.ap[:, j * 128:(j + 1) * 128], TT0[:, 4 * g + j, :], ident)
                    tp = pe.mark(r)
                    ac.need(tp)
                    tT[g] = ac.mark(st.copy(T0[:, 4 * g:4 * g + 4, :], s.ap.rearrange("p (h t) -> p h t", t=128)))
                    s.free = [tT[g]]
                yield 1
                for m in (2, 4, 8, 16, 32, 64):
                    nb = 64 // m
                    ev = T0.rearrange("p h (k two m) -> p h k two m", two=2, m=m)
                    tU = [None, None]
                    for g in range(2):
                        s = SR.get()
                        pe.need(*s.free, tT[g])
                        for j in range(4):
                            r = mm(s.ap[:, j * 64:(j + 1) * 64], LT[:, 4 * g + j, :], ev[:, 4 * g + j, :, 0, :],
                                   True, True)
                        tp = pe.mark(r)
                        ve.need(tp)
                        tU[g] = ve.mark(vt.tensor_tensor(UU[:, 4 * g:4 * g + 4, :],
                                                         s.ap[:, 0:256].rearrange("p (h t) -> p h t", t=64),
                                                         mid(C[f"um{m}"], 4), ALU.mult))
                        s.free = [tU[g]]
                    yield 1
                    for g in range(2):
                        s = TR.get()
                        pe.need(*s.free, tU[g], tTT[g])
                        for j in range(4):
                            r = mm(s.ap[:, j * 64:(j + 1) * 64], TT0[:, 4 * g + j, :], UU[:, 4 * g + j, :], True, True)
                        tp = pe.mark(r)
                        ve.need(tp)
                        for j in range(4):
                            v = ev[:, 4 * g + j, :, 0, :]
                            tT[g] = ve.mark(vt.tensor_tensor(v, s.ap[:, j * 64:(j + 1) * 64].rearrange(
                                "p (k m) -> p k m", m=m), v, ALU.add))
                        s.free = [tT[g]]
                    yield 1
                    for g in range(2):
                        s = SR.get()
                        pe.need(*s.free, tT[g])
                        for j in range(4):
                            r = pt_.transpose(s.ap[:, j * 128:(j + 1) * 128], T0[:, 4 * g + j, :], ident)
                        tp = pe.mark(r)
                        ac.need(tp)
                        tTT[g] = ac.mark(st.copy(TT0[:, 4 * g:4 * g + 4, :], s.ap.rearrange("p (h t) -> p h t", t=128)))
                        s.free = [tTT[g]]
                    yield 1
                ve.need(t_s, t_dm)
                for n in range(4):
                    t_s0 = ve.mark(vt.tensor_scalar(S0[:, n, :], S0[:, n, :], dmid[:, n, c:c + 1], None, ALU.mult))
                s = TR.get()
                pe.need(*s.free, t_s0, t_g)
                for n in range(4):
                    mm(s.ap[:, n * 128:(n + 1) * 128], alT[:, n, cs], S0[:, n, :], n == 0, True, True)
                for h in range(8):
                    r = mm(s.ap[:, h * 64:(h + 1) * 64], AK[:, h, :], vTM[:, c, h * 64:(h + 1) * 64], False, True, True)
                tp = pe.mark(r)
                ac.need(tp)
                t1 = ac.mark(st.copy(RHS, s.ap))
                s.free = [t1]
                yield 1
                s = TR.get()
                pe.need(*s.free, t1, *tTT)
                for h in range(8):
                    r = mm(s.ap[:, h * 64:(h + 1) * 64], TT0[:, h, :], RHS[:, h * 64:(h + 1) * 64], True, True)
                tp = pe.mark(r)
                ac.need(tp)
                t_sa = ac.mark(st.copy(SA, s.ap))
                s.free = [t_sa]
                yield 1
                s = TR.get()
                pe.need(*s.free)
                for n in range(4):
                    mm(s.ap[:, n * 128:(n + 1) * 128], rT[:, n, cs], S0[:, n, :], n == 0, True, True)
                for h in range(8):
                    mm(s.ap[:, h * 64:(h + 1) * 64], RK[:, h, :], vTM[:, c, h * 64:(h + 1) * 64], False, True, True)
                pe.need(t_sa)
                for h in range(8):
                    r = mm(s.ap[:, h * 64:(h + 1) * 64], RB[:, h, :], SA[:, h * 64:(h + 1) * 64], False, True, True)
                tp = pe.mark(r)
                ac.need(tp, t_yb)
                t_y = ac.mark(st.copy(YB, s.ap))
                s.free = [t_y]
                s = SR.get()
                pe.need(*s.free, t_tm)
                for n in range(4):
                    mm(s.ap[:, n * 128:(n + 1) * 128], beTM[:, n * 128:(n + 1) * 128], SA[:, n * 128:(n + 1) * 128],
                       True, False)
                    r = mm(s.ap[:, n * 128:(n + 1) * 128], kaTM[:, n * 128:(n + 1) * 128],
                           vTM[:, c, n * 128:(n + 1) * 128], False, True)
                t_ka = tp = pe.mark(r)
                ve.need(tp)
                for par in range(2):
                    q = slice(64 * par, 64 * par + 64)
                    sv_ = s.ap[q, :].rearrange("p (n v) -> p n v", v=128)[:, :, 64 * par:64 * par + 64]
                    S_ = S0[q, :, 64 * par:64 * par + 64]
                    vop(lambda: vt.tensor_tensor(S_, sv_, S_, ALU.add))
                    t_s = vop(lambda: vt.tensor_tensor(S_, S_, bc(dend[q, :, c], 64), ALU.mult))
                s.free = [t_s]
                yield 1
                y = v8(YB)
                vop(lambda: vt.reduce_sum(mu8, y, AX.X), t_y)
                vop(lambda: vt.tensor_scalar(mu8, mu8, 1.0 / 64, None, ALU.mult))
                t1 = vop(lambda: vt.tensor_tensor(y, y, bc(mu8, 64), ALU.subtract))
                ac.need(t1)
                t2 = ac.mark(st.activation(YQ, YB, ACT.Square))
                t3 = vop(lambda: vt.reduce_sum(va8, v8(YQ), AX.X), t2)
                rstd(rs8, va8, 64, (m8, y8), t3, 1.0, GN_EPS)
                vop(lambda: vt.tensor_tensor(y, y, bc(rs8, 64), ALU.mult))
                vop(lambda: vt.tensor_tensor(YB, YB, gnb[:, 0:512], ALU.mult))
                vop(lambda: vt.tensor_tensor(YB, YB, gnb[:, 512:1024], ALU.add))
                vop(lambda: vt.tensor_tensor(v8(YQ), v8(vTM[:, c, :]), bc(dia[:, c, :], 64), ALU.mult))
                vop(lambda: vt.tensor_tensor(YB, YB, YQ, ALU.add))
                t_yb = vop(lambda: vt.tensor_tensor(oA[:, c, :], oA[:, c, :], YB, ALU.mult), za[c])
                za[("o", c)] = t_yb
                yield 1

        weave(chunks(), dense())
        barrier()
        mq.copy(X[:, :, :], xv)
        gp = Place(vT.rearrange("p a b -> p (a b)"), 2048)
        gpb = gp.take(1024)
        t_gp = mq.copy(gpb, a["g_post_2"].unsqueeze(0).to_broadcast([128, 1024]))
        mxT = AR[:, base + 3 * 2048:base + 5 * 2048].rearrange("p (a b) -> p a b", b=512)
        for c in range(2):
            for t in ALLT:
                tm, _ = turn4(mx[:, t, c * 512:(c + 1) * 512], mxT[:, 4 * c:4 * c + 4, :], t, 4, za[(0, c, t)])
        yo = alT.rearrange("p a b -> p (a b)")
        yo = AR[:, base + 5 * 2048:base + 7 * 2048].rearrange("p (a b) -> p a b", b=1024)
        ss, rs, m, y = (small.take(4) for _ in range(4))
        junk = kaT.rearrange("p a b -> p (a b)")[:, 0:1024]
        ve.need(t_gp, *mq.outstanding())
        wo_ = [wload(wcols(a["w_o_2"], 512 * c, 512), 8, 512) for c in range(2)]

        def w_o(c, t):
            ps, tp = proj(mxT, t, 8, wo_[c][1], 0, 512, SR, wo_[c][2], tm)
            ac.need(tp)
            t1 = ac.mark(st.copy(yo[:, t, c * 512:(c + 1) * 512], ps.ap))
            ps.free = [t1]

        for t in ALLT:
            w_o(0, t)
        outv = out[0].rearrange("(t p) d -> p t d", p=128)
        for t in ALLT:
            w_o(1, t)
            ac.need(ac.last)
            t1 = ac.mark(st.activation(junk, yo[:, t, :], ACT.Square, accum_out=ss[:, t:t + 1]))
            q = slice(t, t + 1)
            t1 = rstd(rs[:, q], ss[:, q], 1024, (m[:, q], y[:, q]), t1)
            vop(lambda: vt.scalar_tensor_tensor(out=yo[:, t, :], in0=yo[:, t, :], scalar=rs[:, t:t + 1], in1=gpb,
                                                op0=ALU.mult, op1=ALU.mult))
            t2 = vop(lambda: vt.tensor_tensor(yo[:, t, :], yo[:, t, :], X[:, t, :], ALU.add))
            oq.copy(outv[:, t, :], yo[:, t, :], t2)
        sy.need(*oq.outstanding())


_INS = ["x", "norm_mix_g", "w_in", "b_forget", "fox_q_g", "fox_k_g", "nsa_q_g", "nsa_k_g", "cmp_k_w1", "cmp_k_w2",
        "cmp_k_pos", "cmp_v_w1", "cmp_v_w2", "cmp_v_pos", "w_fox_up", "w_nsa_up", "w_out", "norm_ffn_g", "w_group",
        "b_group", "w_router", "b_router", "w_gate", "w_up", "w_down", "positions_2", "g_pre_2", "w_in_2",
        "b_gate_2", "mu_shift_2", "w0_2", "w_decay_up_2", "a0_2", "w_iclr_up_2", "k_k_2", "k_a_2", "r_k_2",
        "gn_gain_2", "gn_bias_2", "w_out_a_2", "g_q_2", "w_uq_2", "g_kv_2", "w_ukv_2", "w_out_b_2", "w_o_2",
        "g_post_2"]


def kernel(**inputs):
    import numpy as _np
    import concourse.bacc as _bacc
    from concourse import mybir as _mybir
    from concourse.bass_utils import run_bass_kernel_spmd as _run

    nc = _bacc.Bacc("TRN2", target_bir_lowering=False, num_devices=1)
    consts, coff = constants()
    arrays, args = {}, {}
    for name in _INS:
        arrays[f"in_{name}_dram"] = _np.ascontiguousarray(inputs[name])
    arrays["in_consts_dram"] = consts
    for key, arr in arrays.items():
        args[key[3:-5]] = nc.dram_tensor(key, arr.shape, _mybir.dt.from_np(arr.dtype), kind="ExternalInput").ap()
    out = nc.dram_tensor("out_0_dram", (1, 512, 1024), _mybir.dt.float32, kind="ExternalOutput").ap()
    spill = nc.dram_tensor("spill", (512, 1024), _mybir.dt.float32, kind="Internal").ap()
    ys = nc.dram_tensor("ys", (23 * 128, 1024), _mybir.dt.float32, kind="Internal").ap()
    build(nc, args, coff, out, spill, ys)
    r = _run(nc, [arrays], core_ids=[0])
    return r.results[0]["out_0_dram"]
```
